# Optimizing a Trainium2 kernel written in Bass

```python
import jax, jax.numpy as jnp
from jax import lax
import numpy as np
import math

D_MODEL = 1024
BATCH = 1
SEQ = 256
DEPTH = 2

RET_HEADS = 4
RET_QK_DIM = 128
RET_V_DIM = 256
RET_CHUNK = 128
SB_HEADS = 8
SB_HEAD_DIM = 128
SB_BLOCK = 128
D_FF = 4 * D_MODEL

ROPE_BASE = 10000.0
NORM_EPS = 1e-6
GN_EPS = 1e-5

RET_QK = RET_HEADS * RET_QK_DIM
RET_V = RET_HEADS * RET_V_DIM
SB_W = SB_HEADS * SB_HEAD_DIM
IN_SIZES = (RET_QK, RET_QK, RET_V, RET_V, SB_W, SB_W, SB_W, D_MODEL, D_MODEL)
D_IN = RET_QK * 2 + RET_V * 2 + SB_W * 3 + D_MODEL * 2


def rmsnorm(x, gain):
    xf = x.astype(jnp.float32)
    y = xf * lax.rsqrt(jnp.mean(xf * xf, axis=-1, keepdims=True) + NORM_EPS)
    return (y * gain.astype(jnp.float32)).astype(x.dtype)

def rotary(t, pos):
    half = t.shape[-1] // 2
    inv_freq = ROPE_BASE ** (-jnp.arange(half, dtype=jnp.float32) / half)
    ang = pos.astype(jnp.float32)[:, None] * inv_freq[None, :]
    cos = jnp.cos(ang)[None, :, None, :]
    sin = jnp.sin(ang)[None, :, None, :]
    t1, t2 = t[..., :half], t[..., half:]
    return jnp.concatenate([t1 * cos - t2 * sin, t1 * sin + t2 * cos], axis=-1)

def retention(q, k, v, log_gamma):
    B, S, H, _ = q.shape
    C = RET_CHUNK
    N = S // C
    idx = jnp.arange(C, dtype=jnp.float32)
    diff = idx[:, None] - idx[None, :]
    decay = jnp.where(diff[None] >= 0,
                      jnp.exp(log_gamma[:, None, None] * jnp.maximum(diff, 0.0)[None]), 0.0)
    q_decay = jnp.exp(log_gamma[None, :] * (idx[:, None] + 1.0))
    k_decay = jnp.exp(log_gamma[None, :] * (C - 1.0 - idx[:, None]))
    chunk_decay = jnp.exp(log_gamma * C)

    def to_chunks(t):
        return t.reshape(B, N, C, H, t.shape[-1]).transpose(1, 0, 2, 3, 4)

    def step(state, qkv):
        qc, kc, vc = qkv
        scores = jnp.einsum('bchd,bshd->bhcs', qc, kc) * decay[None]
        inner = jnp.einsum('bhcs,bshe->bche', scores, vc)
        cross = jnp.einsum('bchd,bhde->bche', qc, state) * q_decay[None, :, :, None]
        state = state * chunk_decay[None, :, None, None] + jnp.einsum(
            'bshd,bshe->bhde', kc * k_decay[None, :, :, None], vc)
        return state, inner + cross

    init = jnp.zeros((B, H, q.shape[-1], v.shape[-1]), jnp.float32)
    _, out = lax.scan(step, init, (to_chunks(q), to_chunks(k), to_chunks(v)))
    return out.transpose(1, 0, 2, 3, 4).reshape(B, S, H, v.shape[-1])

def head_group_norm(y):
    mu = jnp.mean(y, axis=-1, keepdims=True)
    var = jnp.mean(jnp.square(y - mu), axis=-1, keepdims=True)
    return (y - mu) * lax.rsqrt(var + GN_EPS)

def stick_breaking(q, k, v):
    S = q.shape[1]
    scale = q.shape[-1] ** -0.5
    outs = []
    for start in range(0, S, SB_BLOCK):
        end = start + SB_BLOCK
        qb = q[:, start:end]
        kb = k[:, :end]
        vb = v[:, :end]
        z = jnp.einsum('bthd,bshd->bhts', qb, kb) * scale
        t_idx = start + jnp.arange(SB_BLOCK)
        s_idx = jnp.arange(end)
        causal = (s_idx[None, :] < t_idx[:, None])[None, None]
        log_beta = jax.nn.log_sigmoid(z)
        log_1m_beta = jnp.where(causal, log_beta - z, 0.0)
        after = lax.cumsum(log_1m_beta, axis=3, reverse=True) - log_1m_beta
        weights = jnp.where(causal, jnp.exp(log_beta + after), 0.0)
        outs.append(jnp.einsum('bhts,bshe->bthe', weights, vb))
    return jnp.concatenate(outs, axis=1)

def first_inputs(seed: int = 0) -> dict:
    key = jax.random.key(seed)
    ks = jax.random.split(key, 10)
    f32 = jnp.float32
    x = jax.random.normal(ks[0], (BATCH, SEQ, D_MODEL), f32)
    w_in = jax.random.normal(ks[1], (DEPTH, D_MODEL, D_IN), f32) * D_MODEL ** -0.5
    p_ret = jax.random.normal(ks[2], (DEPTH, RET_V, D_MODEL), f32) * RET_V ** -0.5
    p_sb = jax.random.normal(ks[3], (DEPTH, SB_W, D_MODEL), f32) * SB_W ** -0.5
    w_out = jax.random.normal(ks[4], (DEPTH, D_MODEL, D_MODEL), f32) * D_MODEL ** -0.5
    w_up = jax.random.normal(ks[5], (DEPTH, D_MODEL, D_FF), f32) * D_MODEL ** -0.5
    w_down = jax.random.normal(ks[6], (DEPTH, D_FF, D_MODEL), f32) * D_FF ** -0.5
    g_mix = 1.0 + 0.02 * jax.random.normal(ks[7], (DEPTH, D_MODEL), f32)
    g_mlp = 1.0 + 0.02 * jax.random.normal(ks[8], (DEPTH, D_MODEL), f32)
    g_final = 1.0 + 0.02 * jax.random.normal(ks[9], (D_MODEL,), f32)
    return {'x': x, 'w_in': w_in, 'p_ret': p_ret, 'p_sb': p_sb, 'w_out': w_out,
            'w_up': w_up, 'w_down': w_down, 'g_mix': g_mix, 'g_mlp': g_mlp,
            'g_final': g_final}

def first_block(x, w_in, p_ret, p_sb, w_out, w_up, w_down, g_mix, g_mlp, g_final):
    B, S, _ = x.shape
    dt = x.dtype
    pos = jnp.arange(S, dtype=jnp.int32)
    log_gamma = jnp.log1p(-(2.0 ** (-5.0 - jnp.arange(RET_HEADS, dtype=jnp.float32))))
    splits = [int(v) for v in np.cumsum(IN_SIZES)[:-1]]
    for l in range(DEPTH):
        h = rmsnorm(x, g_mix[l])
        proj = jnp.matmul(h, w_in[l]).astype(jnp.float32)
        q_r, k_r, v_r, g_r, q_s, k_s, v_s, gate_a, gate_b = jnp.split(proj, splits, axis=-1)
        q_r = rotary(q_r.reshape(B, S, RET_HEADS, RET_QK_DIM), pos)
        k_r = rotary(k_r.reshape(B, S, RET_HEADS, RET_QK_DIM), pos) * (RET_QK_DIM ** -0.5)
        ret = retention(q_r, k_r, v_r.reshape(B, S, RET_HEADS, RET_V_DIM), log_gamma)
        ret = head_group_norm(ret).reshape(B, S, RET_V) * jax.nn.silu(g_r)
        sb = stick_breaking(q_s.reshape(B, S, SB_HEADS, SB_HEAD_DIM),
                            k_s.reshape(B, S, SB_HEADS, SB_HEAD_DIM),
                            v_s.reshape(B, S, SB_HEADS, SB_HEAD_DIM)).reshape(B, S, SB_W)
        branch_a = jnp.matmul(ret.astype(dt), p_ret[l]).astype(jnp.float32)
        branch_b = jnp.matmul(sb.astype(dt), p_sb[l]).astype(jnp.float32)
        merged = jax.nn.sigmoid(gate_a) * branch_a + jax.nn.sigmoid(gate_b) * branch_b
        x = x + jnp.matmul(merged.astype(dt), w_out[l]).astype(dt)
        h = rmsnorm(x, g_mlp[l])
        up = jnp.square(jax.nn.relu(jnp.matmul(h, w_up[l])))
        x = x + jnp.matmul(up, w_down[l]).astype(dt)
    return rmsnorm(x, g_final)


DEPTH_2 = 1

D_MIX = D_MODEL
POOL_WINDOWS = (2, 4, 8, 16)
POOL_GROUPS = len(POOL_WINDOWS)
POOL_CH = 64
POOL_WIDTH = POOL_GROUPS * POOL_CH
MAX_WIN = max(POOL_WINDOWS)
HGRN_WIDTH = D_MIX - POOL_WIDTH
HGRN_HEAD_DIM = 128
HGRN_HEADS = HGRN_WIDTH // HGRN_HEAD_DIM
CHUNK = 64
D_FF_2 = 4 * D_MODEL
RMS_EPS = 1e-5
IN_WIDTH = POOL_WIDTH + 4 * HGRN_WIDTH


def rms_norm(x, g, eps=RMS_EPS):
    xf = x.astype(jnp.float32)
    y = xf * lax.rsqrt(jnp.mean(xf * xf, axis=-1, keepdims=True) + eps)
    return (y * g.astype(jnp.float32)).astype(x.dtype)

def pool_mixer(u, w, scale):
    B, S, _ = u.shape
    uf = u.astype(jnp.float32)
    c = jnp.cumsum(uf, axis=1)
    cp = jnp.pad(c, ((0, 0), (MAX_WIN, 0), (0, 0)))
    t = jnp.arange(S)
    groups = []
    for gi, win in enumerate(POOL_WINDOWS):
        lo, hi = gi * POOL_CH, (gi + 1) * POOL_CH
        win_sum = c[:, :, lo:hi] - cp[:, MAX_WIN - win:MAX_WIN - win + S, lo:hi]
        cnt = jnp.minimum(t + 1, win).astype(jnp.float32)[None, :, None]
        groups.append(win_sum / cnt - uf[:, :, lo:hi])
    p = jnp.stack(groups, axis=2)
    y = jnp.einsum('bsgc,gcd->bsgd', p, w.astype(jnp.float32)).reshape(B, S, POOL_WIDTH)
    return (y * scale.astype(jnp.float32)).astype(u.dtype)

def _to_chunks(t, B, S):
    return t.reshape(B, S // CHUNK, CHUNK, HGRN_HEADS, HGRN_HEAD_DIM).transpose(1, 0, 3, 2, 4)

def hgrn2_mixer(q_raw, f_raw, i_raw, g_raw, lb, norm_g):
    B, S, _ = q_raw.shape
    z = f_raw.astype(jnp.float32)
    lbf = lb.astype(jnp.float32)
    log_f = jnp.logaddexp(jnp.log(lbf), jnp.log1p(-lbf) + jax.nn.log_sigmoid(z))
    k = (1.0 - lbf) * jax.nn.sigmoid(-z)
    q = jax.nn.silu(q_raw.astype(jnp.float32))
    v = i_raw.astype(jnp.float32)
    qc, kc, vc, fc = (_to_chunks(a, B, S) for a in (q, k, v, log_f))
    causal = jnp.tril(jnp.ones((CHUNK, CHUNK), dtype=bool))[None, None, :, :, None]

    def chunk_step(state, inp):
        qb, kb, vb, lfb = inp
        b = jnp.cumsum(lfb, axis=2)
        diff = jnp.where(causal, b[:, :, :, None, :] - b[:, :, None, :, :], -jnp.inf)
        scores = jnp.einsum('bhtk,bhsk,bhtsk->bhts', qb, kb, jnp.exp(diff))
        o = (jnp.einsum('bhts,bhsv->bhtv', scores, vb)
             + jnp.einsum('bhtk,bhkv->bhtv', qb * jnp.exp(b), state))
        b_last = b[:, :, -1:, :]
        new_state = (jnp.exp(b_last[:, :, 0, :])[..., None] * state
                     + jnp.einsum('bhsk,bhsv->bhkv', kb * jnp.exp(b_last - b), vb))
        return new_state, o

    s0 = jnp.zeros((B, HGRN_HEADS, HGRN_HEAD_DIM, HGRN_HEAD_DIM), jnp.float32)
    _, o = lax.scan(chunk_step, s0, (qc, kc, vc, fc))
    o = o.transpose(1, 0, 3, 2, 4).reshape(B, S, HGRN_HEADS, HGRN_HEAD_DIM)
    o = o * lax.rsqrt(jnp.mean(o * o, axis=-1, keepdims=True) + RMS_EPS)
    o = o.reshape(B, S, HGRN_WIDTH) * norm_g.astype(jnp.float32)
    o = o * jax.nn.silu(g_raw.astype(jnp.float32))
    return o.astype(q_raw.dtype)

def second_inputs(seed: int = 0) -> dict:
    key = jax.random.key(seed)
    ks = jax.random.split(key, 12)
    f32 = jnp.float32
    x = jax.random.normal(ks[0], (BATCH, SEQ, D_MODEL), f32)
    norm_mix_g = 1.0 + 0.05 * jax.random.normal(ks[1], (DEPTH_2, D_MODEL), f32)
    w_in = jax.random.normal(ks[2], (DEPTH_2, D_MODEL, IN_WIDTH), f32) * D_MODEL ** -0.5
    pool_w = jax.random.normal(ks[3], (DEPTH_2, POOL_GROUPS, POOL_CH, POOL_CH), f32) * POOL_CH ** -0.5
    pool_scale = 1.0 + 0.1 * jax.random.normal(ks[4], (DEPTH_2, POOL_WIDTH), f32)
    hgrn_lb_logits = 0.5 * jax.random.normal(ks[5], (DEPTH_2, HGRN_WIDTH), f32)
    hgrn_norm_g = 1.0 + 0.05 * jax.random.normal(ks[6], (DEPTH_2, HGRN_WIDTH), f32)
    w_out = jax.random.normal(ks[7], (DEPTH_2, D_MIX, D_MODEL), f32) * D_MIX ** -0.5
    norm_mlp_g = 1.0 + 0.05 * jax.random.normal(ks[8], (DEPTH_2, D_MODEL), f32)
    w_up = jax.random.normal(ks[9], (DEPTH_2, D_MODEL, D_FF_2), f32) * D_MODEL ** -0.5
    w_down = jax.random.normal(ks[10], (DEPTH_2, D_FF_2, D_MODEL), f32) * D_FF_2 ** -0.5
    final_norm_g = 1.0 + 0.05 * jax.random.normal(ks[11], (D_MODEL,), f32)
    return {"x": x, "norm_mix_g": norm_mix_g, "w_in": w_in, "pool_w": pool_w,
            "pool_scale": pool_scale, "hgrn_lb_logits": hgrn_lb_logits,
            "hgrn_norm_g": hgrn_norm_g, "w_out": w_out, "norm_mlp_g": norm_mlp_g,
            "w_up": w_up, "w_down": w_down, "final_norm_g": final_norm_g}

def second_block(x, norm_mix_g, w_in, pool_w, pool_scale, hgrn_lb_logits, hgrn_norm_g,
              w_out, norm_mlp_g, w_up, w_down, final_norm_g):
    lb_cum = jnp.cumsum(jax.nn.softmax(hgrn_lb_logits.astype(jnp.float32), axis=0), axis=0)
    lower_bounds = lb_cum - lb_cum[0:1]
    splits = [POOL_WIDTH + j * HGRN_WIDTH for j in range(4)]
    for l in range(DEPTH_2):
        h = rms_norm(x, norm_mix_g[l])
        u = h @ w_in[l]
        u_pool, q_raw, f_raw, i_raw, g_raw = jnp.split(u, splits, axis=-1)
        y_pool = pool_mixer(u_pool, pool_w[l], pool_scale[l])
        y_hgrn = hgrn2_mixer(q_raw, f_raw, i_raw, g_raw, lower_bounds[l], hgrn_norm_g[l])
        x = x + jnp.concatenate([y_pool, y_hgrn], axis=-1) @ w_out[l]
        h2 = rms_norm(x, norm_mlp_g[l])
        x = x + jnp.square(jax.nn.relu(h2 @ w_up[l])) @ w_down[l]
    return rms_norm(x, final_norm_g)


def setup_inputs(seed=0):
    out = dict(first_inputs(seed))
    for name, value in second_inputs(seed + 1).items():
        if name != "x":
            out[name + "_2"] = value
    return out


def reference(
    x, w_in, p_ret, p_sb, w_out, w_up, w_down, g_mix, g_mlp, g_final, norm_mix_g_2, w_in_2,
    pool_w_2, pool_scale_2, hgrn_lb_logits_2, hgrn_norm_g_2, w_out_2, norm_mlp_g_2, w_up_2,
    w_down_2, final_norm_g_2,
):
    x = first_block(
        x, w_in, p_ret, p_sb, w_out, w_up, w_down, g_mix, g_mlp, g_final,
    )
    return second_block(
        x, norm_mix_g_2, w_in_2, pool_w_2, pool_scale_2, hgrn_lb_logits_2, hgrn_norm_g_2,
        w_out_2, norm_mlp_g_2, w_up_2, w_down_2, final_norm_g_2,
    )


_drawn_inputs = setup_inputs


def setup_inputs(seed=0):
    import zlib

    import numpy as np

    out = dict(_drawn_inputs(seed))
    spreads = {}
    factors = {'hgrn_norm_g_2': 2.67}
    for name, (base, spread) in spreads.items():
        noise = np.random.default_rng([zlib.crc32(name.encode()), seed]).standard_normal(out[name].shape)
        drawn = base * np.exp(spread * noise) if base else spread * noise
        out[name] = __import__('jax').numpy.asarray(drawn.astype(out[name].dtype))
    for name, factor in factors.items():
        out[name] = (out[name] * factor).astype(out[name].dtype)
    return out
```

```python
import math
from contextlib import ExitStack

import numpy as np

import concourse.bass as bass
from concourse import mybir

F32 = mybir.dt.float32
F32R = mybir.dt.float32r
BF16 = mybir.dt.bfloat16
U8 = mybir.dt.uint8
ALU = mybir.AluOpType
ACT = mybir.ActivationFunctionType

P = 128
D = 1024
T = 256
TILES = T // P
KT = D // P
DEPTH = 2
HALF = 512
RET_H, SB_H, HG_H = 4, 8, 6
CAUSAL = T + P
SB_SCALE = P ** -0.5
CHUNK = 64
LEVELS = (64, 32, 16, 8, 4, 2, 1)
WINDOWS = (2, 4, 8, 16)
PAD = 16
NORM_EPS, RMS_EPS, GN_EPS = 1e-6, 1e-5, 1e-5

RAW_SLOTS, SPLIT_SLOTS = 4, 2
MIX_PIECES, MLP_PIECES, MIX2_PIECES = 44, 32, 17
LAYER_PIECES = MIX_PIECES + MLP_PIECES
FF_PAIRS = MLP_PIECES // 2
MIX_USES, MLP_USES, MIX2_USES = 2 + 36, 2 + FF_PAIRS, 2 + 13
LAYER_USES = MIX_USES + MLP_USES
ALL_PIECES = DEPTH * LAYER_PIECES + MIX2_PIECES + MLP_PIECES


class Place:

    def __init__(self, fixed, *terms):
        self.fixed, self.terms = fixed, terms

    def __add__(self, n):
        return Place(self.fixed + n, *self.terms)

    def slot(self, n):
        assert all(stride % n == 0 for _, stride in self.terms)
        return self.fixed % n

    def count(self, more=0, per=1):
        v = self.fixed // per + more
        for reg, stride in self.terms:
            v = reg * (stride // per) + v
        return v


def constants():
    f = np.float32
    half = P // 2
    inv_freq = (10000.0 ** (-np.arange(half, dtype=f) / f(half))).astype(f)
    ang = np.arange(T, dtype=f)[None, :] * np.concatenate([inv_freq, inv_freq])[:, None]
    rope = np.stack([np.cos(ang), np.sin(ang)], 1).astype(f)
    s, t = np.arange(P)[:, None], np.arange(P)[None, :]
    decay = np.zeros((P, RET_H, CAUSAL), f)
    for h in range(RET_H):
        lg = math.log1p(-(2.0 ** (-5.0 - h)))
        d0 = np.arange(T)[None, :] - s
        decay[:, h, :T] = np.where(d0 >= 0, np.exp(lg * np.maximum(d0, 0)), 0.0) * P ** -0.5
        decay[:, h, T:] = np.where(t >= s, np.exp(lg * np.maximum(t - s, 0)), 0.0) * P ** -0.5
    before = (s < t).astype(f)
    mask = np.concatenate([before, np.ones((P, P), f), before], 1)
    mask = np.stack([mask, mask], 1)
    later = (s > t).astype(f)
    turn = np.zeros((P, P), f)
    turn[np.arange(half) + half, np.arange(half)] = -1.0
    turn[np.arange(half), np.arange(half) + half] = 1.0
    square = np.stack([np.eye(P, dtype=f), np.full((P, P), 1.0 / T, f), later, np.ones((P, P), f), turn], 1)
    levels = np.zeros((P, len(LEVELS), CHUNK), f)
    for n, m in enumerate(LEVELS):
        block = np.arange(CHUNK) // m
        levels[:, n] = (s >= block * 2 * m) & (s < block * 2 * m + m)
    restart = np.ones((P, 2 * T), f)
    restart[:, ::CHUNK] = 0.0
    counts = np.zeros((P, 2, T), f)
    for g, w in enumerate(WINDOWS):
        counts[64 * (g % 2):64 * (g % 2) + 64, g // 2] = 1.0 / np.minimum(np.arange(T) + 1, w)
    return {"rope": rope, "decay": decay, "mask": mask, "square": square,
            "levels": levels, "restart": restart, "counts": counts}


def build(nc, x, w_in, p_ret, p_sb, w_out, w_up, w_down, g_mix, g_mlp, g_final, norm_mix_g_2, w_in_2, pool_w_2,
          pool_scale_2, hgrn_lb_logits_2, hgrn_norm_g_2, w_out_2, norm_mlp_g_2, w_up_2, w_down_2, final_norm_g_2,
          rope, decay, mask, square, levels, restart, counts, out):
    ctx = ExitStack()
    with ctx:
        SLAB = 206 * 1024
        slab = ctx.enter_context(nc.sbuf_tensor("slab", [P, SLAB], U8))
        base = slab_base(nc, SLAB)
        at = [0]

        def place(name, shape, dtype, offset=None):
            size = int(np.prod(shape[1:])) * mybir.dt.size(dtype)
            if offset is None:
                offset = at[0]
                at[0] += -(-size // 32) * 32
            assert offset + size <= SLAB, (name, offset + size - SLAB)
            return nc.alloc_sbuf_tensor_at(name, shape, dtype, offset=base + offset)

        PIECE = 2048
        raw = place("raw", [P, RAW_SLOTS, PIECE], F32)
        w_hi = place("w_hi", [P, SPLIT_SLOTS, PIECE], F32R)
        w_lo = place("w_lo", [P, SPLIT_SLOTS, PIECE], F32R)
        xs = place("xs", [P, TILES, D], F32)
        hT = place("hT", [P, KT, 2 * T], F32R)
        gain = place("gain", [P, 2, D], F32)
        htok_at = at[0]
        htok = place("htok", [P, TILES, D], F32)
        carry = place("carry", [P, 2, 2, T], F32)
        sumsq = place("sumsq", [P, 2], F32)
        meansq = place("meansq", [P, 2], F32)
        rstd = place("rstd", [P, 2], F32)
        minus_half = place("minus_half", [P, 2], F32)
        norm_eps = place("norm_eps", [P, 2], F32)
        gn_eps = place("gn_eps", [P, 1], F32)
        sq_c = place("sq_c", [P, 5, P], F32)
        ident, mean_w, later, ones, turn = (sq_c[:, i, :] for i in range(5))
        rope_c = place("rope_c", [P, 2, T], F32)
        mix_c_at = at[0]
        decay_c = place("decay_c", [P, RET_H, CAUSAL], F32)
        mask_c = place("mask_c", [P, 2, CAUSAL], F32)
        mix_at = at[0]
        sb_at = at[0]
        sbqk = place("sbqk", [P, SB_H // 2, 4, T], F32)
        sbT = place("sbT", [P, SB_H, 2 * T], F32R, sb_at)
        sbv = place("sbv", [P, TILES, D], F32)
        ret_at = at[0]
        retqkv = place("retqkv", [P, RET_H, 4, T], F32)
        retT = place("retT", [P, RET_H * 2, 2 * T], F32R, ret_at)
        u_at = at[0]
        gr = place("gr", [P, KT, T], F32)
        gates = place("gates", [P, 2, KT, T], F32)
        zs = place("zs", [P, 2, CAUSAL], F32, htok_at)
        soft = place("soft", [P, 2, CAUSAL], F32, htok_at + 2 * CAUSAL * 4)
        logw = place("logw", [P, 2, CAUSAL], F32)
        wts = place("wts", [P, 2, CAUSAL], F32)
        rs = place("rs", [P, CAUSAL], F32)
        y_at = at[0]
        ry = place("ry", [P, 2, 2, T], F32)
        rsq = place("rsq", [P, 2, T], F32)
        rrstd = place("rrstd", [P, T], F32)
        gtmp = place("gtmp", [P, 2, T], F32)
        uT = place("uT", [P, 2, 2, 2 * T], F32R, u_at)
        us = place("us", [P, 2, T], F32, y_at)
        usq = place("usq", [P, 2, T], F32, y_at + 2 * T * 4)
        at[0] = mix_c_at
        lev_c = place("lev_c", [P, len(LEVELS), HG_H * P], U8)
        restart_c = place("restart_c", [P, 2 * T], F32)
        at[0] = mix_at
        hz = place("hz", [P, HG_H, T], F32)
        hlog = place("hlog", [P, HG_H, T], F32)
        hfloor = place("hfloor", [P, HG_H, T], F32)
        hk = place("hk", [P, HG_H, T], F32)
        hq = place("hq", [P, HG_H, T], F32)
        hg = place("hg", [P, HG_H, T], F32)
        hb = place("hb", [P, HG_H, T], F32)
        hv = place("hv", [P, TILES, HG_H * P], F32)
        st = place("st", [P, HG_H * TILES, P], F32)
        cross = place("cross", [P, HG_H, P], F32)
        ho_at = at[0]
        ho = place("ho", [P, HG_H, T], F32)
        lev_f = place("lev_f", [P, len(LEVELS), CHUNK], F32, ho_at)
        htmp = place("htmp", [P, 2, T], F32)
        pads = place("pads", [P, 5, 2, PAD + T], F32)
        pmix = place("pmix", [P, 2, T], F32)
        py = place("py", [P, 2, T], F32)
        counts_c = place("counts_c", [P, 2, T], F32)
        pool_w = place("pool_w", [P, 2, P], F32)
        hcol = place("hcol", [P, 8, HG_H], F32)
        rms_eps = place("rms_eps", [P, 1], F32)
        btail = place("btail", [P, HG_H, 1], F32)
        LB_LOGIT, LB_EXP, LB, ONE_LESS, HNORM, PSCALE, LB_INV, LB_P = range(8)

        ps = ctx.enter_context(nc.psum_tensor("ps", [P, 8, HALF], F32))

        def sem(name):
            return ctx.enter_context(nc.semaphore(name))

        raw_in = [sem(f"raw_in{i}") for i in range(RAW_SLOTS)]
        hi_ready = sem("hi_ready")
        lo_dve = sem("lo_dve")
        lo_pool = sem("lo_pool")
        piece_used = sem("piece_used")
        pair_act = sem("pair_act")
        pair_free = sem("pair_free")
        consts_in = sem("consts_in")
        x_in = sem("x_in")
        gain_in = [sem("gain_in0"), sem("gain_in1")]
        small_set = sem("small_set")
        x_ready = sem("x_ready")
        sq_ready = sem("sq_ready")
        mean_ready = sem("mean_ready")
        rstd_ready = sem("rstd_ready")
        h_ready = sem("h_ready")
        h_turned = sem("h_turned")
        acc_full = sem("acc_full")
        z_full, z_scaled, z_abs, sb_exp, softplus, log_beta, neg_log_rest, masked_rest = (
            sem(n) for n in ("z_full", "z_scaled", "z_abs", "sb_exp", "softplus", "log_beta", "neg_log_rest",
                             "masked_rest"))
        after_full, log_weight, weight_exp, weight_ready, sb_out, sb_hi, sb_lo = (
            sem(n) for n in ("after_full", "log_weight", "weight_exp", "weight_ready", "sb_out", "sb_hi", "sb_lo"))
        turned, rope_cos, rope_sin, rope_done = (sem(n) for n in ("turned", "rope_cos", "rope_sin", "rope_done"))
        ret_scores, ret_decayed, ret_out, ret_copied, ret_mean, ret_centred, ret_squared, ret_var = (
            sem(n) for n in ("ret_scores", "ret_decayed", "ret_out", "ret_copied", "ret_mean", "ret_centred",
                             "ret_squared", "ret_var"))
        ret_log, ret_rstd, ret_normed, ret_gated, ret_hi, ret_lo = (
            sem(n) for n in ("ret_log", "ret_rstd", "ret_normed", "ret_gated", "ret_hi", "ret_lo"))
        gate_exp, gate_plus, gate_sig, gate_done = (sem(n) for n in ("gate_exp", "gate_plus", "gate_sig", "gate_done"))
        branch_a, branch_b, merged, merged_hi, merged_lo = (
            sem(n) for n in ("branch_a", "branch_b", "merged", "merged_hi", "merged_lo"))
        u_sum, u_squared, u_hi, u_lo = (sem(n) for n in ("u_sum", "u_squared", "u_hi", "u_lo"))
        consts2_in, cols_in, pads_zero, pool_w_zero, pool_w_in = (
            sem(n) for n in ("consts2_in", "cols_in", "pads_zero", "pool_w_zero", "pool_w_in"))
        lb_step, pool_step, pool_full, pool_scaled, pool_hi, pool_lo = (
            sem(n) for n in ("lb_step", "pool_step", "pool_full", "pool_scaled", "pool_hi", "pool_lo"))
        f_abs, f_exp, f_soft, f_ls, f_kexp_in, f_kexp, f_k, f_ez, f_floor, f_floor_log, f_log, f_cum = (
            sem(n) for n in ("f_abs", "f_exp", "f_soft", "f_ls", "f_kexp_in", "f_kexp", "f_k", "f_ez", "f_floor",
                             "f_floor_log", "f_log", "f_cum"))
        silu_exp, silu_plus, silu_sig, silu_done, g_scaled = (
            sem(n) for n in ("silu_exp", "silu_plus", "silu_sig", "silu_done", "g_scaled"))
        e_first, e_second, e_exp, x_first, x_second, pairs_full, pairs_placed = (
            sem(n) for n in ("e_first", "e_second", "e_exp", "x_first", "x_second", "pairs_full", "pairs_placed"))
        o_full, o_copied, o_squared, o_mean, o_log, o_rstd, o_normed, o_gated, o_hi, y_lo = (
            sem(n) for n in ("o_full", "o_copied", "o_squared", "o_mean", "o_log", "o_rstd", "o_normed", "o_gated",
                             "o_hi", "y_lo"))
        levels_set = sem("levels_set")
        out_sent = sem("out_sent")

        block = ctx.enter_context(nc.Block())

        def mixer_piece(k):
            for name, n in (("sbq", 4), ("sbk", 4), ("sbv", 4), ("rq", 2), ("rk", 2), ("rv", 4), ("rg", 4),
                            ("ga", 4), ("gb", 4), ("pret", 4), ("psb", 4), ("wout", 4)):
                if k < n:
                    return name, k
                k -= n

        def mixer_use(k):
            return 2 + (k if k < 8 else 8 + (k - 8) // 2 if k < 12 else k - 2 if k < 16 else
                        14 + (k - 16) // 2 if k < 20 else k - 4)

        def stages(k):
            todo = []
            for p in range(SB_H // 2):
                if k == 10 + 3 * p:
                    todo.append(("sb_after", p))
                if k == 11 + 3 * p:
                    todo.append(("sb_out", p))
            for p in range(SB_H // 2):
                if k == 8 + 3 * p:
                    todo.append(("sb_scores", p))
            if k in (18, 19):
                todo.append(("rotate", k - 18))
            for lag, name in ((3, "ret_var"), (2, "ret_mean"), (1, "ret_out"), (0, "ret_scores")):
                for h in range(RET_H):
                    if k == 20 + 2 * h + lag:
                        todo.append((name, h))
            return todo

        def mixer2_piece(k):
            for name, n in (("f", 3), ("pool", 1), ("q", 3), ("v", 3), ("g", 3), ("wout", 4)):
                if k < n:
                    return name, k
                k -= n

        PAIRS = [("diag", 0), ("diag", 1)] + [("level", n) for n in range(len(LEVELS))] + [("cross", 0)]

        def stages2(k):
            todo = []
            if k == 5:
                todo += [("pool", 0)]
            if k == 7:
                todo += [("diag", 0), ("diag", 1)]
            if 7 <= k <= 12:
                todo += [("level", k - 7)]
            if k == 12:
                todo += [("level", 6), ("cross", 0)]
            return todo

        @block.sync
        def _(sp):
            def piece_in(piece, source, ahead=0):
                if ahead is not None:
                    sp.wait_ge(lo_dve, (piece + ahead).count(1))
                    sp.wait_ge(lo_pool, (piece + ahead).count(1))
                s = piece.slot(RAW_SLOTS)
                d = raw[:, s, :].rearrange("p (k c) -> p k c", k=source.shape[1])
                sp.dma_start(d, source).then_inc(raw_in[s], 16)

            def gain_load(n, source, read=None):
                sp.wait_ge(*(read or (h_ready, n.count(0) * 2 + 2)))
                sp.dma_start(gain[:, n.slot(2), :], source.partition_broadcast(P)).then_inc(gain_in[n.slot(2)], 16)

            def across(w, column):
                return w.rearrange("(k p) c -> p k c", p=P)[:, :, column:column + 256]

            def along(w, row, column):
                return w.rearrange("(k p) c -> p k c", p=P)[:, row:row + 4, column:column + HALF]

            def mlp_loads(piece, up, down):
                ups = up.rearrange("(k p) (i c) -> i p k c", p=P, c=256)
                downs = down.rearrange("(i k p) c -> i p k c", p=P, k=2)
                piece_in(piece, ups[0])
                piece_in(piece + 1, ups[1])
                piece_in(piece + 2, downs[0])
                with sp.Fori(0, (FF_PAIRS - 2) // 2) as i:
                    here = Place(piece.fixed + 3, *piece.terms, (i, 4))
                    for j in range(2):
                        piece_in(here + 2 * j, ups[i * 2 + (2 + j)])
                        piece_in(here + (2 * j + 1), downs[i * 2 + (1 + j)])
                piece_in(piece + 31, downs[FF_PAIRS - 1])

            xt = x.rearrange("b (n p) d -> (b n) p d", p=P)
            sp.dma_start(xs[:, :, :], xt.rearrange("n p d -> p n d")).then_inc(x_in, 16)
            sp.dma_start(sq_c[:, :, :], square).then_inc(consts_in, 16)
            with sp.Fori(0, DEPTH) as L:
                gain_load(Place(0, (L, 2)), g_mix[L])
                for k in range(MIX_PIECES):
                    kind, i = mixer_piece(k)
                    piece = Place(k, (L, LAYER_PIECES))
                    column = {"rq": 0, "rk": 512, "rv": 1024, "rg": 2048, "sbq": 3072, "sbk": 4096, "sbv": 5120,
                              "ga": 6144, "gb": 7168}.get(kind)
                    if kind in ("sbv", "rv"):
                        source = along(w_in[L], 4 * (i % 2), column + HALF * (i // 2))
                    elif column is not None:
                        source = across(w_in[L], column + 256 * i)
                    elif kind == "wout":
                        source = along(w_out[L], 4 * (i // 2), HALF * (i % 2))
                    else:
                        source = across({"pret": p_ret, "psb": p_sb}[kind][L], 256 * i)
                    piece_in(piece, source, {11: 1, 12: None}.get(k, 0))
                    if k == 1:
                        gain_load(Place(1, (L, 2)), g_mlp[L])
                    if k == 7:
                        if True:
                            sp.dma_start(rope_c[:, :, :], rope).then_inc(consts_in, 16)
                            sp.dma_start(decay_c[:, :, :], decay).then_inc(consts_in, 16)
                            sp.dma_start(mask_c[:, :, :], mask).then_inc(consts_in, 16)
                mlp_loads(Place(MIX_PIECES, (L, LAYER_PIECES)), w_up[L], w_down[L])

            gain_load(Place(4), g_final)
            gain_load(Place(5), norm_mix_g_2[0])
            first = DEPTH * LAYER_PIECES
            for k in range(MIX2_PIECES):
                kind, i = mixer2_piece(k)
                column = {"pool": 0, "q": 256, "f": 1024, "v": 1792, "g": 2560}.get(kind)
                source = (along(w_out_2[0], 4 * (i // 2), HALF * (i % 2)) if kind == "wout"
                          else across(w_in_2[0], column + 256 * i))
                piece_in(Place(first + k), source)
                if k == 3:
                    gain_load(Place(6), norm_mlp_g_2[0], (x_ready, 2 + 2 * 5))
                if k == 3:
                    sp.wait_ge(x_ready, 2 + 2 * 2 * DEPTH)
                    sp.dma_start(lev_f[:, :, :], levels).then_inc(consts2_in, 16)
                    sp.dma_start(restart_c[:, :], restart).then_inc(consts2_in, 16)
                    sp.dma_start(counts_c[:, :, :], counts).then_inc(consts2_in, 16)
                    for row, source, n in ((LB_LOGIT, hgrn_lb_logits_2, HG_H), (HNORM, hgrn_norm_g_2, HG_H),
                                           (PSCALE, pool_scale_2, 2)):
                        sp.dma_start(hcol[:, row, 0:n], source[0].rearrange("(h p) -> p h", p=P),
                                     allow_slow_non_contiguous=True).then_inc(cols_in, 16)
                    sp.wait_ge(pool_w_zero, 1)
                    for g in range(len(WINDOWS)):
                        lo = 64 * (g % 2)
                        sp.dma_start(pool_w[lo:lo + 64, g // 2, lo:lo + 64], pool_w_2[0, g]).then_inc(pool_w_in, 16)
            mlp_loads(Place(first + MIX2_PIECES), w_up_2[0], w_down_2[0])
            gain_load(Place(7), final_norm_g_2, (h_ready, 4 + 2 * 5))
            ot = out.rearrange("b (n p) d -> (b n) p d", p=P)
            for t in range(TILES):
                sp.wait_ge(h_ready, 4 + 2 * 6 + t + 1)
                sp.dma_start(ot[t], htok[:, t, :]).then_inc(out_sent, 16)
            sp.wait_ge(out_sent, 16 * TILES)

        @block.tensor
        def _(pe):
            def mm(o, lhsT, rhs, start, stop):
                return pe.matmul(o, lhsT, rhs, start=start, stop=stop)

            def split_ready(piece):
                pe.wait_ge(lo_dve, piece.count(RAW_SLOTS + 1))
                pe.wait_ge(lo_pool, piece.count(RAW_SLOTS + 1))
                s = piece.slot(SPLIT_SLOTS)
                return w_hi[:, s, :], w_lo[:, s, :]

            def across(piece, use, moving):
                hi, lo = split_ready(piece)
                pe.wait_ge(pair_free, use.count(1))
                for m in range(2):
                    bank = ps[:, 2 * use.slot(2) + m, :]
                    for k in range(KT):
                        c = k * 256 + m * P
                        mm(bank, hi[:, c:c + P], moving[:, k, :], k == 0, False)
                        last = mm(bank[:, T:2 * T], lo[:, c:c + P], moving[:, k, 0:T], False, k == KT - 1)
                last.then_inc(piece_used, 1)

            def three(o, stationary, t, hi, lo, start, stop):
                a, b = stationary[:, t * P:(t + 1) * P], stationary[:, T + t * P:T + (t + 1) * P]
                mm(o, a, hi, start, False)
                mm(o, a, lo, False, False)
                return mm(o, b, hi, False, stop)

            def norm(n, use):
                for t in range(TILES):
                    pe.wait_ge(h_ready, n.count(0) * 2 + (4 + t + 1))
                    pe.wait_ge(pair_free, (use + t).count(1))
                    for k in range(KT):
                        bank = ps[:, 2 * (use + t).slot(2) + k // 4, (k % 4) * P:(k % 4 + 1) * P]
                        last = pe.transpose(bank, htok[:, t, k * P:(k + 1) * P], ident)
                    last.then_inc(h_turned, 1)
                pe.wait_ge(pair_free, (use + 1).count(3))

            def down(piece, i, first, last_one, slot):
                hi, lo = split_ready(piece)
                pe.wait_ge(u_lo, i.count(1))
                for t in range(TILES):
                    for k in range(2):
                        for c in range(2):
                            w = slice(k * D + c * HALF, k * D + (c + 1) * HALF)
                            last = three(ps[:, 4 + 2 * t + c, :], uT[:, slot, k, :], t, hi[:, w], lo[:, w],
                                         first and k == 0, last_one and k == 1)
                    if last_one and t == 0:
                        last.then_inc(acc_full, 1)
                last.then_inc(piece_used, 1)

            def mlp(n, stage, piece, use):
                norm(n, use)
                use = use + 2
                across(piece, use, hT)
                across(piece + 1, use + 1, hT)
                down(piece + 2, Place(0, *stage), True, False, 0)
                with pe.Fori(0, (FF_PAIRS - 2) // 2) as i:
                    here = Place(piece.fixed + 3, *piece.terms, (i, 4))
                    up = Place(use.fixed + 2, *use.terms, (i, 2))
                    for j in range(2):
                        across(here + 2 * j, up + j, hT)
                        down(here + (2 * j + 1), Place(1 + j, *stage, (i, 2)), False, False, (1 + j) % 2)
                down(piece + 31, Place(FF_PAIRS - 1, *stage), False, True, 1)

            def out_piece(piece, i):
                hi, lo = split_ready(piece)
                for t in range(TILES):
                    for k in range(4):
                        w = slice(k * HALF, (k + 1) * HALF)
                        last = three(ps[:, 4 + 2 * t + i % 2, :], hT[:, 4 * (i // 2) + k, :], t, hi[:, w], lo[:, w],
                                     i < 2 and k == 0, i >= 2 and k == 3)
                    if i == 3 and t == 0:
                        last.then_inc(acc_full, 1)
                last.then_inc(piece_used, 1)

            def causal(bank, lhs0, lhs1, rhs):
                mm(bank[:, 0:T], lhs0, rhs, True, True)
                return mm(bank[:, T:CAUSAL], lhs1, rhs[:, P:T], True, True)

            pe.wait_ge(consts_in, 16)
            with pe.Fori(0, DEPTH) as L:
                norm(Place(0, (L, 2)), Place(0, (L, LAYER_USES)))

                def stage(name, i):
                    pair, head = Place(i, (L, SB_H // 2)), Place(i, (L, RET_H))
                    if name == "sb_scores":
                        pe.wait_ge(pair_free, Place(mixer_use(7), (L, LAYER_USES)).count(3))
                        for j in range(2):
                            q, k = sbqk[:, i, j, :], sbqk[:, i, 2 + j, :]
                            last = causal(ps[:, 4 + j, :], k[:, 0:P], k[:, P:T], q)
                        last.then_inc(z_full, 1)
                    elif name == "sb_after":
                        pe.wait_ge(masked_rest, pair.count(1))
                        for j in range(2):
                            rest = zs[:, j, :]
                            bank = ps[:, 6 + j, :]
                            mm(bank[:, 0:T], later, rest[:, 0:T], True, False)
                            mm(bank[:, P:T], ones, rest[:, T:CAUSAL], False, True)
                            last = mm(bank[:, T:CAUSAL], later, rest[:, T:CAUSAL], True, True)
                        last.then_inc(after_full, 1)
                    elif name == "sb_out":
                        pe.wait_ge(weight_ready, pair.count(1))
                        pe.wait_ge(pair_free, Place(mixer_use(8 + 2 * (i // 2)), (L, LAYER_USES)).count(3))
                        for j in range(2):
                            o = ps[:, 6, j * T:(j + 1) * T]
                            c = (2 * i + j) * P
                            mm(o, sbv[:, 0, c:c + P], wts[:, j, 0:T], True, False)
                            last = mm(o[:, P:T], sbv[:, 1, c:c + P], wts[:, j, T:CAUSAL], False, True)
                        last.then_inc(sb_out, 1)
                    elif name == "rotate":
                        pe.wait_ge(pair_free, Place(mixer_use(15), (L, LAYER_USES)).count(3))
                        pe.wait_ge(z_scaled, Place(3, (L, 4)).count(1))
                        if i:
                            pe.wait_ge(rope_sin, Place(0, (L, 2)).count(1))
                        for j in range(2):
                            last = mm(ps[:, 4 + j, :], turn, retqkv[:, 2 * j:2 * j + 2, i, :], True, True)
                        last.then_inc(turned, 1)
                    elif name == "ret_scores":
                        pe.wait_ge(rope_done, Place(1, (L, 2)).count(1))
                        if i:
                            pe.wait_ge(ret_decayed, head.count(0))
                        k = retqkv[:, i, 1, :]
                        causal(ps[:, 4, :], k[:, 0:P], k[:, P:T], retqkv[:, i, 0, :]).then_inc(ret_scores, 1)
                    elif name == "ret_out":
                        pe.wait_ge(ret_decayed, head.count(1))
                        pe.wait_ge(pair_free, Place(mixer_use(16 + 2 * (i // 2)), (L, LAYER_USES)).count(3))
                        for e in range(2):
                            o = ps[:, 5, e * T:(e + 1) * T]
                            mm(o, retqkv[:, i, 2, e * P:(e + 1) * P], rs[:, 0:T], True, False)
                            last = mm(o[:, P:T], retqkv[:, i, 3, e * P:(e + 1) * P], rs[:, T:CAUSAL], False, True)
                        last.then_inc(ret_out, 1)
                    elif name == "ret_mean":
                        pe.wait_ge(ret_copied, head.count(1))
                        if i == 0:
                            pe.wait_ge(sb_lo, Place(3, (L, 4)).count(1))
                        for e in range(2):
                            last = mm(ps[:, 6, 0:T], mean_w, ry[:, i % 2, e, :], e == 0, e == 1)
                        last.then_inc(ret_mean, 1)
                    elif name == "ret_var":
                        pe.wait_ge(ret_squared, head.count(1))
                        for e in range(2):
                            last = mm(ps[:, 7, 0:T], mean_w, rsq[:, e, :], e == 0, e == 1)
                        last.then_inc(ret_var, 1)

                for k in range(MIX_PIECES):
                    kind, i = mixer_piece(k)
                    piece = Place(k, (L, LAYER_PIECES))
                    use = Place(mixer_use(k), (L, LAYER_USES))
                    if kind in ("sbv", "rv"):
                        hi, lo = split_ready(piece)
                        if i % 2 == 0:
                            pe.wait_ge(pair_free, use.count(1))
                        for t in range(TILES):
                            for kk in range(4):
                                w = slice(kk * HALF, (kk + 1) * HALF)
                                last = three(ps[:, 2 * use.slot(2) + t, :], hT[:, 4 * (i % 2) + kk, :], t, hi[:, w],
                                             lo[:, w], i % 2 == 0 and kk == 0, i % 2 == 1 and kk == 3)
                        last.then_inc(piece_used, 1)
                    elif kind == "wout":
                        pe.wait_ge(merged_lo, Place(2 * (i // 2) + 1, (L, 4)).count(1))
                        out_piece(piece, i)
                    else:
                        if kind == "pret":
                            pe.wait_ge(ret_lo, Place(RET_H - 1, (L, RET_H)).count(1))
                        if kind == "psb":
                            pe.wait_ge(sb_lo, Place(3, (L, 4)).count(1))
                        across(piece, use, {"pret": retT, "psb": sbT}.get(kind, hT))
                    for s in stages(k):
                        stage(*s)
                mlp(Place(1, (L, 2)), ((L, FF_PAIRS),), Place(MIX_PIECES, (L, LAYER_PIECES)),
                    Place(MIX_USES, (L, LAYER_USES)))

            first, use0 = DEPTH * LAYER_PIECES, DEPTH * LAYER_USES
            norm(Place(4), Place(use0))

            def pairs(n):
                kind, i = PAIRS[n]
                if n >= 2:
                    pe.wait_ge(pairs_placed, n - 1)
                o = ps[:, 4 + 2 * (n % 2):6 + 2 * (n % 2), :].rearrange("p b c -> p (b c)")
                if kind == "diag":
                    for j in range(6):
                        h, t = divmod(6 * i + j, 2)
                        c = slice(t * P, (t + 1) * P)
                        last = mm(o[:, j * P:(j + 1) * P], hk[:, h, c], hq[:, h, c], True, True)
                elif kind == "level":
                    m = LEVELS[i]
                    pe.wait_ge(x_first, i + 1)
                    pe.wait_ge(x_second, i + 1)
                    for j in range(HG_H * TILES):
                        side = (hz, hlog)[i % 2][:, j // 2, (j % 2) * P:(j % 2 + 1) * P]
                        rhs = side.rearrange("p (b two m) -> p b two m", two=2, m=m)[:, :, 1, :]
                        last = mm(o[:, j * CHUNK:(j + 1) * CHUNK].rearrange("p (b m) -> p b m", m=m), side, rhs,
                                  True, True)
                else:
                    pe.wait_ge(x_first, len(LEVELS) + 1)
                    pe.wait_ge(x_second, len(LEVELS) + 1)
                    side = (hz, hlog)[len(LEVELS) % 2]
                    for h in range(HG_H):
                        last = mm(o[:, h * P:(h + 1) * P], side[:, h, 0:P], side[:, h, P:T], True, True)
                last.then_inc(pairs_full, 1)

            for k in range(MIX2_PIECES):
                kind, i = mixer2_piece(k)
                piece, use = Place(first + k), Place(use0 + 2 + k)
                if kind == "v":
                    hi, lo = split_ready(piece)
                    pe.wait_ge(pair_free, use.count(1))
                    for t in range(TILES):
                        for kk in range(KT):
                            w = slice(kk * 256, (kk + 1) * 256)
                            last = three(ps[:, 2 * use.slot(2) + t, 0:256], hT[:, kk, :], t, hi[:, w], lo[:, w],
                                         kk == 0, kk == KT - 1)
                    last.then_inc(piece_used, 1)
                elif kind == "wout":
                    pe.wait_ge(y_lo, 2 if i < 2 else 4)
                    out_piece(piece, i)
                else:
                    across(piece, use, hT)
                for name, j in stages2(k):
                    if name == "pool":
                        pe.wait_ge(pool_step, 9)
                        pe.wait_ge(pool_w_in, 16 * len(WINDOWS))
                        for b in range(2):
                            last = mm(ps[:, 7, b * T:(b + 1) * T], pool_w[:, b, :], pmix[:, b, :], True, True)
                        last.then_inc(pool_full, 1)
                    elif (name, j) == ("diag", 0):
                        pe.wait_ge(f_k, 3)
                        pe.wait_ge(silu_done, 3)
                        pe.wait_ge(pool_scaled, 2)
                        pairs(0)
                    else:
                        pairs(PAIRS.index((name, j)))
                if k == 12:
                    pe.wait_ge(pairs_placed, len(PAIRS))
                    for r in range(3):
                        for j in range(2):
                            h = 2 * r + j
                            o, c = ps[:, 4 + r, j * T:(j + 1) * T], slice(h * P, (h + 1) * P)
                            mm(o[:, 0:P], hv[:, 0, c], st[:, 2 * h, :], True, True)
                            mm(o[:, P:T], hv[:, 0, c], cross[:, h, :], True, False)
                            last = mm(o[:, P:T], hv[:, 1, c], st[:, 2 * h + 1, :], False, True)
                        last.then_inc(o_full, 1)
                    for r in range(3):
                        pe.wait_ge(o_copied, r + 1)
                        pe.wait_ge(o_squared, r + 1)
                        mm(ps[:, 4 + r, :], mean_w, hfloor[:, 2 * r:2 * r + 2, :], True, True).then_inc(o_mean, 1)
            mlp(Place(5), ((1, DEPTH * FF_PAIRS),), Place(first + MIX2_PIECES), Place(use0 + MIX2_USES))

        @block.scalar
        def _(act):
            def convert(piece):
                act.wait_ge(raw_in[piece.slot(RAW_SLOTS)], piece.count(1, RAW_SLOTS) * 16)
                act.wait_ge(piece_used, piece.count(1))
                act.activation(w_hi[:, piece.slot(SPLIT_SLOTS), :], raw[:, piece.slot(RAW_SLOTS), :],
                               ACT.Copy).then_inc(hi_ready, 1)

            def carry_cross(piece, use):
                act.wait_ge(piece_used, piece.count(SPLIT_SLOTS + 1))
                b = 2 * use.slot(2)
                act.activation(carry[:, use.slot(2), :, :], ps[:, b:b + 2, T:2 * T], ACT.Copy).then_inc(pair_act, 1)

            def norm_sums(n):
                for t in range(TILES):
                    act.wait_ge(x_ready, n.count(0) * 2 + (t + 1))
                    act.activation(htok[:, t, :], xs[:, t, :], ACT.Square, scale=D ** -0.5,
                                   accum_out=sumsq[:, t:t + 1]).then_inc(sq_ready, 1)

            def norm(n, use, h=None):
                norm_sums(n)
                for t in range(TILES):
                    act.wait_ge(h_turned, (h or n).count(0) * 2 + (t + 1))
                    b = 2 * (use + t).slot(2)
                    act.activation(hT[:, :, t * P:(t + 1) * P],
                                   ps[:, b:b + 2, :].rearrange("p b (k c) -> p (b k) c", c=P),
                                   ACT.Copy).then_inc(pair_act, 1)

            def mlp(n, stage, piece, use, last, h=None):
                norm(n, use, h)
                use = use + 2

                def up(piece, use, i, slot):
                    carry_cross(piece, use)
                    convert(piece + 2)
                    act.wait_ge(u_squared, i.count(1))
                    act.activation(uT[:, slot, :, 0:T], usq[:, :, :], ACT.Copy).then_inc(u_hi, 1)

                def two(here, use, i, ahead=True):
                    for j in range(2):
                        up(here + 2 * j, use + j, i + j, j)
                        if ahead or j == 0:
                            convert(here + (2 * j + 3))

                up(piece, use, Place(0, *stage), 0)
                up(piece + 1, use + 1, Place(1, *stage), 1)
                convert(piece + 4)
                steps = (FF_PAIRS - 2) // 2 - (1 if last else 0)
                with act.Fori(0, steps) as i:
                    two(Place(piece.fixed + 3, *piece.terms, (i, 4)), Place(use.fixed + 2, *use.terms, (i, 2)),
                        Place(2, *stage, (i, 2)))
                if last:
                    two(piece + (3 + 4 * steps), use + (2 + 2 * steps), Place(2 + 2 * steps, *stage), False)
                else:
                    convert(piece + 33)

            act.wait_ge(x_in, 16)
            act.wait_ge(small_set, 4)
            convert(Place(0))
            convert(Place(1))
            with act.Fori(0, DEPTH) as L:
                norm(Place(0, (L, 2)), Place(0, (L, LAYER_USES)))

                def stage(name, i):
                    pair, head = Place(i, (L, SB_H // 2)), Place(i, (L, RET_H))
                    if name == "sb_scores":
                        act.wait_ge(z_full, pair.count(1))
                        act.activation(zs[:, :, :], ps[:, 4:6, 0:CAUSAL], ACT.Copy, scale=SB_SCALE).then_inc(z_scaled, 1)
                        act.wait_ge(z_abs, pair.count(1))
                        act.activation(soft[:, :, :], soft[:, :, :], ACT.Exp).then_inc(sb_exp, 1)
                        act.wait_ge(sb_exp, pair.count(1))
                        act.activation(soft[:, :, :], soft[:, :, :], ACT.Ln, bias=1.0).then_inc(softplus, 1)
                    elif name == "sb_after":
                        act.wait_ge(log_weight, pair.count(1))
                        act.activation(wts[:, :, :], logw[:, :, :], ACT.Exp).then_inc(weight_exp, 1)
                    elif name == "sb_out":
                        act.wait_ge(sb_out, pair.count(1))
                        act.activation(sbT[:, 2 * i:2 * i + 2, 0:T],
                                       ps[:, 6, :].rearrange("p (j t) -> p j t", j=2), ACT.Copy).then_inc(sb_hi, 1)
                    elif name == "ret_out":
                        act.wait_ge(ret_out, head.count(1))
                        act.activation(ry[:, i % 2, :, :], ps[:, 5, :].rearrange("p (e t) -> p e t", e=2),
                                       ACT.Copy).then_inc(ret_copied, 1)
                    elif name == "ret_mean":
                        act.wait_ge(ret_centred, head.count(1))
                        act.activation(rsq[:, :, :], ry[:, i % 2, :, :], ACT.Square).then_inc(ret_squared, 1)
                    elif name == "ret_var":
                        act.wait_ge(ret_var, head.count(1))
                        act.activation(rrstd[:, :], ps[:, 7, 0:T], ACT.Ln, bias=gn_eps[:, 0:1]).then_inc(ret_log, 1)
                        act.wait_ge(ret_log, head.count(1))
                        act.activation(rrstd[:, :], rrstd[:, :], ACT.Exp, scale=-0.5).then_inc(ret_rstd, 1)
                        act.wait_ge(ret_gated, head.count(1))
                        act.activation(retT[:, 2 * i:2 * i + 2, 0:T], ry[:, i % 2, :, :], ACT.Copy).then_inc(ret_hi, 1)

                for k in range(MIX_PIECES):
                    kind, i = mixer_piece(k)
                    piece = Place(k, (L, LAYER_PIECES))
                    use = Place(mixer_use(k), (L, LAYER_USES))
                    if kind in ("sbv", "rv"):
                        if i % 2 == 1:
                            act.wait_ge(piece_used, piece.count(SPLIT_SLOTS + 1))
                            b = ps[:, 2 * use.slot(2), :]
                            if kind == "sbv":
                                act.activation(sbv[:, 0, HALF * (i // 2):HALF * (i // 2 + 1)], b,
                                               ACT.Copy).then_inc(pair_act, 1)
                            else:
                                act.activation(retqkv[:, 2 * (i // 2):2 * (i // 2) + 2, 2, :],
                                               b.rearrange("p (h c) -> p h c", h=2), ACT.Copy).then_inc(pair_act, 1)
                    elif kind != "wout":
                        carry_cross(piece, use)
                    convert(piece + 2)
                    if kind in ("rg", "ga", "gb"):
                        gate = Place(k - 20, (L, 12))
                        act.wait_ge(pair_free, use.count(3))
                        src = gr[:, 2 * i:2 * i + 2, :] if kind == "rg" else gates[:, kind == "gb", 2 * i:2 * i + 2, :]
                        act.activation(gtmp[:, :, :], src, ACT.Exp, scale=-1.0).then_inc(gate_exp, 1)
                    if kind == "psb":
                        act.wait_ge(merged, Place(i, (L, 4)).count(1))
                        act.activation(hT[:, 2 * i:2 * i + 2, 0:T], gtmp[:, :, :], ACT.Copy).then_inc(merged_hi, 1)
                    for s in stages(k):
                        stage(*s)
                mlp(Place(1, (L, 2)), ((L, FF_PAIRS),), Place(MIX_PIECES, (L, LAYER_PIECES)),
                    Place(MIX_USES, (L, LAYER_USES)), False)

            first, use0 = DEPTH * LAYER_PIECES, DEPTH * LAYER_USES
            norm_sums(Place(4))
            norm(Place(5), Place(use0), Place(4))
            act.wait_ge(lb_step, 1)
            act.activation(hcol[:, LB_EXP, :], hcol[:, LB_EXP, :], ACT.Exp).then_inc(lb_step, 1)

            def exponents(n):
                side = (hz, hlog)[n % 2]
                act.wait_ge(e_first, n + 1)
                act.wait_ge(e_second, n + 1)
                if n == 0:
                    v = side[:, :, :].rearrange("p h (b two m) -> p (h b) two m", two=2, m=CHUNK)
                    b = hb[:, :, :].rearrange("p h (b two m) -> p (h b) two m", two=2, m=CHUNK)
                    act.activation(v[:, :, 1, :], b[:, :, 1, :], ACT.Exp)
                    act.activation(v[:, :, 0, :], v[:, :, 0, :], ACT.Exp).then_inc(e_exp, 1)
                elif n == len(LEVELS):
                    act.activation(side[:, :, 0:P], side[:, :, 0:P], ACT.Exp)
                    act.activation(side[:, :, P:P + CHUNK], hb[:, :, P:P + CHUNK], ACT.Exp)
                    act.activation(side[:, :, P + CHUNK:T], side[:, :, P + CHUNK:T], ACT.Exp).then_inc(e_exp, 1)
                else:
                    act.activation(side[:, :, :], side[:, :, :], ACT.Exp).then_inc(e_exp, 1)

            for k in range(MIX2_PIECES):
                kind, i = mixer2_piece(k)
                piece, use = Place(first + k), Place(use0 + 2 + k)
                if kind == "v":
                    act.wait_ge(piece_used, piece.count(SPLIT_SLOTS + 1))
                    act.activation(hv[:, 0, 256 * i:256 * (i + 1)], ps[:, 2 * use.slot(2), 0:256],
                                   ACT.Copy).then_inc(pair_act, 1)
                elif kind != "wout":
                    carry_cross(piece, use)
                convert(piece + 2)
                h2 = slice(2 * i, 2 * i + 2)
                if kind == "f":
                    act.wait_ge(pair_free, use.count(3))
                    act.activation(hfloor[:, h2, :], hz[:, h2, :], ACT.Exp, scale=-1.0).then_inc(f_ez, 1)
                    act.activation(hlog[:, h2, :], hz[:, h2, :], ACT.Abs).then_inc(f_abs, 1)
                    act.wait_ge(f_abs, i + 1)
                    act.activation(hlog[:, h2, :], hlog[:, h2, :], ACT.Exp, scale=-1.0).then_inc(f_exp, 1)
                    act.wait_ge(f_exp, i + 1)
                    act.activation(hlog[:, h2, :], hlog[:, h2, :], ACT.Ln, bias=1.0).then_inc(f_soft, 1)
                    act.wait_ge(f_floor, i + 1)
                    act.activation(hfloor[:, h2, :], hfloor[:, h2, :], ACT.Ln, bias=1.0).then_inc(f_floor_log, 1)
                    act.wait_ge(f_kexp_in, i + 1)
                    act.activation(hk[:, h2, :], hk[:, h2, :], ACT.Exp).then_inc(f_kexp, 1)
                if kind in ("q", "g"):
                    act.wait_ge(pair_free, use.count(3))
                    act.activation(htmp[:, :, :], (hq if kind == "q" else hg)[:, h2, :], ACT.Exp,
                                   scale=-1.0).then_inc(silu_exp, 1)
                if k == 5:
                    act.wait_ge(pool_full, 1)
                    act.wait_ge(cols_in, 48)
                    for b in range(2):
                        act.activation(py[:, b, :], ps[:, 7, b * T:(b + 1) * T], ACT.Copy,
                                       scale=hcol[:, PSCALE, b:b + 1]).then_inc(pool_scaled, 1)
                if 6 <= k <= 12:
                    exponents(k - 6)
                if k == 12:
                    exponents(7)
                    act.wait_ge(pool_scaled, 2)
                    act.activation(hT[:, 0:2, 0:T], py[:, :, :], ACT.Copy).then_inc(pool_hi, 1)
                    act.wait_ge(pairs_full, len(PAIRS))
                    b = 4 + 2 * ((len(PAIRS) - 1) % 2)
                    act.activation(cross[:, :, :], ps[:, b:b + 2, :].rearrange("p b (h c) -> p (b h) c", c=P)[:, 0:HG_H, :],
                                   ACT.Copy).then_inc(pairs_placed, 1)
                    for r in range(3):
                        act.wait_ge(o_full, r + 1)
                        o = ps[:, 4 + r, :].rearrange("p (h t) -> p h t", h=2)
                        act.activation(hfloor[:, 2 * r:2 * r + 2, :], o, ACT.Square).then_inc(o_squared, 1)
                    for r in range(3):
                        act.wait_ge(o_mean, r + 1)
                        v = hk[:, 2 * r:2 * r + 2, :]
                        act.activation(v, ps[:, 4 + r, :].rearrange("p (h t) -> p h t", h=2), ACT.Ln, scale=T / P,
                                       bias=rms_eps[:, 0:1]).then_inc(o_log, 1)
                        act.wait_ge(o_log, r + 1)
                        act.activation(v, v, ACT.Exp, scale=-0.5).then_inc(o_rstd, 1)
                    for r in range(3):
                        act.wait_ge(o_gated, r + 1)
                        act.activation(hT[:, 2 + 2 * r:4 + 2 * r, 0:T], ho[:, 2 * r:2 * r + 2, :],
                                       ACT.Copy).then_inc(o_hi, 1)
            mlp(Place(6), ((1, DEPTH * FF_PAIRS),), Place(first + MIX2_PIECES), Place(use0 + MIX2_USES), True, Place(5))
            norm_sums(Place(7))

        @block.gpsimd
        def _(pool):
            def convert(piece):
                pool.wait_ge(hi_ready, piece.count(1))
                s, r = piece.slot(SPLIT_SLOTS), piece.slot(RAW_SLOTS)
                half = slice(PIECE // 2, PIECE)
                pool.tensor_tensor(w_lo[:, s, half], raw[:, r, half], w_hi[:, s, half].bitcast(F32),
                                   ALU.subtract).then_inc(lo_pool, 1)

            def norm(n, eps):
                for t in range(TILES):
                    pool.wait_ge(sq_ready, n.count(0) * 2 + (t + 1))
                    pool.tensor_tensor(meansq[:, t:t + 1], sumsq[:, t:t + 1], eps, ALU.add).then_inc(mean_ready, 1)
                    pool.wait_ge(mean_ready, n.count(0) * 2 + (t + 1))
                    pool.tensor_tensor(rstd[:, t:t + 1], meansq[:, t:t + 1], minus_half[:, t:t + 1],
                                       ALU.pow).then_inc(rstd_ready, 1)

            def mlp(n, eps, piece, last):
                norm(n, eps)
                convert(piece + 2)
                convert(piece + 3)
                convert(piece + 4)
                steps = (FF_PAIRS - 2) // 2 - (1 if last else 0)
                with pool.Fori(0, steps) as i:
                    here = Place(piece.fixed + 5, *piece.terms, (i, 4))
                    for j in range(4):
                        convert(here + j)
                for j in range(3 if last else 1):
                    convert(piece + (5 + 4 * steps + j))

            pool.memset(minus_half[:, :], -0.5).then_inc(small_set, 1)
            pool.memset(gn_eps[:, :], GN_EPS).then_inc(small_set, 1)
            pool.memset(norm_eps[:, 0:1], NORM_EPS).then_inc(small_set, 1)
            pool.memset(norm_eps[:, 1:2], RMS_EPS).then_inc(small_set, 1)
            pool.wait_ge(small_set, 4)
            pool.sem_inc(lo_dve, RAW_SLOTS)
            pool.sem_inc(lo_pool, RAW_SLOTS)
            pool.sem_inc(piece_used, SPLIT_SLOTS)
            pool.sem_inc(pair_free, 2)
            pool.sem_inc(x_ready, 2)
            pool.sem_inc(h_ready, 4)
            convert(Place(0))
            convert(Place(1))
            with pool.Fori(0, DEPTH) as L:
                norm(Place(0, (L, 2)), norm_eps[:, 0:1])
                for k in range(MIX_PIECES):
                    convert(Place(k + 2, (L, LAYER_PIECES)))
                    for name, i in stages(k):
                        pair = Place(i, (L, SB_H // 2))
                        if name == "sb_scores":
                            pool.wait_ge(neg_log_rest, pair.count(1))
                            pool.tensor_tensor(zs[:, :, :], zs[:, :, :], mask_c[:, :, :], ALU.mult).then_inc(masked_rest, 1)
                        elif name == "sb_after":
                            pool.wait_ge(weight_exp, pair.count(1))
                            pool.tensor_tensor(wts[:, :, :], wts[:, :, :], mask_c[:, :, :], ALU.mult).then_inc(weight_ready, 1)
                        elif name == "rotate":
                            pool.wait_ge(turned, Place(i, (L, 2)).count(1))
                            v = retqkv[:, :, i, :]
                            pool.tensor_tensor(v, v, rope_c[:, 0:1, :].to_broadcast([P, RET_H, T]),
                                               ALU.mult).then_inc(rope_cos, 1)
                mlp(Place(1, (L, 2)), norm_eps[:, 0:1], Place(MIX_PIECES, (L, LAYER_PIECES)), False)

            first = DEPTH * LAYER_PIECES
            norm(Place(4), norm_eps[:, 0:1])
            norm(Place(5), norm_eps[:, 1:2])
            pool.memset(pads[:, :, :, 0:PAD], 0.0).then_inc(pads_zero, 1)
            pool.memset(pool_w[:, :, :], 0.0).then_inc(pool_w_zero, 1)
            pool.memset(rms_eps[:, :], RMS_EPS).then_inc(pads_zero, 1)
            pool.wait_ge(consts2_in, 48)
            for n in range(len(LEVELS)):
                o = lev_c[:, n, :].rearrange("p (j c) -> p j c", c=CHUNK)
                pool.tensor_copy(o, lev_f[:, n:n + 1, :].to_broadcast([P, HG_H * TILES, CHUNK])).then_inc(levels_set, 1)
            lbs = [hcol[:, r, :] for r in (LB_LOGIT, LB_EXP, LB, ONE_LESS)]
            pool.wait_ge(cols_in, 48)
            pool.tensor_tensor(lbs[1], lbs[0], lbs[0], ALU.subtract).then_inc(lb_step, 1)
            pool.wait_ge(lb_step, 3)
            pool.tensor_tensor(hcol[:, LB_P, :], lbs[1], hcol[:, LB_INV, :], ALU.mult).then_inc(lb_step, 1)
            pool.wait_ge(lb_step, 4)
            pool.tensor_tensor(lbs[2], hcol[:, LB_P, :], hcol[:, LB_P, :], ALU.subtract).then_inc(lb_step, 1)
            pool.wait_ge(lb_step, 5)
            pool.tensor_scalar(lbs[3], lbs[2], -1.0, 1.0, ALU.mult, ALU.add).then_inc(lb_step, 1)
            pool.wait_ge(lb_step, 6)

            def first_gaps(n):
                if n >= 2:
                    pool.wait_ge(pairs_full, n + 1)
                else:
                    pool.wait_ge(f_cum, 3)
                    pool.wait_ge(f_k, 3)
                m = LEVELS[n]
                v = (hz, hlog)[n % 2][:, :, :].rearrange("p h (b two m) -> p (h b) two m", two=2, m=m)
                b = hb[:, :, :].rearrange("p h (b two m) -> p (h b) two m", two=2, m=m)
                end = b[:, :, 0, m - 1:m].to_broadcast([P, HG_H * T // (2 * m), m])
                pool.tensor_tensor(v[:, :, 0, :], end, b[:, :, 0, :], ALU.subtract).then_inc(e_first, 1)

            def first_side(n):
                m = LEVELS[n] if n < len(LEVELS) else P
                pool.wait_ge(e_exp, n + 1)
                v = (hz, hlog)[n % 2][:, :, :].rearrange("p h (b two m) -> p (h b) two m", two=2, m=m)[:, :, 0, :]
                kk = hk[:, :, :].rearrange("p h (b two m) -> p (h b) two m", two=2, m=m)[:, :, 0, :]
                pool.tensor_tensor(v, v, kk, ALU.mult).then_inc(x_first, 1)

            for k in range(MIX2_PIECES):
                convert(Place(first + k + 2))
                kind, i = mixer2_piece(k)
                if kind == "f":
                    pool.wait_ge(f_kexp, i + 1)
                    v = hk[:, 2 * i:2 * i + 2, :]
                    pool.tensor_tensor(v, v, lbs[3][:, 2 * i:2 * i + 2].unsqueeze(2).to_broadcast([P, 2, T]),
                                       ALU.mult).then_inc(f_k, 1)
                if kind == "pool":
                    use = Place(DEPTH * LAYER_USES + 2 + k)
                    pool.wait_ge(pair_free, use.count(3))
                    pool.wait_ge(pads_zero, 2)
                    pool.wait_ge(consts2_in, 48)
                    for j, w in enumerate((1, 2, 4, 8)):
                        b = slice(0 if j < 2 else 1, 2)
                        pool.tensor_tensor(pads[:, j + 1, b, PAD:], pads[:, j, b, PAD:], pads[:, j, b, PAD - w:PAD + T - w],
                                           ALU.add).then_inc(pool_step, 1)
                        pool.wait_ge(pool_step, j + 1)
                    for g in range(len(WINDOWS)):
                        rows = slice(64 * (g % 2), 64 * (g % 2) + 64)
                        pool.tensor_tensor(pmix[rows, g // 2, :], pads[rows, g + 1, g // 2, PAD:],
                                           counts_c[rows, g // 2, :], ALU.mult).then_inc(pool_step, 1)
                    pool.wait_ge(pool_step, 8)
                    pool.tensor_tensor(pmix[:, :, :], pmix[:, :, :], pads[:, 0, :, PAD:],
                                       ALU.subtract).then_inc(pool_step, 1)
                if k == 5:
                    first_gaps(0)
                if 6 <= k <= 11:
                    first_side(k - 6)
                    first_gaps(k - 5)
                if k == 12:
                    first_side(6)
                    n = len(LEVELS)
                    pool.wait_ge(pairs_full, n + 1)
                    side = (hz, hlog)[n % 2]
                    pool.tensor_tensor(side[:, :, CHUNK:P], hb[:, :, P - 1:P].to_broadcast([P, HG_H, CHUNK]),
                                       hb[:, :, CHUNK:P], ALU.subtract).then_inc(e_first, 1)
                    first_side(7)
                if kind == "g":
                    pool.wait_ge(silu_done, 4 + i)
                    v = hg[:, 2 * i:2 * i + 2, :]
                    pool.tensor_tensor(v, v, hcol[:, HNORM, 2 * i:2 * i + 2].unsqueeze(2).to_broadcast([P, 2, T]),
                                       ALU.mult).then_inc(g_scaled, 1)
            mlp(Place(6), norm_eps[:, 1:2], Place(first + MIX2_PIECES), True)
            norm(Place(7), norm_eps[:, 1:2])

        @block.vector
        def _(dve):
            def convert(piece):
                dve.wait_ge(hi_ready, piece.count(1))
                s, r = piece.slot(SPLIT_SLOTS), piece.slot(RAW_SLOTS)
                half = slice(0, PIECE // 2)
                dve.tensor_tensor(w_lo[:, s, half], raw[:, r, half], w_hi[:, s, half].bitcast(F32),
                                  ALU.subtract).then_inc(lo_dve, 1)

            def split_lo(o, hi, value):
                return dve.tensor_tensor(o, value, hi.bitcast(F32), ALU.subtract)

            def add_cross(use, o):
                dve.wait_ge(pair_act, use.count(1))
                b = 2 * use.slot(2)
                dve.tensor_tensor(o, ps[:, b:b + 2, 0:T], carry[:, use.slot(2), :, :], ALU.add).then_inc(pair_free, 1)

            def norm_rows(n, o=htok, done=h_ready):
                for t in range(TILES):
                    dve.wait_ge(rstd_ready, n.count(0) * 2 + (t + 1))
                    dve.wait_ge(gain_in[n.slot(2)], n.count(1, 2) * 16)
                    dve.scalar_tensor_tensor(out=o[:, t, :], in0=xs[:, t, :], scalar=rstd[:, t:t + 1],
                                             in1=gain[:, n.slot(2), :], op0=ALU.mult, op1=ALU.mult).then_inc(done, 1)

            def norm(n, use):
                norm_rows(n)
                for t in range(TILES):
                    dve.wait_ge(pair_act, (use + t).count(1))
                    b = 2 * (use + t).slot(2)
                    split_lo(hT[:, :, T + t * P:T + (t + 1) * P], hT[:, :, t * P:(t + 1) * P],
                             ps[:, b:b + 2, :].rearrange("p b (k c) -> p (b k) c", c=P)).then_inc(pair_free, 1)

            def residual(event, piece):
                for t in range(TILES):
                    if t == 0:
                        dve.wait_ge(acc_full, event.count(1))
                    else:
                        dve.wait_ge(piece_used, piece.count(SPLIT_SLOTS + 1))
                    dve.tensor_tensor(xs[:, t, :], ps[:, 4 + 2 * t:6 + 2 * t, :].rearrange("p b c -> p (b c)"),
                                      xs[:, t, :], ALU.add).then_inc(x_ready, 1)

            def mlp(n, stage, piece, use, last, h=None):
                norm(n, use)
                use = use + 2

                def up(piece, use, i, slot, before):
                    if before:
                        dve.wait_ge(u_lo, i.count(0))
                    dve.wait_ge(pair_act, use.count(1))
                    b = 2 * use.slot(2)
                    dve.tensor_tensor(us[:, :, :], ps[:, b:b + 2, 0:T], carry[:, use.slot(2), :, :],
                                      ALU.add).then_inc(pair_free, 1)
                    dve.wait_ge(pair_free, use.count(3))
                    dve.scalar_tensor_tensor(out=usq[:, :, :], in0=us[:, :, :], scalar=0.0, in1=us[:, :, :],
                                             op0=ALU.max, op1=ALU.mult).then_inc(u_squared, 1)
                    convert(piece + 2)
                    dve.wait_ge(u_hi, i.count(1))
                    split_lo(uT[:, slot, :, T:2 * T], uT[:, slot, :, 0:T], usq[:, :, :]).then_inc(u_lo, 1)

                def two(here, use, i, ahead=True):
                    for j in range(2):
                        up(here + 2 * j, use + j, i + j, j, True)
                        if ahead or j == 0:
                            convert(here + (2 * j + 3))

                up(piece, use, Place(0, *stage), 0, False)
                up(piece + 1, use + 1, Place(1, *stage), 1, True)
                convert(piece + 4)
                steps = (FF_PAIRS - 2) // 2 - (1 if last else 0)
                with dve.Fori(0, steps) as i:
                    two(Place(piece.fixed + 3, *piece.terms, (i, 4)), Place(use.fixed + 2, *use.terms, (i, 2)),
                        Place(2, *stage, (i, 2)))
                if last:
                    two(piece + (3 + 4 * steps), use + (2 + 2 * steps), Place(2 + 2 * steps, *stage), False)
                residual(h or n, piece + 31)
                if not last:
                    convert(piece + 33)

            dve.wait_ge(x_in, 16)
            convert(Place(0))
            convert(Place(1))
            with dve.Fori(0, DEPTH) as L:
                norm(Place(0, (L, 2)), Place(0, (L, LAYER_USES)))

                def stage(name, i):
                    pair, head = Place(i, (L, SB_H // 2)), Place(i, (L, RET_H))
                    if name == "sb_scores":
                        dve.wait_ge(z_scaled, pair.count(1))
                        dve.scalar_tensor_tensor(out=soft[:, :, :], in0=zs[:, :, :], scalar=-1.0, in1=zs[:, :, :],
                                                 op0=ALU.mult, op1=ALU.min).then_inc(z_abs, 1)
                        dve.wait_ge(softplus, pair.count(1))
                        dve.scalar_tensor_tensor(out=logw[:, :, :], in0=zs[:, :, :], scalar=0.0, in1=soft[:, :, :],
                                                 op0=ALU.min, op1=ALU.subtract).then_inc(log_beta, 1)
                        dve.wait_ge(log_beta, pair.count(1))
                        dve.scalar_tensor_tensor(out=zs[:, :, :], in0=zs[:, :, :], scalar=0.0, in1=soft[:, :, :],
                                                 op0=ALU.max, op1=ALU.add).then_inc(neg_log_rest, 1)
                    elif name == "sb_after":
                        dve.wait_ge(after_full, pair.count(1))
                        dve.tensor_tensor(logw[:, :, :], logw[:, :, :], ps[:, 6:8, 0:CAUSAL],
                                          ALU.subtract).then_inc(log_weight, 1)
                    elif name == "sb_out":
                        dve.wait_ge(sb_hi, pair.count(1))
                        split_lo(sbT[:, 2 * i:2 * i + 2, T:2 * T], sbT[:, 2 * i:2 * i + 2, 0:T],
                                 ps[:, 6, :].rearrange("p (j t) -> p j t", j=2)).then_inc(sb_lo, 1)
                    elif name == "rotate":
                        part = Place(i, (L, 2))
                        dve.wait_ge(turned, part.count(1))
                        if i:
                            dve.wait_ge(rope_done, part.count(0))
                        v, tmp = retqkv[:, :, i, :], ry[:, :, :, :].rearrange("p a e t -> p (a e) t")
                        dve.tensor_tensor(tmp, ps[:, 4:6, :].rearrange("p b (h t) -> p (b h) t", h=2),
                                          rope_c[:, 1:2, :].to_broadcast([P, RET_H, T]), ALU.mult).then_inc(rope_sin, 1)
                        dve.wait_ge(rope_cos, part.count(1))
                        dve.wait_ge(rope_sin, part.count(1))
                        dve.tensor_tensor(v, v, tmp, ALU.add).then_inc(rope_done, 1)
                    elif name == "ret_scores":
                        dve.wait_ge(ret_scores, head.count(1))
                        dve.tensor_tensor(rs[:, :], ps[:, 4, 0:CAUSAL], decay_c[:, i, :], ALU.mult).then_inc(ret_decayed, 1)
                    elif name == "ret_mean":
                        dve.wait_ge(ret_mean, head.count(1))
                        y = ry[:, i % 2, :, :]
                        dve.tensor_tensor(y, y, ps[:, 6:7, 0:T].to_broadcast([P, 2, T]), ALU.subtract).then_inc(ret_centred, 1)
                    elif name == "ret_var":
                        y = ry[:, i % 2, :, :]
                        dve.wait_ge(ret_rstd, head.count(1))
                        dve.tensor_tensor(y, y, rrstd[:, :].unsqueeze(1).to_broadcast([P, 2, T]), ALU.mult).then_inc(ret_normed, 1)
                        dve.wait_ge(ret_normed, head.count(1))
                        dve.wait_ge(gate_done, head.count(1))
                        dve.tensor_tensor(y, y, gr[:, 2 * i:2 * i + 2, :], ALU.mult).then_inc(ret_gated, 1)
                        dve.wait_ge(ret_hi, head.count(1))
                        split_lo(retT[:, 2 * i:2 * i + 2, T:2 * T], retT[:, 2 * i:2 * i + 2, 0:T], y).then_inc(ret_lo, 1)

                for k in range(MIX_PIECES):
                    kind, i = mixer_piece(k)
                    piece = Place(k, (L, LAYER_PIECES))
                    use = Place(mixer_use(k), (L, LAYER_USES))
                    if kind in ("sbv", "rv"):
                        if i % 2 == 1:
                            dve.wait_ge(pair_act, use.count(1))
                            b = ps[:, 2 * use.slot(2) + 1, :]
                            if kind == "sbv":
                                dve.tensor_copy(sbv[:, 1, HALF * (i // 2):HALF * (i // 2 + 1)], b).then_inc(pair_free, 1)
                            else:
                                dve.tensor_copy(retqkv[:, 2 * (i // 2):2 * (i // 2) + 2, 3, :],
                                                b.rearrange("p (h c) -> p h c", h=2)).then_inc(pair_free, 1)
                    elif kind == "sbq":
                        add_cross(use, sbqk[:, i, 0:2, :])
                    elif kind == "sbk":
                        add_cross(use, sbqk[:, i, 2:4, :])
                    elif kind in ("rq", "rk"):
                        add_cross(use, retqkv[:, 2 * i:2 * i + 2, kind == "rk", :])
                    elif kind == "rg":
                        add_cross(use, gr[:, 2 * i:2 * i + 2, :])
                    elif kind in ("ga", "gb"):
                        add_cross(use, gates[:, kind == "gb", 2 * i:2 * i + 2, :])
                    elif kind in ("pret", "psb"):
                        if kind == "pret" and i == 0:
                            dve.wait_ge(gate_sig, Place(11, (L, 12)).count(1))
                        elif kind == "pret" or i == 0:
                            dve.wait_ge(branch_a, Place((i - 1) % 4, (L, 4)).count(1))
                        else:
                            dve.wait_ge(merged_lo, Place(i - 1, (L, 4)).count(1))
                        add_cross(use, gtmp[:, :, :])
                        a, g = gates[:, 0, 2 * i:2 * i + 2, :], gates[:, kind == "psb", 2 * i:2 * i + 2, :]
                        quarter = Place(i, (L, 4))
                        dve.wait_ge(pair_free, use.count(3))
                        if kind == "pret":
                            dve.tensor_tensor(a, a, gtmp[:, :, :], ALU.mult).then_inc(branch_a, 1)
                        else:
                            dve.tensor_tensor(gtmp[:, :, :], g, gtmp[:, :, :], ALU.mult).then_inc(branch_b, 1)
                            dve.wait_ge(branch_b, quarter.count(1))
                            dve.tensor_tensor(gtmp[:, :, :], a, gtmp[:, :, :], ALU.add).then_inc(merged, 1)
                            dve.wait_ge(merged_hi, quarter.count(1))
                            split_lo(hT[:, 2 * i:2 * i + 2, T:2 * T], hT[:, 2 * i:2 * i + 2, 0:T],
                                     gtmp[:, :, :]).then_inc(merged_lo, 1)
                    convert(piece + 2)
                    if kind in ("rg", "ga", "gb"):
                        gate = Place(k - 20, (L, 12))
                        dve.wait_ge(gate_exp, gate.count(1))
                        dve.tensor_scalar(gtmp[:, :, :], gtmp[:, :, :], 1.0, None, ALU.add).then_inc(gate_plus, 1)
                        dve.wait_ge(gate_plus, gate.count(1))
                        if kind == "rg":
                            g = gr[:, 2 * i:2 * i + 2, :]
                            dve.reciprocal(gtmp[:, :, :], gtmp[:, :, :]).then_inc(gate_sig, 1)
                            dve.wait_ge(gate_sig, gate.count(1))
                            dve.tensor_tensor(g, g, gtmp[:, :, :], ALU.mult).then_inc(gate_done, 1)
                        else:
                            dve.reciprocal(gates[:, kind == "gb", 2 * i:2 * i + 2, :], gtmp[:, :, :]).then_inc(gate_sig, 1)
                    if k == 8:
                        dve.wait_ge(consts_in, Place(1, (L, 3)).count(3) * 16)
                    for s in stages(k):
                        stage(*s)
                    if k == MIX_PIECES - 1:
                        residual(Place(0, (L, 2)), piece)
                mlp(Place(1, (L, 2)), ((L, FF_PAIRS),), Place(MIX_PIECES, (L, LAYER_PIECES)),
                    Place(MIX_USES, (L, LAYER_USES)), False)

            first, use0 = DEPTH * LAYER_PIECES, DEPTH * LAYER_USES
            norm_rows(Place(4), xs, x_ready)
            norm(Place(5), Place(use0))
            dve.wait_ge(lb_step, 2)
            dve.reciprocal(hcol[:, LB_INV, :], hcol[:, LB_EXP, :]).then_inc(lb_step, 1)

            def second_gaps(n):
                if n == 0:
                    dve.wait_ge(f_cum, 3)
                    dve.tensor_tensor(btail[:, :, :], hb[:, :, CHUNK - 1:CHUNK], hb[:, :, P - 1:P],
                                      ALU.add).then_inc(e_second, 1)
                    return
                if n >= 2:
                    dve.wait_ge(pairs_full, n + 1)
                side = (hz, hlog)[n % 2]
                if n == len(LEVELS):
                    dve.tensor_tensor(side[:, :, 0:CHUNK], btail[:, :, :].to_broadcast([P, HG_H, CHUNK]),
                                      hb[:, :, 0:CHUNK], ALU.subtract)
                    dve.tensor_tensor(side[:, :, P + CHUNK:T], hb[:, :, P + CHUNK - 1:P + CHUNK].to_broadcast([P, HG_H, CHUNK]),
                                      hb[:, :, P + CHUNK:T], ALU.add).then_inc(e_second, 1)
                    return
                m = LEVELS[n]
                v = side[:, :, :].rearrange("p h (b two m) -> p (h b) two m", two=2, m=m)
                b = hb[:, :, :].rearrange("p h (b two m) -> p (h b) two m", two=2, m=m)
                end = b[:, :, 0, m - 1:m].to_broadcast([P, HG_H * T // (2 * m), m])
                dve.tensor_tensor(v[:, :, 1, :], b[:, :, 1, :], end, ALU.subtract).then_inc(e_second, 1)

            def second_side(n):
                m = LEVELS[n] if n < len(LEVELS) else P
                dve.wait_ge(e_exp, n + 1)
                if n == 0:
                    dve.wait_ge(silu_done, 3)
                v = (hz, hlog)[n % 2][:, :, :].rearrange("p h (b two m) -> p (h b) two m", two=2, m=m)[:, :, 1, :]
                q = hq[:, :, :].rearrange("p h (b two m) -> p (h b) two m", two=2, m=m)[:, :, 1, :]
                dve.tensor_tensor(v, v, q, ALU.mult).then_inc(x_second, 1)

            def put(n):
                dve.wait_ge(pairs_full, n + 1)
                kind, i = PAIRS[n]
                o = ps[:, 4 + 2 * (n % 2):6 + 2 * (n % 2), :].rearrange("p b c -> p (b c)")[:, 0:HG_H * P]
                if kind == "diag":
                    dve.tensor_tensor(st[:, 6 * i:6 * i + 6, :], o.rearrange("p (j c) -> p j c", c=P),
                                      ident.unsqueeze(1).to_broadcast([P, 6, P]), ALU.mult).then_inc(pairs_placed, 1)
                else:
                    m = LEVELS[i]
                    dve.wait_ge(pairs_placed, n)
                    if i == 0:
                        dve.wait_ge(levels_set, len(LEVELS))
                    dve.copy_predicated(
                        out=st[:, :, :].rearrange("p j (b two m) -> p (j b) two m", two=2, m=m)[:, :, 1, :],
                        mask=lev_c[:, i, :].rearrange("p (a m) -> p a m", m=m),
                        data=o.rearrange("p (a m) -> p a m", m=m)).then_inc(pairs_placed, 1)

            for k in range(MIX2_PIECES):
                kind, i = mixer2_piece(k)
                piece, use = Place(first + k), Place(use0 + 2 + k)
                h2 = slice(2 * i, 2 * i + 2)
                if kind == "v":
                    dve.wait_ge(pair_act, use.count(1))
                    dve.tensor_copy(hv[:, 1, 256 * i:256 * (i + 1)],
                                    ps[:, 2 * use.slot(2) + 1, 0:256]).then_inc(pair_free, 1)
                elif kind == "f":
                    add_cross(use, hz[:, h2, :])
                elif kind == "pool":
                    add_cross(use, pads[:, 0, :, PAD:])
                elif kind in ("q", "g"):
                    add_cross(use, (hq if kind == "q" else hg)[:, h2, :])
                convert(piece + 2)
                if kind == "f":
                    z, lg, fl = hz[:, h2, :], hlog[:, h2, :], hfloor[:, h2, :]
                    if i == 0:
                        dve.wait_ge(lb_step, 6)
                        dve.wait_ge(consts2_in, 48)
                    dve.wait_ge(f_ez, i + 1)
                    dve.scalar_tensor_tensor(out=fl, in0=fl, scalar=2.0 ** 63,
                                             in1=hcol[:, LB, h2].unsqueeze(2).to_broadcast([P, 2, T]),
                                             op0=ALU.min, op1=ALU.mult).then_inc(f_floor, 1)
                    dve.wait_ge(f_soft, i + 1)
                    dve.scalar_tensor_tensor(out=lg, in0=z, scalar=0.0, in1=lg, op0=ALU.min,
                                             op1=ALU.subtract).then_inc(f_ls, 1)
                    dve.wait_ge(f_ls, i + 1)
                    dve.tensor_tensor(hk[:, h2, :], lg, z, ALU.subtract).then_inc(f_kexp_in, 1)
                    dve.wait_ge(f_floor_log, i + 1)
                    dve.wait_ge(f_kexp_in, i + 1)
                    dve.tensor_tensor(lg, lg, fl, ALU.add).then_inc(f_log, 1)
                    dve.wait_ge(f_log, i + 1)
                    dve.tensor_tensor_scan(out=hb[:, h2, :].rearrange("p h t -> p (h t)"), data0=restart_c[:, :],
                                           data1=lg.rearrange("p h t -> p (h t)"), initial=0.0, op0=ALU.mult,
                                           op1=ALU.add).then_inc(f_cum, 1)
                if kind in ("q", "g"):
                    n = i + (3 if kind == "g" else 0)
                    v = (hq if kind == "q" else hg)[:, h2, :]
                    dve.wait_ge(silu_exp, n + 1)
                    dve.tensor_scalar(htmp[:, :, :], htmp[:, :, :], 1.0, None, ALU.add).then_inc(silu_plus, 1)
                    dve.wait_ge(silu_plus, n + 1)
                    dve.reciprocal(htmp[:, :, :], htmp[:, :, :]).then_inc(silu_sig, 1)
                    dve.wait_ge(silu_sig, n + 1)
                    dve.tensor_tensor(v, v, htmp[:, :, :], ALU.mult).then_inc(silu_done, 1)
                if k == 5:
                    second_gaps(0)
                if k == 7:
                    put(0)
                    put(1)
                if 6 <= k <= 12:
                    second_side(k - 6)
                if 7 <= k <= 12:
                    put(k - 5)
                if 6 <= k <= 11:
                    second_gaps(k - 5)
                if k == 12:
                    second_gaps(7)
                    second_side(7)
                    put(8)
                    dve.wait_ge(pool_hi, 1)
                    split_lo(hT[:, 0:2, T:2 * T], hT[:, 0:2, 0:T], py[:, :, :]).then_inc(y_lo, 1)
                    for r in range(3):
                        dve.wait_ge(o_squared, r + 1)
                        dve.tensor_copy(ho[:, 2 * r:2 * r + 2, :],
                                        ps[:, 4 + r, :].rearrange("p (h t) -> p h t", h=2)).then_inc(o_copied, 1)
                    for r in range(3):
                        v, hs = ho[:, 2 * r:2 * r + 2, :], slice(2 * r, 2 * r + 2)
                        dve.wait_ge(o_rstd, r + 1)
                        dve.wait_ge(o_copied, r + 1)
                        dve.tensor_tensor(v, v, hk[:, hs, :], ALU.mult).then_inc(o_normed, 1)
                        dve.wait_ge(o_normed, r + 1)
                        dve.wait_ge(g_scaled, r + 1)
                        dve.tensor_tensor(v, v, hg[:, hs, :], ALU.mult).then_inc(o_gated, 1)
                        dve.wait_ge(o_hi, r + 1)
                        split_lo(hT[:, 2 + 2 * r:4 + 2 * r, T:2 * T], hT[:, 2 + 2 * r:4 + 2 * r, 0:T], v).then_inc(y_lo, 1)
                if k == MIX2_PIECES - 1:
                    residual(Place(4), piece)
            mlp(Place(6), ((1, DEPTH * FF_PAIRS),), Place(first + MIX2_PIECES), Place(use0 + MIX2_USES), True, Place(5))
            norm_rows(Place(7))


def slab_base(nc, size):
    return nc.sbuf_base - size


_INS = ["x", "w_in", "p_ret", "p_sb", "w_out", "w_up", "w_down", "g_mix", "g_mlp", "g_final", "norm_mix_g_2", "w_in_2",
        "pool_w_2", "pool_scale_2", "hgrn_lb_logits_2", "hgrn_norm_g_2", "w_out_2", "norm_mlp_g_2", "w_up_2",
        "w_down_2", "final_norm_g_2"]


def kernel(**inputs):
    import concourse.bacc as _bacc
    from concourse.bass_utils import run_bass_kernel_spmd as _run

    nc = _bacc.Bacc("TRN2", target_bir_lowering=False, num_devices=1)
    arrays, args = {}, []
    for name, a in [(n, np.ascontiguousarray(inputs[n])) for n in _INS] + list(constants().items()):
        arrays[f"in_{name}_dram"] = a
        args.append(nc.dram_tensor(f"in_{name}_dram", a.shape, mybir.dt.from_np(a.dtype), kind="ExternalInput").ap())
    args.append(nc.dram_tensor("out_0_dram", (1, T, D), F32, kind="ExternalOutput").ap())
    build(nc, *args)
    return _run(nc, [arrays], core_ids=[0]).results[0]["out_0_dram"]
```

```python
import math
from contextlib import ExitStack

import numpy as np

import concourse.bass as bass
from concourse import mybir

F32 = mybir.dt.float32
F32R = mybir.dt.float32r
U32 = mybir.dt.uint32
U8 = mybir.dt.uint8
ALU = mybir.AluOpType
ACT = mybir.ActivationFunctionType

P = 128
D = 1024
T = 256
TILES = T // P
KT = D // P
DEPTH = 2
HALF = 512
RET_H, SB_H, HG_H = 4, 8, 6
CAUSAL = T + P
SB_SCALE = P ** -0.5
CHUNK = 64
LEVELS = (64, 32, 16, 8, 4, 2, 1)
WINDOWS = (2, 4, 8, 16)
PAD = 16
GATE_FLOOR = -40.0
NORM_EPS, RMS_EPS, GN_EPS = 1e-6, 1e-5, 1e-5

RAW_SLOTS, SPLIT_SLOTS = 4, 2
MIX_PIECES, MLP_PIECES, MIX2_PIECES = 44, 32, 17
LAYER_PIECES = MIX_PIECES + MLP_PIECES
FF_PAIRS = MLP_PIECES // 2
MIX_USES, MLP_USES, MIX2_USES = 36, FF_PAIRS, 13
LAYER_USES = MIX_USES + MLP_USES
ALL_PIECES = DEPTH * LAYER_PIECES + MIX2_PIECES + MLP_PIECES


class Place:

    def __init__(self, fixed, *terms):
        self.fixed, self.terms = fixed, terms

    def __add__(self, n):
        return Place(self.fixed + n, *self.terms)

    def slot(self, n):
        assert all(stride % n == 0 for _, stride in self.terms)
        return self.fixed % n

    def count(self, more=0, per=1):
        v = self.fixed // per + more
        for reg, stride in self.terms:
            v = reg * (stride // per) + v
        return v


def constants():
    f = np.float32
    half = P // 2
    inv_freq = (10000.0 ** (-np.arange(half, dtype=f) / f(half))).astype(f)
    ang = np.arange(T, dtype=f)[None, :] * np.concatenate([inv_freq, inv_freq])[:, None]
    rope = np.stack([np.cos(ang), np.sin(ang)], 1).astype(f)
    s, t = np.arange(P)[:, None], np.arange(P)[None, :]
    decay = np.zeros((P, RET_H, CAUSAL), f)
    for h in range(RET_H):
        lg = math.log1p(-(2.0 ** (-5.0 - h)))
        d0 = np.arange(T)[None, :] - s
        decay[:, h, :T] = np.where(d0 >= 0, np.exp(lg * np.maximum(d0, 0)), 0.0) * P ** -0.5
        decay[:, h, T:] = np.where(t >= s, np.exp(lg * np.maximum(t - s, 0)), 0.0) * P ** -0.5
    before = (s < t).astype(f)
    mask = np.concatenate([before, np.ones((P, P), f), before], 1)
    mask = np.stack([mask, mask], 1)
    later = (s > t).astype(f)
    turn = np.zeros((P, P), f)
    turn[np.arange(half) + half, np.arange(half)] = -1.0
    turn[np.arange(half), np.arange(half) + half] = 1.0
    square = np.stack([np.eye(P, dtype=f), np.full((P, P), 1.0 / T, f), later, np.ones((P, P), f), turn], 1)
    levels = np.zeros((P, len(LEVELS), CHUNK), f)
    for n, m in enumerate(LEVELS):
        block = np.arange(CHUNK) // m
        levels[:, n] = (s >= block * 2 * m) & (s < block * 2 * m + m)
    restart = np.ones((P, 2 * T), f)
    restart[:, ::CHUNK] = 0.0
    counts = np.zeros((P, 2, T), f)
    for g, w in enumerate(WINDOWS):
        counts[64 * (g % 2):64 * (g % 2) + 64, g // 2] = 1.0 / np.minimum(np.arange(T) + 1, w)
    return {"rope": rope, "decay": decay, "mask": mask, "square": square,
            "levels": levels, "restart": restart, "counts": counts}


def build(nc, x, w_in, p_ret, p_sb, w_out, w_up, w_down, g_mix, g_mlp, g_final, norm_mix_g_2, w_in_2, pool_w_2,
          pool_scale_2, hgrn_lb_logits_2, hgrn_norm_g_2, w_out_2, norm_mlp_g_2, w_up_2, w_down_2, final_norm_g_2,
          rope, decay, mask, square, levels, restart, counts, out):
    ctx = ExitStack()
    with ctx:
        SLAB = 206 * 1024
        slab = ctx.enter_context(nc.sbuf_tensor("slab", [P, SLAB], U8))
        base = slab_base(nc, SLAB)
        at = [0]

        def place(name, shape, dtype, offset=None):
            size = int(np.prod(shape[1:])) * mybir.dt.size(dtype)
            if offset is None:
                offset = at[0]
                at[0] += -(-size // 32) * 32
            assert offset + size <= SLAB, (name, offset + size - SLAB)
            return nc.alloc_sbuf_tensor_at(name, shape, dtype, offset=base + offset)

        PIECE = 2048
        LO_POOL, LO_DVE = slice(0, 768), slice(768, PIECE)
        raw = place("raw", [P, RAW_SLOTS, PIECE], F32)
        w_hi = place("w_hi", [P, SPLIT_SLOTS, PIECE], F32R)
        w_lo = place("w_lo", [P, SPLIT_SLOTS, PIECE], F32R)
        xs = place("xs", [P, TILES, D], F32)
        hT = place("hT", [P, KT, 2 * T], F32R)
        gain = place("gain", [P, 2, D], F32)
        htok_at = at[0]
        htok = place("htok", [P, TILES, D], F32)
        carry = place("carry", [P, 2, 2, T], F32)
        sumsq = place("sumsq", [P, 4], F32)
        wide_sums = place("wide_sums", [P, 4], F32)
        wide_scale = place("wide_scale", [P, 2], F32)
        row_sumsq = place("row_sumsq", [P, 2], F32)
        row_scale = place("row_scale", [P, 2], F32)
        meansq = place("meansq", [P, 2], F32)
        rstd = place("rstd", [P, 2], F32)
        powers = place("powers", [P, 2], F32)
        rms_eps = place("rms_eps", [P, 1], F32)
        norm_eps = place("norm_eps", [P, 2], F32)
        gn_eps = place("gn_eps", [P, 1], F32)
        sq_c = place("sq_c", [P, 5, P], F32)
        ident, mean_w, later, ones, turn = (sq_c[:, i, :] for i in range(5))
        rope_c = place("rope_c", [P, 2, T], F32)
        levels_c = place("levels_c", [P, len(LEVELS), CHUNK], F32)
        hcol = place("hcol", [P, 8, HG_H], F32)
        pool_w = place("pool_w", [P, 2, P], F32)
        mix_c_at = at[0]
        decay_c = place("decay_c", [P, RET_H, CAUSAL], F32)
        mask_c = place("mask_c", [P, 2, CAUSAL], F32)
        mix_at = at[0]
        sb_at = at[0]
        sbqk = place("sbqk", [P, SB_H // 2, 4, T], F32)
        sbT = place("sbT", [P, SB_H, 2 * T], F32R, sb_at)
        sbv = place("sbv", [P, TILES, D], F32)
        ret_at = at[0]
        retqkv = place("retqkv", [P, RET_H, 4, T], F32)
        retT = place("retT", [P, RET_H * 2, 2 * T], F32R, ret_at)
        u_at = at[0]
        gr = place("gr", [P, KT, T], F32)
        squares_at = at[0]
        gates = place("gates", [P, 2, KT, T], F32)
        zs = place("zs", [P, 2, CAUSAL], F32, htok_at)
        soft = place("soft", [P, 2, CAUSAL], F32, htok_at + 2 * CAUSAL * 4)
        logw = place("logw", [P, 2, CAUSAL], F32)
        wts = place("wts", [P, 2, CAUSAL], F32)
        rs = place("rs", [P, CAUSAL], F32)
        y_at = at[0]
        ry = place("ry", [P, 2, 2, T], F32)
        rsq = place("rsq", [P, 2, T], F32)
        rrstd = place("rrstd", [P, T], F32)
        gtmp = place("gtmp", [P, 2, T], F32)
        squares = place("squares", [P, D], F32, squares_at)
        uT = place("uT", [P, 2, 2, 2 * T], F32R, u_at)
        us = place("us", [P, 2, T], F32, y_at)
        usq = place("usq", [P, 2, T], F32, y_at + 2 * T * 4)
        wide = place("wide", [P, TILES, D], F32, squares_at)
        wide_sq = place("wide_sq", [P, TILES, D], F32, squares_at + TILES * D * 4)
        at[0] = mix_c_at
        restart_c = place("restart_c", [P, 2 * T], F32, htok_at)
        counts_c = place("counts_c", [P, 2, T], F32, htok_at + 2 * T * 4)
        at[0] = mix_at
        hz = place("hz", [P, HG_H, T], F32)
        hlog = place("hlog", [P, HG_H, T], F32)
        hfloor = place("hfloor", [P, HG_H, T], F32)
        hk = place("hk", [P, HG_H, T], F32)
        hq = place("hq", [P, HG_H, T], F32)
        hg = place("hg", [P, HG_H, T], F32)
        hb = place("hb", [P, HG_H, T], F32)
        hv = place("hv", [P, TILES, HG_H * P], F32)
        st = place("st", [P, HG_H * TILES, P], F32)
        cross = place("cross", [P, HG_H, P], F32)
        ho = place("ho", [P, HG_H, T], F32)
        htmp = place("htmp", [P, 2, T], F32)
        pads = place("pads", [P, 5, 2, PAD + T], F32)
        pmix = place("pmix", [P, 2, T], F32)
        py = place("py", [P, 2, T], F32)
        btail = place("btail", [P, HG_H, 1], F32)
        LB_LOGIT, LB_EXP, LB, ONE_LESS, HNORM, PSCALE, LB_INV, LB_P = range(8)

        ps = ctx.enter_context(nc.psum_tensor("ps", [P, 8, HALF], F32))

        def sem(name):
            return ctx.enter_context(nc.semaphore(name))

        raw_in = [sem(f"raw_in{i}") for i in range(RAW_SLOTS)]
        hi_ready = sem("hi_ready")
        lo_dve = sem("lo_dve")
        lo_pool = sem("lo_pool")
        piece_used = sem("piece_used")
        pair_act = sem("pair_act")
        pair_free = sem("pair_free")
        consts_in = sem("consts_in")
        x_in = [sem("x_in0"), sem("x_in1")]
        ident_in = sem("ident_in")
        gain_in = [sem("gain_in0"), sem("gain_in1")]
        small_set = sem("small_set")
        x_ready = sem("x_ready")
        sq_ready = sem("sq_ready")
        wide_ready, wide_sq_ready, wide_step = (sem(n) for n in ("wide_ready", "wide_sq_ready", "wide_step"))
        mean_ready = sem("mean_ready")
        rstd_ready = sem("rstd_ready")
        h_ready = sem("h_ready")
        h_hi, h_lo, row_sq, row_mean, row_ready = (sem(n) for n in ("h_hi", "h_lo", "row_sq", "row_mean", "row_ready"))
        h_turned = sem("h_turned")
        out_full = sem("out_full")
        down_full = sem("down_full")
        z_full, z_scaled, z_abs, sb_exp, softplus, log_beta, neg_log_rest, masked_rest = (
            sem(n) for n in ("z_full", "z_scaled", "z_abs", "sb_exp", "softplus", "log_beta", "neg_log_rest",
                             "masked_rest"))
        after_full, log_weight, weight_exp, weight_ready, sb_out, sb_hi, sb_lo = (
            sem(n) for n in ("after_full", "log_weight", "weight_exp", "weight_ready", "sb_out", "sb_hi", "sb_lo"))
        turned, rope_cos, rope_sin, rope_done = (sem(n) for n in ("turned", "rope_cos", "rope_sin", "rope_done"))
        ret_scores, ret_decayed, ret_out, ret_copied, ret_mean, ret_centred, ret_squared, ret_var = (
            sem(n) for n in ("ret_scores", "ret_decayed", "ret_out", "ret_copied", "ret_mean", "ret_centred",
                             "ret_squared", "ret_var"))
        ret_log, ret_rstd, ret_normed, ret_gated, ret_hi, ret_lo = (
            sem(n) for n in ("ret_log", "ret_rstd", "ret_normed", "ret_gated", "ret_hi", "ret_lo"))
        gate_clamped, gate_exp, gate_soft, gate_max, gate_sig, gate_done = (
            sem(n) for n in ("gate_clamped", "gate_exp", "gate_soft", "gate_max", "gate_sig", "gate_done"))
        branch_a, branch_b, merged, merged_hi, merged_lo = (
            sem(n) for n in ("branch_a", "branch_b", "merged", "merged_hi", "merged_lo"))
        u_sum, u_squared, u_hi, u_lo = (sem(n) for n in ("u_sum", "u_squared", "u_hi", "u_lo"))
        consts2_in, cols_in, pads_zero, pool_w_zero, pool_w_in = (
            sem(n) for n in ("consts2_in", "cols_in", "pads_zero", "pool_w_zero", "pool_w_in"))
        lb_step, pool_step, pool_full, pool_scaled, pool_hi, pool_lo = (
            sem(n) for n in ("lb_step", "pool_step", "pool_full", "pool_scaled", "pool_hi", "pool_lo"))
        f_abs, f_exp, f_soft, f_ls, f_kexp_in, f_kexp, f_k, f_ez, f_floor, f_floor_log, f_log, f_cum = (
            sem(n) for n in ("f_abs", "f_exp", "f_soft", "f_ls", "f_kexp_in", "f_kexp", "f_k", "f_ez", "f_floor",
                             "f_floor_log", "f_log", "f_cum"))
        silu_clamped, silu_exp, silu_soft, silu_max, silu_sig, silu_done, g_gated, g_scaled = (
            sem(n) for n in ("silu_clamped", "silu_exp", "silu_soft", "silu_max", "silu_sig", "silu_done", "g_gated",
                             "g_scaled"))
        e_first, e_second, e_exp, x_first, x_second, pairs_full, pairs_placed = (
            sem(n) for n in ("e_first", "e_second", "e_exp", "x_first", "x_second", "pairs_full", "pairs_placed"))
        o_full, o_copied, o_squared, o_mean, o_log, o_rstd, o_normed, o_gated, o_hi, y_lo = (
            sem(n) for n in ("o_full", "o_copied", "o_squared", "o_mean", "o_log", "o_rstd", "o_normed", "o_gated",
                             "o_hi", "y_lo"))
        out_sent = sem("out_sent")

        block = ctx.enter_context(nc.Block())

        MIXER = [(name, i) for name, n in (("ga", 4), ("sbq", 4), ("sbk", 4), ("sbv", 4), ("rq", 2), ("rk", 2),
                                           ("rv", 4), ("rg", 4), ("gb", 4), ("psb", 4), ("pret", 4), ("wout", 4))
                 for i in range(n)]
        assert len(MIXER) == MIX_PIECES

        def mixer_piece(k):
            return MIXER[k]

        def mixer_use(k):
            return sum(1 for name, i in MIXER[:k] if name not in ("sbv", "rv") or i % 2)

        def use_of(name, i, L):
            return Place(mixer_use(MIXER.index((name, i))), (L, LAYER_USES))

        BY_TILE = [(0, 0), (0, 1), (1, 0), (1, 1)]
        BY_HALF = [(0, 0), (1, 0), (0, 1), (1, 1)]

        def norm_bank(use, j):
            return 2 * ((j // 2 + use.slot(2)) % 2) + j % 2

        def stages(k):
            todo = []
            for p in range(SB_H // 2):
                if k == 14 + 3 * p:
                    todo.append(("sb_after", p))
                if k == 15 + 3 * p:
                    todo.append(("sb_out", p))
            for p in range(SB_H // 2):
                if k == 12 + 3 * p:
                    todo.append(("sb_scores", p))
            if k in (22, 23):
                todo.append(("rotate", k - 22))
            for lag, name in ((3, "ret_var"), (2, "ret_mean"), (1, "ret_out"), (0, "ret_scores")):
                for h in range(RET_H):
                    if k == 24 + 2 * h + lag:
                        todo.append((name, h))
            return todo

        def mixer2_piece(k):
            for name, n in (("f", 3), ("pool", 1), ("q", 3), ("v", 3), ("g", 3), ("wout", 4)):
                if k < n:
                    return name, k
                k -= n

        PAIRS = [("diag", 0), ("diag", 1)] + [("level", n) for n in range(len(LEVELS))] + [("cross", 0)]

        def stages2(k):
            todo = []
            if k == 5:
                todo += [("pool", 0)]
            if k == 7:
                todo += [("diag", 0), ("diag", 1)]
            if 7 <= k <= 12:
                todo += [("level", k - 7)]
            if k == 12:
                todo += [("level", 6), ("cross", 0)]
            return todo

        @block.sync
        def _(sp):
            def piece_in(piece, source, ahead=0):
                if ahead is not None:
                    sp.wait_ge(lo_dve, (piece + ahead).count(1))
                    sp.wait_ge(lo_pool, (piece + ahead).count(1))
                s = piece.slot(RAW_SLOTS)
                d = raw[:, s, :].rearrange("p (k c) -> p k c", k=source.shape[1])
                sp.dma_start(d, source).then_inc(raw_in[s], 16)

            def gain_load(n, source, read=None):
                sp.wait_ge(*(read or (h_ready, n.count(1) * 4)))
                sp.dma_start(gain[:, n.slot(2), :], source.partition_broadcast(P)).then_inc(gain_in[n.slot(2)], 16)

            def across(w, column):
                return w.rearrange("(k p) c -> p k c", p=P)[:, :, column:column + 256]

            def along(w, row, column):
                return w.rearrange("(k p) c -> p k c", p=P)[:, row:row + 4, column:column + HALF]

            def mlp_loads(piece, up, down):
                ups = up.rearrange("(k p) (i c) -> i p k c", p=P, c=256)
                downs = down.rearrange("(i k p) c -> i p k c", p=P, k=2)
                piece_in(piece, ups[0])
                piece_in(piece + 1, ups[1])
                piece_in(piece + 2, downs[0])
                with sp.Fori(0, (FF_PAIRS - 2) // 2) as i:
                    here = Place(piece.fixed + 3, *piece.terms, (i, 4))
                    for j in range(2):
                        piece_in(here + 2 * j, ups[i * 2 + (2 + j)])
                        piece_in(here + (2 * j + 1), downs[i * 2 + (1 + j)])
                piece_in(piece + 31, downs[FF_PAIRS - 1])

            xt = x.rearrange("b (n p) d -> (b n) p d", p=P)
            for t in range(TILES):
                sp.dma_start(xs[:, t, :], xt[t]).then_inc(x_in[t], 16)
            sp.dma_start(sq_c[:, 0, :], square[:, 0]).then_inc(ident_in, 16)
            COLUMN_0 = MIXER.index(("rq", 0))
            with sp.Fori(0, DEPTH) as L:
                gain_load(Place(0, (L, 2)), g_mix[L])
                for k in range(MIX_PIECES):
                    kind, i = mixer_piece(k)
                    piece = Place(k, (L, LAYER_PIECES))
                    column = {"rq": 0, "rk": 512, "rv": 1024, "rg": 2048, "sbq": 3072, "sbk": 4096, "sbv": 5120,
                              "ga": 6144, "gb": 7168}.get(kind)
                    if kind in ("sbv", "rv"):
                        source = along(w_in[L], 4 * (i % 2), column + HALF * (i // 2))
                    elif column is not None:
                        source = across(w_in[L], column + 256 * i)
                    elif kind == "wout":
                        source = along(w_out[L], 4 * (i // 2), HALF * (i % 2))
                    else:
                        source = across({"pret": p_ret, "psb": p_sb}[kind][L], 256 * i)
                    piece_in(piece, source, {COLUMN_0 - 1: 1, COLUMN_0: None}.get(k, 0))
                    if k == 1:
                        gain_load(Place(1, (L, 2)), g_mlp[L])
                    if k == 7:
                        sp.dma_start(sq_c[:, 1:5, :], square[:, 1:5]).then_inc(consts_in, 16)
                        sp.dma_start(rope_c[:, :, :], rope).then_inc(consts_in, 16)
                        sp.dma_start(decay_c[:, :, :], decay).then_inc(consts_in, 16)
                        sp.dma_start(mask_c[:, :, :], mask).then_inc(consts_in, 16)
                mlp_loads(Place(MIX_PIECES, (L, LAYER_PIECES)), w_up[L], w_down[L])

            sp.dma_start(levels_c[:, :, :], levels).then_inc(cols_in, 16)
            for row, source, n in ((LB_LOGIT, hgrn_lb_logits_2, HG_H), (HNORM, hgrn_norm_g_2, HG_H),
                                   (PSCALE, pool_scale_2, 2)):
                sp.dma_start(hcol[:, row, 0:n], source[0].rearrange("(h p) -> p h", p=P),
                             allow_slow_non_contiguous=True).then_inc(cols_in, 16)
            sp.wait_ge(pool_w_zero, 1)
            for g in range(len(WINDOWS)):
                lo = 64 * (g % 2)
                sp.dma_start(pool_w[lo:lo + 64, g // 2, lo:lo + 64], pool_w_2[0, g]).then_inc(pool_w_in, 16)
            gain_load(Place(4), g_final)
            gain_load(Place(5), norm_mix_g_2[0])
            first = DEPTH * LAYER_PIECES
            for k in range(MIX2_PIECES):
                kind, i = mixer2_piece(k)
                column = {"pool": 0, "q": 256, "f": 1024, "v": 1792, "g": 2560}.get(kind)
                source = (along(w_out_2[0], 4 * (i // 2), HALF * (i % 2)) if kind == "wout"
                          else across(w_in_2[0], column + 256 * i))
                piece_in(Place(first + k), source)
                if k == 3:
                    gain_load(Place(6), norm_mlp_g_2[0], (x_ready, 4 * 6))
                if k == 3:
                    sp.wait_ge(x_ready, 4 * 6)
                    sp.dma_start(restart_c[:, :], restart).then_inc(consts2_in, 16)
                    sp.dma_start(counts_c[:, :, :], counts).then_inc(consts2_in, 16)
            mlp_loads(Place(first + MIX2_PIECES), w_up_2[0], w_down_2[0])
            gain_load(Place(7), final_norm_g_2, (h_ready, 8 + 4 * 5))
            ot = out.rearrange("b (n p) d -> (b n) p d", p=P)
            for t in range(TILES):
                sp.wait_ge(h_ready, 8 + 4 * 6 + 2 * (t + 1))
                sp.dma_start(ot[t], htok[:, t, :]).then_inc(out_sent, 16)
            sp.wait_ge(out_sent, 16 * TILES)

        @block.tensor
        def _(pe):
            def mm(o, lhsT, rhs, start, stop):
                return pe.matmul(o, lhsT, rhs, start=start, stop=stop)

            def split_ready(piece):
                pe.wait_ge(lo_dve, piece.count(RAW_SLOTS + 1))
                pe.wait_ge(lo_pool, piece.count(RAW_SLOTS + 1))
                s = piece.slot(SPLIT_SLOTS)
                return w_hi[:, s, :], w_lo[:, s, :]

            def across(piece, use, moving, between=None):
                hi, lo = split_ready(piece)
                pe.wait_ge(pair_free, use.count(1))
                for m in range(2):
                    bank = ps[:, 2 * use.slot(2) + m, :]
                    for k in range(KT):
                        c = k * 256 + m * P
                        mm(bank, hi[:, c:c + P], moving[:, k, :], k == 0, False)
                        last = mm(bank[:, T:2 * T], lo[:, c:c + P], moving[:, k, 0:T], False, k == KT - 1)
                    if m == 0 and between:
                        between()
                last.then_inc(piece_used, 1)

            def three(o, stationary, t, hi, lo, start, stop):
                a, b = stationary[:, t * P:(t + 1) * P], stationary[:, T + t * P:T + (t + 1) * P]
                mm(o, a, hi, start, False)
                mm(o, a, lo, False, False)
                return mm(o, b, hi, False, stop)

            def norm(n, piece, use, order):
                by_tile = order is BY_TILE

                def turn_quarter(j):
                    t, c = order[j]
                    pe.wait_ge(h_ready, n.count(0) * 4 + (8 + j + 1))
                    for k in range(4):
                        last = pe.transpose(ps[:, norm_bank(use, j), k * P:(k + 1) * P],
                                            htok[:, t, c * HALF + k * P:c * HALF + (k + 1) * P], ident)
                    last.then_inc(h_turned, 1)

                def products(m, g):
                    bank = ps[:, 2 * use.slot(2) + m, :].rearrange("p (s t) -> p s t", s=2)
                    tokens = slice(g * P, (g + 1) * P) if by_tile else slice(0, T)
                    for k in range(KT) if by_tile else range(4 * g, 4 * g + 4):
                        c = k * 256 + m * P
                        both = hT[:, k, :].rearrange("p (s t) -> p s t", s=2)
                        mm(bank[:, :, tokens], hi[:, c:c + P], both[:, :, tokens], k == 0, False)
                        last = mm(bank[:, 1, tokens], lo[:, c:c + P], both[:, 0, tokens], False, k == KT - 1)
                    return last

                pe.wait_ge(pair_free, use.count(2))
                turn_quarter(0)
                turn_quarter(1)
                hi, lo = split_ready(piece)
                turn_quarter(2)
                pe.wait_ge(h_lo, n.count(0) * 4 + 2)
                products(0, 0)
                turn_quarter(3)
                products(1, 0)
                pe.wait_ge(h_lo, n.count(0) * 4 + 4)
                products(0, 1)
                products(1, 1).then_inc(piece_used, 1)

            def down(piece, i, first, last_one, slot):
                hi, lo = split_ready(piece)
                pe.wait_ge(u_lo, i.count(1))
                for t, c in BY_TILE:
                    for k in range(2):
                        w = slice(k * D + c * HALF, k * D + (c + 1) * HALF)
                        last = three(ps[:, 4 + 2 * t + c, :], uT[:, slot, k, :], t, hi[:, w], lo[:, w],
                                     first and k == 0, last_one and k == 1)
                    if last_one and (t, c) != BY_TILE[-1]:
                        last.then_inc(down_full, 1)
                last.then_inc(piece_used, 1)

            def mlp(n, stage, piece, use):
                norm(n, piece, use, BY_HALF)
                across(piece + 1, use + 1, hT)
                down(piece + 2, Place(0, *stage), True, False, 0)
                with pe.Fori(0, (FF_PAIRS - 2) // 2) as i:
                    here = Place(piece.fixed + 3, *piece.terms, (i, 4))
                    up = Place(use.fixed + 2, *use.terms, (i, 2))
                    for j in range(2):
                        across(here + 2 * j, up + j, hT)
                        down(here + (2 * j + 1), Place(1 + j, *stage, (i, 2)), False, False, (1 + j) % 2)
                down(piece + 31, Place(FF_PAIRS - 1, *stage), False, True, 1)

            def out_piece(piece, i):
                hi, lo = split_ready(piece)
                for t in range(TILES):
                    for k in range(4):
                        w = slice(k * HALF, (k + 1) * HALF)
                        last = three(ps[:, 4 + 2 * t + i % 2, :], hT[:, 4 * (i // 2) + k, :], t, hi[:, w], lo[:, w],
                                     i < 2 and k == 0, i >= 2 and k == 3)
                    if (i, t) in ((2, 0), (3, 0)):
                        last.then_inc(out_full, 1)
                last.then_inc(piece_used, 1)

            def causal(bank, lhs0, lhs1, rhs):
                mm(bank[:, 0:T], lhs0, rhs, True, True)
                return mm(bank[:, T:CAUSAL], lhs1, rhs[:, P:T], True, True)

            pe.wait_ge(ident_in, 16)
            with pe.Fori(0, DEPTH) as L:
                norm(Place(0, (L, 2)), Place(0, (L, LAYER_PIECES)), Place(0, (L, LAYER_USES)), BY_TILE)

                def stage(name, i):
                    pair, head = Place(i, (L, SB_H // 2)), Place(i, (L, RET_H))
                    if name == "sb_scores":
                        pe.wait_ge(pair_free, use_of("sbk", 3, L).count(3))
                        for j in range(2):
                            q, k = sbqk[:, i, j, :], sbqk[:, i, 2 + j, :]
                            last = causal(ps[:, 4 + j, :], k[:, 0:P], k[:, P:T], q)
                        last.then_inc(z_full, 1)
                    elif name == "sb_after":
                        pe.wait_ge(masked_rest, pair.count(1))
                        for j in range(2):
                            rest = zs[:, j, :]
                            bank = ps[:, 6 + j, :]
                            mm(bank[:, 0:T], later, rest[:, 0:T], True, False)
                            mm(bank[:, P:T], ones, rest[:, T:CAUSAL], False, True)
                            last = mm(bank[:, T:CAUSAL], later, rest[:, T:CAUSAL], True, True)
                        last.then_inc(after_full, 1)
                    elif name == "sb_out":
                        pe.wait_ge(weight_ready, pair.count(1))
                        pe.wait_ge(pair_free, use_of("sbv", 2 * (i // 2), L).count(3))
                        for j in range(2):
                            o = ps[:, 6, j * T:(j + 1) * T]
                            c = (2 * i + j) * P
                            mm(o, sbv[:, 0, c:c + P], wts[:, j, 0:T], True, False)
                            last = mm(o[:, P:T], sbv[:, 1, c:c + P], wts[:, j, T:CAUSAL], False, True)
                        last.then_inc(sb_out, 1)
                    elif name == "rotate":
                        pe.wait_ge(pair_free, use_of("rk", 1, L).count(3))
                        pe.wait_ge(z_scaled, Place(3, (L, 4)).count(1))
                        if i:
                            pe.wait_ge(rope_sin, Place(0, (L, 2)).count(1))
                        for j in range(2):
                            last = mm(ps[:, 4 + j, :], turn, retqkv[:, 2 * j:2 * j + 2, i, :], True, True)
                        last.then_inc(turned, 1)
                    elif name == "ret_scores":
                        pe.wait_ge(rope_done, Place(1, (L, 2)).count(1))
                        if i:
                            pe.wait_ge(ret_decayed, head.count(0))
                        k = retqkv[:, i, 1, :]
                        causal(ps[:, 4, :], k[:, 0:P], k[:, P:T], retqkv[:, i, 0, :]).then_inc(ret_scores, 1)
                    elif name == "ret_out":
                        pe.wait_ge(ret_decayed, head.count(1))
                        pe.wait_ge(pair_free, use_of("rv", 2 * (i // 2), L).count(3))
                        for e in range(2):
                            o = ps[:, 5, e * T:(e + 1) * T]
                            mm(o, retqkv[:, i, 2, e * P:(e + 1) * P], rs[:, 0:T], True, False)
                            last = mm(o[:, P:T], retqkv[:, i, 3, e * P:(e + 1) * P], rs[:, T:CAUSAL], False, True)
                        last.then_inc(ret_out, 1)
                    elif name == "ret_mean":
                        pe.wait_ge(ret_copied, head.count(1))
                        if i == 0:
                            pe.wait_ge(sb_lo, Place(3, (L, 4)).count(1))
                        for e in range(2):
                            last = mm(ps[:, 6, 0:T], mean_w, ry[:, i % 2, e, :], e == 0, e == 1)
                        last.then_inc(ret_mean, 1)
                    elif name == "ret_var":
                        pe.wait_ge(ret_squared, head.count(1))
                        for e in range(2):
                            last = mm(ps[:, 7, 0:T], mean_w, rsq[:, e, :], e == 0, e == 1)
                        last.then_inc(ret_var, 1)

                for k in range(MIX_PIECES):
                    kind, i = mixer_piece(k)
                    piece = Place(k, (L, LAYER_PIECES))
                    use = Place(mixer_use(k), (L, LAYER_USES))
                    if kind in ("sbv", "rv"):
                        hi, lo = split_ready(piece)
                        if i % 2 == 0:
                            pe.wait_ge(pair_free, use.count(1))
                        for t in range(TILES):
                            for kk in range(4):
                                w = slice(kk * HALF, (kk + 1) * HALF)
                                last = three(ps[:, 2 * use.slot(2) + t, :], hT[:, 4 * (i % 2) + kk, :], t, hi[:, w],
                                             lo[:, w], i % 2 == 0 and kk == 0, i % 2 == 1 and kk == 3)
                        last.then_inc(piece_used, 1)
                    elif kind == "wout":
                        pe.wait_ge(merged_lo, Place(2 * (i // 2) + 1, (L, 4)).count(1))
                        out_piece(piece, i)
                    else:
                        if kind == "pret":
                            pe.wait_ge(ret_lo, Place(RET_H - 1, (L, RET_H)).count(1))
                        if kind == "psb":
                            pe.wait_ge(sb_lo, Place(3, (L, 4)).count(1))
                        if k:
                            across(piece, use, {"pret": retT, "psb": sbT}.get(kind, hT))
                    if k == 11:
                        pe.wait_ge(consts_in, Place(4, (L, 4)).count(0) * 16)
                    for s in stages(k):
                        stage(*s)
                mlp(Place(1, (L, 2)), ((L, FF_PAIRS),), Place(MIX_PIECES, (L, LAYER_PIECES)),
                    Place(MIX_USES, (L, LAYER_USES)))

            first, use0 = DEPTH * LAYER_PIECES, DEPTH * LAYER_USES
            norm(Place(4), Place(first), Place(use0), BY_TILE)

            def pairs(n):
                kind, i = PAIRS[n]
                if n >= 2:
                    pe.wait_ge(pairs_placed, n - 1)
                o = ps[:, 4 + 2 * (n % 2):6 + 2 * (n % 2), :].rearrange("p b c -> p (b c)")
                if kind == "diag":
                    for j in range(6):
                        h, t = divmod(6 * i + j, 2)
                        c = slice(t * P, (t + 1) * P)
                        last = mm(o[:, j * P:(j + 1) * P], hk[:, h, c], hq[:, h, c], True, True)
                elif kind == "level":
                    m = LEVELS[i]
                    pe.wait_ge(x_first, i + 1)
                    pe.wait_ge(x_second, i + 1)
                    for j in range(HG_H * TILES):
                        side = (hz, hlog)[i % 2][:, j // 2, (j % 2) * P:(j % 2 + 1) * P]
                        rhs = side.rearrange("p (b two m) -> p b two m", two=2, m=m)[:, :, 1, :]
                        last = mm(o[:, j * CHUNK:(j + 1) * CHUNK].rearrange("p (b m) -> p b m", m=m), side, rhs,
                                  True, True)
                else:
                    pe.wait_ge(x_first, len(LEVELS) + 1)
                    pe.wait_ge(x_second, len(LEVELS) + 1)
                    side = (hz, hlog)[len(LEVELS) % 2]
                    for h in range(HG_H):
                        last = mm(o[:, h * P:(h + 1) * P], side[:, h, 0:P], side[:, h, P:T], True, True)
                last.then_inc(pairs_full, 1)

            for k in range(MIX2_PIECES):
                kind, i = mixer2_piece(k)
                piece, use = Place(first + k), Place(use0 + k)
                if kind == "v":
                    hi, lo = split_ready(piece)
                    pe.wait_ge(pair_free, use.count(1))
                    for t in range(TILES):
                        for kk in range(KT):
                            w = slice(kk * 256, (kk + 1) * 256)
                            last = three(ps[:, 2 * use.slot(2) + t, 0:256], hT[:, kk, :], t, hi[:, w], lo[:, w],
                                         kk == 0, kk == KT - 1)
                    last.then_inc(piece_used, 1)
                elif kind == "wout":
                    pe.wait_ge(y_lo, 2 if i < 2 else 4)
                    out_piece(piece, i)
                elif k:
                    across(piece, use, hT)
                for name, j in stages2(k):
                    if name == "pool":
                        pe.wait_ge(pool_step, 9)
                        pe.wait_ge(pool_w_in, 16 * len(WINDOWS))
                        for b in range(2):
                            last = mm(ps[:, 7, b * T:(b + 1) * T], pool_w[:, b, :], pmix[:, b, :], True, True)
                        last.then_inc(pool_full, 1)
                    elif (name, j) == ("diag", 0):
                        pe.wait_ge(f_k, 3)
                        pe.wait_ge(silu_done, 3)
                        pe.wait_ge(pool_scaled, 2)
                        pairs(0)
                    else:
                        pairs(PAIRS.index((name, j)))
                if k == 12:
                    pe.wait_ge(pairs_placed, len(PAIRS))
                    for r in range(3):
                        for j in range(2):
                            h = 2 * r + j
                            o, c = ps[:, 4 + r, j * T:(j + 1) * T], slice(h * P, (h + 1) * P)
                            mm(o[:, 0:P], hv[:, 0, c], st[:, 2 * h, :], True, True)
                            mm(o[:, P:T], hv[:, 0, c], cross[:, h, :], True, False)
                            last = mm(o[:, P:T], hv[:, 1, c], st[:, 2 * h + 1, :], False, True)
                        last.then_inc(o_full, 1)
                    for r in range(3):
                        pe.wait_ge(o_copied, r + 1)
                        pe.wait_ge(o_squared, r + 1)
                        mm(ps[:, 4 + r, :], mean_w, hfloor[:, 2 * r:2 * r + 2, :], True, True).then_inc(o_mean, 1)
            mlp(Place(5), ((1, DEPTH * FF_PAIRS),), Place(first + MIX2_PIECES), Place(use0 + MIX2_USES))

        @block.scalar
        def _(act):
            def convert(piece):
                act.wait_ge(raw_in[piece.slot(RAW_SLOTS)], piece.count(1, RAW_SLOTS) * 16)
                act.wait_ge(piece_used, piece.count(1))
                for part in (LO_POOL, LO_DVE):
                    act.activation(w_hi[:, piece.slot(SPLIT_SLOTS), part], raw[:, piece.slot(RAW_SLOTS), part],
                                   ACT.Copy).then_inc(hi_ready, 1)

            def carry_cross(piece, use):
                act.wait_ge(piece_used, piece.count(SPLIT_SLOTS + 1))
                b = 2 * use.slot(2)
                act.activation(carry[:, use.slot(2), :, :], ps[:, b:b + 2, T:2 * T], ACT.Copy).then_inc(pair_act, 1)

            def square_sums(n):
                for j, (t, c) in enumerate(BY_TILE):
                    act.wait_ge(x_ready, n.count(0) * 4 + (j + 1))
                    half = slice(c * HALF, (c + 1) * HALF)
                    act.activation(htok[:, t, half], xs[:, t, half], ACT.Square, scale=D ** -0.5,
                                   accum_out=sumsq[:, 2 * t + c:2 * t + c + 1]).then_inc(sq_ready, 1)

            def turned_hi(h, use, order):
                for j, (t, c) in enumerate(order):
                    act.wait_ge(h_turned, h.count(0) * 4 + (j + 1))
                    act.activation(hT[:, 4 * c:4 * c + 4, t * P:(t + 1) * P],
                                   ps[:, norm_bank(use, j), :].rearrange("p (k c) -> p k c", c=P),
                                   ACT.Copy).then_inc(h_hi, 1)

            def norm(n, h, piece, use):
                square_sums(n)
                convert(piece)
                turned_hi(h, use, BY_TILE)
                convert(piece + 1)

            def mlp(n, h, stage, piece, use):
                convert(piece)
                turned_hi(h, use, BY_HALF)
                convert(piece + 1)
                for t in range(TILES):
                    act.wait_ge(x_ready, n.count(1) * 4)
                    act.activation(squares[:, :], xs[:, t, :], ACT.Square, scale=D ** -0.5,
                                   accum_out=row_sumsq[:, t:t + 1]).then_inc(row_sq, 1)
                    if t == 0:
                        act.wait_ge(row_sq, stage.count(0) * 2 + 1)

                def up(piece, use):
                    carry_cross(piece, use)
                    convert(piece + 2)

                up(piece, use)
                up(piece + 1, use + 1)
                convert(piece + 4)
                steps = (FF_PAIRS - 2) // 2 - 1
                with act.Fori(0, steps) as i:
                    here, u = Place(piece.fixed + 3, *piece.terms, (i, 4)), Place(use.fixed + 2, *use.terms, (i, 2))
                    for j in range(2):
                        up(here + 2 * j, u + j)
                        convert(here + (2 * j + 3))
                here, u = piece + (3 + 4 * steps), use + (2 + 2 * steps)
                up(here, u)
                convert(here + 3)
                up(here + 2, u + 1)

            act.preload_act_table_set("natural_log_exp_and_others")
            act.wait_ge(small_set, 6)
            with act.Fori(0, DEPTH) as L:
                norm(Place(0, (L, 2)), Place(0, (L, 2)), Place(0, (L, LAYER_PIECES)), Place(0, (L, LAYER_USES)))

                def stage(name, i):
                    pair, head = Place(i, (L, SB_H // 2)), Place(i, (L, RET_H))
                    if name == "sb_scores":
                        act.wait_ge(z_full, pair.count(1))
                        act.activation(zs[:, :, :], ps[:, 4:6, 0:CAUSAL], ACT.Copy, scale=SB_SCALE).then_inc(z_scaled, 1)
                        act.wait_ge(z_abs, pair.count(1))
                        act.activation(soft[:, :, :], soft[:, :, :], ACT.Exp).then_inc(sb_exp, 1)
                        act.wait_ge(sb_exp, pair.count(1))
                        act.activation(soft[:, :, :], soft[:, :, :], ACT.Ln, bias=1.0).then_inc(softplus, 1)
                    elif name == "sb_after":
                        act.wait_ge(log_weight, pair.count(1))
                        act.activation(wts[:, :, :], logw[:, :, :], ACT.Exp).then_inc(weight_exp, 1)
                    elif name == "sb_out":
                        act.wait_ge(sb_out, pair.count(1))
                        act.activation(sbT[:, 2 * i:2 * i + 2, 0:T],
                                       ps[:, 6, :].rearrange("p (j t) -> p j t", j=2), ACT.Copy).then_inc(sb_hi, 1)
                    elif name == "ret_out":
                        act.wait_ge(ret_out, head.count(1))
                        act.activation(ry[:, i % 2, :, :], ps[:, 5, :].rearrange("p (e t) -> p e t", e=2),
                                       ACT.Copy).then_inc(ret_copied, 1)
                    elif name == "ret_mean":
                        act.wait_ge(ret_centred, head.count(1))
                        act.activation(rsq[:, :, :], ry[:, i % 2, :, :], ACT.Square).then_inc(ret_squared, 1)
                    elif name == "ret_var":
                        act.wait_ge(ret_var, head.count(1))
                        act.activation(rrstd[:, :], ps[:, 7, 0:T], ACT.Ln, bias=gn_eps[:, 0:1]).then_inc(ret_log, 1)
                        act.wait_ge(ret_log, head.count(1))
                        act.activation(rrstd[:, :], rrstd[:, :], ACT.Exp, scale=-0.5).then_inc(ret_rstd, 1)

                for k in range(MIX_PIECES):
                    kind, i = mixer_piece(k)
                    piece = Place(k, (L, LAYER_PIECES))
                    use = Place(mixer_use(k), (L, LAYER_USES))
                    if kind in ("sbv", "rv"):
                        if i % 2 == 1:
                            act.wait_ge(piece_used, piece.count(SPLIT_SLOTS + 1))
                            b = ps[:, 2 * use.slot(2), :]
                            if kind == "sbv":
                                act.activation(sbv[:, 0, HALF * (i // 2):HALF * (i // 2 + 1)], b,
                                               ACT.Copy).then_inc(pair_act, 1)
                            else:
                                act.activation(retqkv[:, 2 * (i // 2):2 * (i // 2) + 2, 2, :],
                                               b.rearrange("p (h c) -> p h c", h=2), ACT.Copy).then_inc(pair_act, 1)
                    elif kind != "wout":
                        carry_cross(piece, use)
                    if k + 2 < MIX_PIECES:
                        convert(piece + 2)
                    gate = Place({"ga": 0, "rg": 4, "gb": 8}.get(kind, 0) + i, (L, 12))
                    if kind in ("rg", "ga", "gb"):
                        act.wait_ge(gate_clamped, gate.count(1))
                        act.activation(gtmp[:, :, :], gtmp[:, :, :], ACT.Exp, scale=-1.0).then_inc(gate_exp, 1)
                        act.wait_ge(gate_exp, gate.count(1))
                        act.activation(gtmp[:, :, :], gtmp[:, :, :], ACT.Ln, bias=1.0).then_inc(gate_soft, 1)
                        act.wait_ge(gate_max, gate.count(1))
                        o = gtmp[:, :, :] if kind == "rg" else gates[:, kind == "gb", 2 * i:2 * i + 2, :]
                        act.activation(o, gtmp[:, :, :], ACT.Exp, scale=-1.0).then_inc(gate_sig, 1)
                    for s in stages(k):
                        stage(*s)
                mlp(Place(1, (L, 2)), Place(1, (L, 2)), Place(0, (L, 1)), Place(MIX_PIECES, (L, LAYER_PIECES)),
                    Place(MIX_USES, (L, LAYER_USES)))

            first, use0 = DEPTH * LAYER_PIECES, DEPTH * LAYER_USES
            for j, (t, c) in enumerate(BY_TILE):
                q = slice(c * HALF, (c + 1) * HALF)
                act.wait_ge(x_ready, 4 * 4 + (j + 1))
                act.activation(htok[:, t, q], xs[:, t, q], ACT.Square, scale=D ** -0.5,
                               accum_out=sumsq[:, j:j + 1]).then_inc(sq_ready, 1)
                act.wait_ge(wide_ready, j + 1)
                act.activation(wide_sq[:, t, q], wide[:, t, q], ACT.Square, scale=D ** -0.5,
                               accum_out=wide_sums[:, j:j + 1]).then_inc(wide_sq_ready, 1)
            convert(Place(first))
            turned_hi(Place(4), Place(use0), BY_TILE)
            convert(Place(first + 1))
            for t in range(TILES):
                act.wait_ge(rstd_ready, 2 * 2 + (t + 1))
                act.activation(xs[:, t, :], wide[:, t, :], ACT.Copy, scale=rstd[:, t:t + 1]).then_inc(x_ready, 2)
            act.wait_ge(lb_step, 1)
            act.activation(hcol[:, LB_EXP, :], hcol[:, LB_EXP, :], ACT.Exp).then_inc(lb_step, 1)

            def exponents(n):
                side = (hz, hlog)[n % 2]
                act.wait_ge(e_first, n + 1)
                act.wait_ge(e_second, n + 1)
                if n == 0:
                    v = side[:, :, :].rearrange("p h (b two m) -> p (h b) two m", two=2, m=CHUNK)
                    b = hb[:, :, :].rearrange("p h (b two m) -> p (h b) two m", two=2, m=CHUNK)
                    act.activation(v[:, :, 1, :], b[:, :, 1, :], ACT.Exp)
                    act.activation(v[:, :, 0, :], v[:, :, 0, :], ACT.Exp).then_inc(e_exp, 1)
                elif n == len(LEVELS):
                    act.activation(side[:, :, 0:P], side[:, :, 0:P], ACT.Exp)
                    act.activation(side[:, :, P:P + CHUNK], hb[:, :, P:P + CHUNK], ACT.Exp)
                    act.activation(side[:, :, P + CHUNK:T], side[:, :, P + CHUNK:T], ACT.Exp).then_inc(e_exp, 1)
                else:
                    act.activation(side[:, :, :], side[:, :, :], ACT.Exp).then_inc(e_exp, 1)

            for k in range(MIX2_PIECES):
                kind, i = mixer2_piece(k)
                piece, use = Place(first + k), Place(use0 + k)
                if kind == "v":
                    act.wait_ge(piece_used, piece.count(SPLIT_SLOTS + 1))
                    act.activation(hv[:, 0, 256 * i:256 * (i + 1)], ps[:, 2 * use.slot(2), 0:256],
                                   ACT.Copy).then_inc(pair_act, 1)
                elif kind != "wout":
                    carry_cross(piece, use)
                n = i + (3 if kind == "g" else 0)
                if k + 2 < MIX2_PIECES:
                    convert(piece + 2)
                if kind in ("q", "g"):
                    act.wait_ge(silu_clamped, n + 1)
                    act.activation(htmp[:, :, :], htmp[:, :, :], ACT.Exp, scale=-1.0).then_inc(silu_exp, 1)
                    act.wait_ge(silu_exp, n + 1)
                    act.activation(htmp[:, :, :], htmp[:, :, :], ACT.Ln, bias=1.0).then_inc(silu_soft, 1)
                h2 = slice(2 * i, 2 * i + 2)
                if kind == "f":
                    act.wait_ge(pair_free, use.count(3))
                    act.activation(hfloor[:, h2, :], hz[:, h2, :], ACT.Exp, scale=-1.0).then_inc(f_ez, 1)
                    act.activation(hlog[:, h2, :], hz[:, h2, :], ACT.Abs).then_inc(f_abs, 1)
                    act.wait_ge(f_abs, i + 1)
                    act.activation(hlog[:, h2, :], hlog[:, h2, :], ACT.Exp, scale=-1.0).then_inc(f_exp, 1)
                    act.wait_ge(f_exp, i + 1)
                    act.activation(hlog[:, h2, :], hlog[:, h2, :], ACT.Ln, bias=1.0).then_inc(f_soft, 1)
                    act.wait_ge(f_floor, i + 1)
                    act.activation(hfloor[:, h2, :], hfloor[:, h2, :], ACT.Ln, bias=1.0).then_inc(f_floor_log, 1)
                    act.wait_ge(f_kexp_in, i + 1)
                    act.activation(hk[:, h2, :], hk[:, h2, :], ACT.Exp).then_inc(f_kexp, 1)
                if kind in ("q", "g"):
                    act.wait_ge(silu_max, n + 1)
                    act.activation(htmp[:, :, :], htmp[:, :, :], ACT.Exp, scale=-1.0).then_inc(silu_sig, 1)
                if k == 5:
                    act.wait_ge(pool_full, 1)
                    act.wait_ge(cols_in, 64)
                    for b in range(2):
                        act.activation(py[:, b, :], ps[:, 7, b * T:(b + 1) * T], ACT.Copy,
                                       scale=hcol[:, PSCALE, b:b + 1]).then_inc(pool_scaled, 1)
                if 6 <= k <= 12:
                    exponents(k - 6)
                if k == 12:
                    exponents(7)
                    act.wait_ge(pool_scaled, 2)
                    act.activation(hT[:, 0:2, 0:T], py[:, :, :], ACT.Copy).then_inc(pool_hi, 1)
                    act.wait_ge(pairs_full, len(PAIRS))
                    b = 4 + 2 * ((len(PAIRS) - 1) % 2)
                    act.activation(cross[:, :, :], ps[:, b:b + 2, :].rearrange("p b (h c) -> p (b h) c", c=P)[:, 0:HG_H, :],
                                   ACT.Copy).then_inc(pairs_placed, 1)
                    for r in range(3):
                        act.wait_ge(o_full, r + 1)
                        o = ps[:, 4 + r, :].rearrange("p (h t) -> p h t", h=2)
                        act.activation(hfloor[:, 2 * r:2 * r + 2, :], o, ACT.Square).then_inc(o_squared, 1)
                    for r in range(3):
                        act.wait_ge(o_mean, r + 1)
                        v = hk[:, 2 * r:2 * r + 2, :]
                        act.activation(v, ps[:, 4 + r, :].rearrange("p (h t) -> p h t", h=2), ACT.Ln, scale=T / P,
                                       bias=rms_eps[:, 0:1]).then_inc(o_log, 1)
                        act.wait_ge(o_log, r + 1)
                        act.activation(v, v, ACT.Exp, scale=-0.5).then_inc(o_rstd, 1)
                    for r in range(3):
                        act.wait_ge(o_gated, r + 1)
                        act.activation(hT[:, 2 + 2 * r:4 + 2 * r, 0:T], ho[:, 2 * r:2 * r + 2, :],
                                       ACT.Copy).then_inc(o_hi, 1)
            mlp(Place(6), Place(5), Place(2), Place(first + MIX2_PIECES), Place(use0 + MIX2_USES))
            square_sums(Place(7))

        @block.gpsimd
        def _(pool):
            def convert(piece):
                pool.wait_ge(hi_ready, piece.count(0) * 2 + 1)
                s, r = piece.slot(SPLIT_SLOTS), piece.slot(RAW_SLOTS)
                pool.tensor_tensor(w_lo[:, s, LO_POOL], raw[:, r, LO_POOL], w_hi[:, s, LO_POOL].bitcast(F32),
                                   ALU.subtract).then_inc(lo_pool, 1)

            def scales(m, eps):
                for t in range(TILES):
                    c = slice(t, t + 1)
                    pool.wait_ge(sq_ready, m.count(0) * 4 + 2 * (t + 1))
                    pool.tensor_tensor(meansq[:, c], sumsq[:, 2 * t:2 * t + 1], sumsq[:, 2 * t + 1:2 * t + 2],
                                       ALU.add).then_inc(mean_ready, 1)
                    pool.wait_ge(mean_ready, m.count(0) * 4 + (2 * t + 1))
                    pool.tensor_tensor(meansq[:, c], meansq[:, c], eps, ALU.add).then_inc(mean_ready, 1)
                    pool.wait_ge(mean_ready, m.count(0) * 4 + (2 * t + 2))
                    pool.tensor_tensor(rstd[:, c], meansq[:, c], powers[:, 0:1], ALU.pow).then_inc(rstd_ready, 1)

            def norm(m, eps, piece):
                scales(m, eps)
                convert(piece)
                convert(piece + 1)

            def mlp(stage, eps, piece):
                convert(piece)
                convert(piece + 1)
                for t in range(TILES):
                    c = slice(t, t + 1)
                    pool.wait_ge(row_sq, stage.count(0) * 2 + (t + 1))
                    pool.tensor_tensor(row_sumsq[:, c], row_sumsq[:, c], eps, ALU.add).then_inc(row_mean, 1)
                    pool.wait_ge(row_mean, stage.count(0) * 2 + (t + 1))
                    pool.tensor_tensor(row_scale[:, c], row_sumsq[:, c], powers[:, 1:2], ALU.pow).then_inc(row_ready, 1)
                convert(piece + 2)
                steps = (MLP_PIECES - 4) // 4
                with pool.Fori(0, steps) as i:
                    here = Place(piece.fixed + 3, *piece.terms, (i, 4))
                    for j in range(4):
                        convert(here + j)
                for j in range(3 + 4 * steps, MLP_PIECES):
                    convert(piece + j)

            pool.memset(pool_w[:, :, :], 0.0).then_inc(pool_w_zero, 1)
            pool.memset(powers[:, 0:1], -0.5).then_inc(small_set, 1)
            pool.memset(powers[:, 1:2], -1.0).then_inc(small_set, 1)
            pool.memset(rms_eps[:, :], RMS_EPS).then_inc(small_set, 1)
            pool.memset(gn_eps[:, :], GN_EPS).then_inc(small_set, 1)
            pool.memset(norm_eps[:, 0:1], NORM_EPS).then_inc(small_set, 1)
            pool.memset(norm_eps[:, 1:2], RMS_EPS).then_inc(small_set, 1)
            pool.wait_ge(small_set, 6)
            pool.sem_inc(lo_dve, RAW_SLOTS)
            pool.sem_inc(lo_pool, RAW_SLOTS)
            pool.sem_inc(piece_used, SPLIT_SLOTS)
            pool.sem_inc(pair_free, 2)
            pool.sem_inc(h_ready, 8)
            for t in range(TILES):
                pool.wait_ge(x_in[t], 16)
                pool.sem_inc(x_ready, 2)
            with pool.Fori(0, DEPTH) as L:
                norm(Place(0, (L, 1)), norm_eps[:, 0:1], Place(0, (L, LAYER_PIECES)))
                for k in range(MIX_PIECES):
                    if k + 2 < MIX_PIECES:
                        convert(Place(k + 2, (L, LAYER_PIECES)))
                    kind, i = mixer_piece(k)
                    if kind == "rg":
                        pool.wait_ge(gate_sig, Place(4 + i, (L, 12)).count(1))
                        g = gr[:, 2 * i:2 * i + 2, :]
                        pool.tensor_tensor(g, g, gtmp[:, :, :], ALU.mult).then_inc(gate_done, 1)
                    for name, i in stages(k):
                        pair = Place(i, (L, SB_H // 2))
                        if name == "sb_scores":
                            pool.wait_ge(neg_log_rest, pair.count(1))
                            pool.tensor_tensor(zs[:, :, :], zs[:, :, :], mask_c[:, :, :], ALU.mult).then_inc(masked_rest, 1)
                        elif name == "sb_after":
                            pool.wait_ge(weight_exp, pair.count(1))
                            pool.tensor_tensor(wts[:, :, :], wts[:, :, :], mask_c[:, :, :], ALU.mult).then_inc(weight_ready, 1)
                        elif name == "rotate":
                            pool.wait_ge(turned, Place(i, (L, 2)).count(1))
                            v = retqkv[:, :, i, :]
                            pool.tensor_tensor(v, v, rope_c[:, 0:1, :].to_broadcast([P, RET_H, T]),
                                               ALU.mult).then_inc(rope_cos, 1)
                mlp(Place(0, (L, 1)), norm_eps[:, 0:1], Place(MIX_PIECES, (L, LAYER_PIECES)))

            first = DEPTH * LAYER_PIECES
            scales(Place(2), norm_eps[:, 0:1])
            for t in range(TILES):
                c, r1, both = slice(t, t + 1), rstd[:, t:t + 1], wide_scale[:, t:t + 1]
                pool.wait_ge(wide_sq_ready, 2 * (t + 1))
                steps = ((wide_sums[:, 2 * t:2 * t + 1], wide_sums[:, 2 * t + 1:2 * t + 2], ALU.add), (both, r1, ALU.mult),
                         (both, r1, ALU.mult), (both, norm_eps[:, 1:2], ALU.add), (both, powers[:, 0:1], ALU.pow),
                         (both, r1, ALU.mult))
                for j, (a, b, op) in enumerate(steps):
                    if j == 1:
                        pool.wait_ge(rstd_ready, 2 * 2 + (t + 1))
                    if j:
                        pool.wait_ge(wide_step, len(steps) * t + j)
                    pool.tensor_tensor(both, a, b, op).then_inc(wide_step, 1)
            convert(Place(first))
            convert(Place(first + 1))
            pool.memset(pads[:, :, :, 0:PAD], 0.0).then_inc(pads_zero, 1)
            lbs = [hcol[:, r, :] for r in (LB_LOGIT, LB_EXP, LB, ONE_LESS)]
            pool.wait_ge(cols_in, 64)
            pool.tensor_tensor(lbs[1], lbs[0], lbs[0], ALU.subtract).then_inc(lb_step, 1)
            pool.wait_ge(lb_step, 3)
            pool.tensor_tensor(hcol[:, LB_P, :], lbs[1], hcol[:, LB_INV, :], ALU.mult).then_inc(lb_step, 1)
            pool.wait_ge(lb_step, 4)
            pool.tensor_tensor(lbs[2], hcol[:, LB_P, :], hcol[:, LB_P, :], ALU.subtract).then_inc(lb_step, 1)
            pool.wait_ge(lb_step, 5)
            pool.tensor_scalar(lbs[3], lbs[2], -1.0, 1.0, ALU.mult, ALU.add).then_inc(lb_step, 1)
            pool.wait_ge(lb_step, 6)

            def first_gaps(n):
                if n >= 2:
                    pool.wait_ge(pairs_full, n + 1)
                else:
                    pool.wait_ge(f_cum, 3)
                    pool.wait_ge(f_k, 3)
                m = LEVELS[n]
                v = (hz, hlog)[n % 2][:, :, :].rearrange("p h (b two m) -> p (h b) two m", two=2, m=m)
                b = hb[:, :, :].rearrange("p h (b two m) -> p (h b) two m", two=2, m=m)
                end = b[:, :, 0, m - 1:m].to_broadcast([P, HG_H * T // (2 * m), m])
                pool.tensor_tensor(v[:, :, 0, :], end, b[:, :, 0, :], ALU.subtract).then_inc(e_first, 1)

            def first_side(n):
                m = LEVELS[n] if n < len(LEVELS) else P
                pool.wait_ge(e_exp, n + 1)
                v = (hz, hlog)[n % 2][:, :, :].rearrange("p h (b two m) -> p (h b) two m", two=2, m=m)[:, :, 0, :]
                kk = hk[:, :, :].rearrange("p h (b two m) -> p (h b) two m", two=2, m=m)[:, :, 0, :]
                pool.tensor_tensor(v, v, kk, ALU.mult).then_inc(x_first, 1)

            for k in range(MIX2_PIECES):
                if k + 2 < MIX2_PIECES:
                    convert(Place(first + k + 2))
                kind, i = mixer2_piece(k)
                if kind == "f":
                    pool.wait_ge(f_kexp, i + 1)
                    v = hk[:, 2 * i:2 * i + 2, :]
                    pool.tensor_tensor(v, v, lbs[3][:, 2 * i:2 * i + 2].unsqueeze(2).to_broadcast([P, 2, T]),
                                       ALU.mult).then_inc(f_k, 1)
                if kind == "pool":
                    use = Place(DEPTH * LAYER_USES + k)
                    pool.wait_ge(pair_free, use.count(3))
                    pool.wait_ge(pads_zero, 1)
                    pool.wait_ge(consts2_in, 32)
                    for j, w in enumerate((1, 2, 4, 8)):
                        b = slice(0 if j < 2 else 1, 2)
                        pool.tensor_tensor(pads[:, j + 1, b, PAD:], pads[:, j, b, PAD:], pads[:, j, b, PAD - w:PAD + T - w],
                                           ALU.add).then_inc(pool_step, 1)
                        pool.wait_ge(pool_step, j + 1)
                    for g in range(len(WINDOWS)):
                        rows = slice(64 * (g % 2), 64 * (g % 2) + 64)
                        pool.tensor_tensor(pmix[rows, g // 2, :], pads[rows, g + 1, g // 2, PAD:],
                                           counts_c[rows, g // 2, :], ALU.mult).then_inc(pool_step, 1)
                    pool.wait_ge(pool_step, 8)
                    pool.tensor_tensor(pmix[:, :, :], pmix[:, :, :], pads[:, 0, :, PAD:],
                                       ALU.subtract).then_inc(pool_step, 1)
                if k == 5:
                    first_gaps(0)
                if 6 <= k <= 11:
                    first_side(k - 6)
                    first_gaps(k - 5)
                if k == 12:
                    first_side(6)
                    n = len(LEVELS)
                    pool.wait_ge(pairs_full, n + 1)
                    side = (hz, hlog)[n % 2]
                    pool.tensor_tensor(side[:, :, CHUNK:P], hb[:, :, P - 1:P].to_broadcast([P, HG_H, CHUNK]),
                                       hb[:, :, CHUNK:P], ALU.subtract).then_inc(e_first, 1)
                    first_side(7)
                if kind == "g":
                    pool.wait_ge(silu_sig, 4 + i)
                    v = hg[:, 2 * i:2 * i + 2, :]
                    pool.tensor_tensor(v, v, htmp[:, :, :], ALU.mult).then_inc(g_gated, 1)
                    pool.wait_ge(g_gated, i + 1)
                    pool.tensor_tensor(v, v, hcol[:, HNORM, 2 * i:2 * i + 2].unsqueeze(2).to_broadcast([P, 2, T]),
                                       ALU.mult).then_inc(g_scaled, 1)
            mlp(Place(2), norm_eps[:, 1:2], Place(first + MIX2_PIECES))
            scales(Place(3), norm_eps[:, 1:2])

        @block.vector
        def _(dve):
            def convert(piece):
                dve.wait_ge(hi_ready, piece.count(1) * 2)
                s, r = piece.slot(SPLIT_SLOTS), piece.slot(RAW_SLOTS)
                dve.tensor_tensor(w_lo[:, s, LO_DVE], raw[:, r, LO_DVE], w_hi[:, s, LO_DVE].bitcast(F32),
                                  ALU.subtract).then_inc(lo_dve, 1)

            def split_lo(o, hi, value):
                return dve.tensor_tensor(o, value, hi.bitcast(F32), ALU.subtract)

            def add_cross(use, o):
                dve.wait_ge(pair_act, use.count(1))
                b = 2 * use.slot(2)
                dve.tensor_tensor(o, ps[:, b:b + 2, 0:T], carry[:, use.slot(2), :, :], ALU.add).then_inc(pair_free, 1)

            def quarter(t, c):
                return slice(c * HALF, (c + 1) * HALF)

            def norm_rows(n, m):
                for t, c in BY_TILE:
                    q = quarter(t, c)
                    if c == 0:
                        dve.wait_ge(rstd_ready, m.count(0) * 2 + (t + 1))
                        dve.wait_ge(gain_in[n.slot(2)], n.count(1, 2) * 16)
                    dve.scalar_tensor_tensor(out=htok[:, t, q], in0=xs[:, t, q], scalar=rstd[:, t:t + 1],
                                             in1=gain[:, n.slot(2), q], op0=ALU.mult, op1=ALU.mult).then_inc(h_ready, 1)

            def turned_lo(h, use, j, t, c):
                dve.wait_ge(h_hi, h.count(0) * 4 + (j + 1))
                split_lo(hT[:, 4 * c:4 * c + 4, T + t * P:T + (t + 1) * P], hT[:, 4 * c:4 * c + 4, t * P:(t + 1) * P],
                         ps[:, norm_bank(use, j), :].rearrange("p (k c) -> p k c", c=P)).then_inc(h_lo, 1)

            def split_rows(h, piece, use):
                convert(piece)
                for j, (t, c) in enumerate(BY_TILE):
                    turned_lo(h, use, j, t, c)
                convert(piece + 1)

            def out_sums(h, j, piece):
                if j % 2 == 0:
                    dve.wait_ge(out_full, h.count(0, 2) * 2 + (j // 2 + 1))
                else:
                    dve.wait_ge(piece_used, (piece + (j // 2 - 1)).count(SPLIT_SLOTS + 1))

            def down_sums(h, j, piece):
                if j < 3:
                    dve.wait_ge(down_full, h.count(0, 2) * 3 + (j + 1))
                else:
                    dve.wait_ge(piece_used, piece.count(SPLIT_SLOTS + 1))

            def mlp(n, h, stage, piece, use):
                for j, (t, c) in enumerate(BY_HALF):
                    q = quarter(t, c)
                    out_sums(h, j, piece + -1)
                    dve.tensor_tensor(xs[:, t, q], ps[:, 4 + 2 * t + c, :], xs[:, t, q], ALU.add).then_inc(x_ready, 1)
                    dve.wait_ge(x_ready, n.count(0) * 4 + (j + 1))
                    dve.wait_ge(gain_in[n.slot(2)], n.count(1, 2) * 16)
                    dve.tensor_tensor(htok[:, t, q], xs[:, t, q], gain[:, n.slot(2), q], ALU.mult).then_inc(h_ready, 1)
                    if j == 1:
                        convert(piece)
                    if j >= 1:
                        turned_lo(h, use, j - 1, *BY_HALF[j - 1])
                turned_lo(h, use, 3, *BY_HALF[3])
                convert(piece + 1)

                def up(piece, use, i, slot, before=True):
                    if before:
                        dve.wait_ge(u_lo, i.count(0))
                    dve.wait_ge(pair_act, use.count(1))
                    b = 2 * use.slot(2)
                    dve.tensor_tensor(us[:, :, :], ps[:, b:b + 2, 0:T], carry[:, use.slot(2), :, :],
                                      ALU.add).then_inc(pair_free, 1)
                    dve.wait_ge(pair_free, use.count(3))
                    dve.scalar_tensor_tensor(out=usq[:, :, :], in0=us[:, :, :], scalar=0.0, in1=us[:, :, :],
                                             op0=ALU.max, op1=ALU.mult).then_inc(u_squared, 1)
                    convert(piece + 2)
                    dve.wait_ge(u_squared, i.count(1))
                    dve.tensor_copy(uT[:, slot, :, 0:T], usq[:, :, :]).then_inc(u_hi, 1)
                    dve.wait_ge(u_hi, i.count(1))
                    split_lo(uT[:, slot, :, T:2 * T], uT[:, slot, :, 0:T], usq[:, :, :]).then_inc(u_lo, 1)

                count = lambda i, *more: Place(i, *((reg, stride * FF_PAIRS) for reg, stride in stage.terms), *more) \
                    + stage.fixed * FF_PAIRS
                up(piece, use, count(0), 0, before=False)
                up(piece + 1, use + 1, count(1), 1)
                convert(piece + 4)
                steps = (FF_PAIRS - 2) // 2 - 1
                with dve.Fori(0, steps) as i:
                    here, u = Place(piece.fixed + 3, *piece.terms, (i, 4)), Place(use.fixed + 2, *use.terms, (i, 2))
                    for j in range(2):
                        up(here + 2 * j, u + j, count(2 + j, (i, 2)), j)
                        convert(here + (2 * j + 3))
                here, u = piece + (3 + 4 * steps), use + (2 + 2 * steps)
                up(here, u, count(2 + 2 * steps), 0)
                convert(here + 3)
                up(here + 2, u + 1, count(3 + 2 * steps), 1)
                dve.wait_ge(row_ready, stage.count(1) * 2)
                for j, (t, c) in enumerate(BY_TILE):
                    q = quarter(t, c)
                    down_sums(h, j, piece + 31)
                    dve.scalar_tensor_tensor(out=xs[:, t, q], in0=ps[:, 4 + 2 * t + c, :], scalar=row_scale[:, t:t + 1],
                                             in1=xs[:, t, q], op0=ALU.mult, op1=ALU.add).then_inc(x_ready, 1)

            with dve.Fori(0, DEPTH) as L:
                norm_rows(Place(0, (L, 2)), Place(0, (L, 1)))
                split_rows(Place(0, (L, 2)), Place(0, (L, LAYER_PIECES)), Place(0, (L, LAYER_USES)))

                def stage(name, i):
                    pair, head = Place(i, (L, SB_H // 2)), Place(i, (L, RET_H))
                    if name == "sb_scores":
                        dve.wait_ge(z_scaled, pair.count(1))
                        dve.scalar_tensor_tensor(out=soft[:, :, :], in0=zs[:, :, :], scalar=-1.0, in1=zs[:, :, :],
                                                 op0=ALU.mult, op1=ALU.min).then_inc(z_abs, 1)
                        dve.wait_ge(softplus, pair.count(1))
                        dve.scalar_tensor_tensor(out=logw[:, :, :], in0=zs[:, :, :], scalar=0.0, in1=soft[:, :, :],
                                                 op0=ALU.min, op1=ALU.subtract).then_inc(log_beta, 1)
                        dve.wait_ge(log_beta, pair.count(1))
                        dve.scalar_tensor_tensor(out=zs[:, :, :], in0=zs[:, :, :], scalar=0.0, in1=soft[:, :, :],
                                                 op0=ALU.max, op1=ALU.add).then_inc(neg_log_rest, 1)
                    elif name == "sb_after":
                        dve.wait_ge(after_full, pair.count(1))
                        dve.tensor_tensor(logw[:, :, :], logw[:, :, :], ps[:, 6:8, 0:CAUSAL],
                                          ALU.subtract).then_inc(log_weight, 1)
                    elif name == "sb_out":
                        dve.wait_ge(sb_hi, pair.count(1))
                        split_lo(sbT[:, 2 * i:2 * i + 2, T:2 * T], sbT[:, 2 * i:2 * i + 2, 0:T],
                                 ps[:, 6, :].rearrange("p (j t) -> p j t", j=2)).then_inc(sb_lo, 1)
                    elif name == "rotate":
                        part = Place(i, (L, 2))
                        dve.wait_ge(turned, part.count(1))
                        if i:
                            dve.wait_ge(rope_done, part.count(0))
                        v, tmp = retqkv[:, :, i, :], ry[:, :, :, :].rearrange("p a e t -> p (a e) t")
                        dve.tensor_tensor(tmp, ps[:, 4:6, :].rearrange("p b (h t) -> p (b h) t", h=2),
                                          rope_c[:, 1:2, :].to_broadcast([P, RET_H, T]), ALU.mult).then_inc(rope_sin, 1)
                        dve.wait_ge(rope_cos, part.count(1))
                        dve.wait_ge(rope_sin, part.count(1))
                        dve.tensor_tensor(v, v, tmp, ALU.add).then_inc(rope_done, 1)
                    elif name == "ret_scores":
                        dve.wait_ge(ret_scores, head.count(1))
                        dve.tensor_tensor(rs[:, :], ps[:, 4, 0:CAUSAL], decay_c[:, i, :], ALU.mult).then_inc(ret_decayed, 1)
                    elif name == "ret_mean":
                        dve.wait_ge(ret_mean, head.count(1))
                        y = ry[:, i % 2, :, :]
                        dve.tensor_tensor(y, y, ps[:, 6:7, 0:T].to_broadcast([P, 2, T]), ALU.subtract).then_inc(ret_centred, 1)
                    elif name == "ret_var":
                        y = ry[:, i % 2, :, :]
                        dve.wait_ge(ret_rstd, head.count(1))
                        dve.tensor_tensor(y, y, rrstd[:, :].unsqueeze(1).to_broadcast([P, 2, T]), ALU.mult).then_inc(ret_normed, 1)
                        dve.wait_ge(ret_normed, head.count(1))
                        dve.wait_ge(gate_done, head.count(1))
                        dve.tensor_tensor(y, y, gr[:, 2 * i:2 * i + 2, :], ALU.mult).then_inc(ret_gated, 1)
                        dve.wait_ge(ret_gated, head.count(1))
                        dve.tensor_copy(retT[:, 2 * i:2 * i + 2, 0:T], y).then_inc(ret_hi, 1)
                        dve.wait_ge(ret_hi, head.count(1))
                        split_lo(retT[:, 2 * i:2 * i + 2, T:2 * T], retT[:, 2 * i:2 * i + 2, 0:T], y).then_inc(ret_lo, 1)

                for k in range(MIX_PIECES):
                    kind, i = mixer_piece(k)
                    piece = Place(k, (L, LAYER_PIECES))
                    use = Place(mixer_use(k), (L, LAYER_USES))
                    if kind in ("sbv", "rv"):
                        if i % 2 == 1:
                            dve.wait_ge(pair_act, use.count(1))
                            b = ps[:, 2 * use.slot(2) + 1, :]
                            if kind == "sbv":
                                dve.tensor_copy(sbv[:, 1, HALF * (i // 2):HALF * (i // 2 + 1)], b).then_inc(pair_free, 1)
                            else:
                                dve.tensor_copy(retqkv[:, 2 * (i // 2):2 * (i // 2) + 2, 3, :],
                                                b.rearrange("p (h c) -> p h c", h=2)).then_inc(pair_free, 1)
                    elif kind == "sbq":
                        add_cross(use, sbqk[:, i, 0:2, :])
                    elif kind == "sbk":
                        add_cross(use, sbqk[:, i, 2:4, :])
                    elif kind in ("rq", "rk"):
                        add_cross(use, retqkv[:, 2 * i:2 * i + 2, kind == "rk", :])
                    elif kind == "rg":
                        add_cross(use, gr[:, 2 * i:2 * i + 2, :])
                    elif kind in ("ga", "gb"):
                        add_cross(use, gates[:, kind == "gb", 2 * i:2 * i + 2, :])
                    elif kind in ("psb", "pret"):
                        if kind == "psb" and i == 0:
                            dve.wait_ge(gate_sig, Place(11, (L, 12)).count(1))
                        elif kind == "psb" or i == 0:
                            dve.wait_ge(branch_b, Place((i - 1) % 4, (L, 4)).count(1))
                        else:
                            dve.wait_ge(merged_lo, Place(i - 1, (L, 4)).count(1))
                        add_cross(use, gtmp[:, :, :])
                        rows = slice(2 * i, 2 * i + 2)
                        part = Place(i, (L, 4))
                        dve.wait_ge(pair_free, use.count(3))
                        if kind == "psb":
                            dve.tensor_tensor(gates[:, 1, rows, :], gates[:, 1, rows, :], gtmp[:, :, :],
                                              ALU.mult).then_inc(branch_b, 1)
                        else:
                            dve.tensor_tensor(gtmp[:, :, :], gates[:, 0, rows, :], gtmp[:, :, :],
                                              ALU.mult).then_inc(branch_a, 1)
                            dve.wait_ge(branch_a, part.count(1))
                            dve.tensor_tensor(gtmp[:, :, :], gates[:, 1, rows, :], gtmp[:, :, :],
                                              ALU.add).then_inc(merged, 1)
                            dve.wait_ge(merged, part.count(1))
                            dve.tensor_copy(hT[:, rows, 0:T], gtmp[:, :, :]).then_inc(merged_hi, 1)
                            dve.wait_ge(merged_hi, part.count(1))
                            split_lo(hT[:, rows, T:2 * T], hT[:, rows, 0:T], gtmp[:, :, :]).then_inc(merged_lo, 1)
                    gate = {"ga": 0, "rg": 4, "gb": 8}.get(kind)
                    if gate is not None:
                        gate = Place(gate + i, (L, 12))
                        g = gr[:, 2 * i:2 * i + 2, :] if kind == "rg" else gates[:, kind == "gb", 2 * i:2 * i + 2, :]
                        dve.wait_ge(pair_free, use.count(3))
                        if gate.fixed:
                            dve.wait_ge(gate_sig, gate.count(0))
                        if kind == "rg" and i or kind == "gb" and i == 0:
                            dve.wait_ge(gate_done, Place(i if kind == "rg" else RET_H, (L, RET_H)).count(0))
                        dve.tensor_scalar(gtmp[:, :, :], g, GATE_FLOOR, None, ALU.max).then_inc(gate_clamped, 1)
                    if k + 2 < MIX_PIECES:
                        convert(piece + 2)
                    if gate is not None:
                        dve.wait_ge(gate_soft, gate.count(1))
                        dve.scalar_tensor_tensor(out=gtmp[:, :, :], in0=g, scalar=-1.0, in1=gtmp[:, :, :],
                                                 op0=ALU.mult, op1=ALU.max).then_inc(gate_max, 1)
                    if k == 11:
                        dve.wait_ge(consts_in, Place(4, (L, 4)).count(0) * 16)
                    for s in stages(k):
                        stage(*s)
                mlp(Place(1, (L, 2)), Place(1, (L, 2)), Place(0, (L, 1)), Place(MIX_PIECES, (L, LAYER_PIECES)),
                    Place(MIX_USES, (L, LAYER_USES)))

            first, use0 = DEPTH * LAYER_PIECES, DEPTH * LAYER_USES
            dve.wait_ge(gain_in[0], 3 * 16)
            for j, (t, c) in enumerate(BY_TILE):
                q = quarter(t, c)
                dve.wait_ge(x_ready, 4 * 4 + (j + 1))
                dve.tensor_tensor(wide[:, t, q], xs[:, t, q], gain[:, 0, q], ALU.mult).then_inc(wide_ready, 1)
            dve.wait_ge(gain_in[1], 3 * 16)
            for t, c in BY_TILE:
                q = quarter(t, c)
                if c == 0:
                    dve.wait_ge(wide_step, 6 * (t + 1))
                dve.scalar_tensor_tensor(out=htok[:, t, q], in0=wide[:, t, q], scalar=wide_scale[:, t:t + 1],
                                         in1=gain[:, 1, q], op0=ALU.mult, op1=ALU.mult).then_inc(h_ready, 1)
            split_rows(Place(4), Place(first), Place(use0))
            dve.wait_ge(lb_step, 2)
            dve.reciprocal(hcol[:, LB_INV, :], hcol[:, LB_EXP, :]).then_inc(lb_step, 1)

            def second_gaps(n):
                if n == 0:
                    dve.wait_ge(f_cum, 3)
                    dve.tensor_tensor(btail[:, :, :], hb[:, :, CHUNK - 1:CHUNK], hb[:, :, P - 1:P],
                                      ALU.add).then_inc(e_second, 1)
                    return
                if n >= 2:
                    dve.wait_ge(pairs_full, n + 1)
                side = (hz, hlog)[n % 2]
                if n == len(LEVELS):
                    dve.tensor_tensor(side[:, :, 0:CHUNK], btail[:, :, :].to_broadcast([P, HG_H, CHUNK]),
                                      hb[:, :, 0:CHUNK], ALU.subtract)
                    dve.tensor_tensor(side[:, :, P + CHUNK:T], hb[:, :, P + CHUNK - 1:P + CHUNK].to_broadcast([P, HG_H, CHUNK]),
                                      hb[:, :, P + CHUNK:T], ALU.add).then_inc(e_second, 1)
                    return
                m = LEVELS[n]
                v = side[:, :, :].rearrange("p h (b two m) -> p (h b) two m", two=2, m=m)
                b = hb[:, :, :].rearrange("p h (b two m) -> p (h b) two m", two=2, m=m)
                end = b[:, :, 0, m - 1:m].to_broadcast([P, HG_H * T // (2 * m), m])
                dve.tensor_tensor(v[:, :, 1, :], b[:, :, 1, :], end, ALU.subtract).then_inc(e_second, 1)

            def second_side(n):
                m = LEVELS[n] if n < len(LEVELS) else P
                dve.wait_ge(e_exp, n + 1)
                if n == 0:
                    dve.wait_ge(silu_done, 3)
                v = (hz, hlog)[n % 2][:, :, :].rearrange("p h (b two m) -> p (h b) two m", two=2, m=m)[:, :, 1, :]
                q = hq[:, :, :].rearrange("p h (b two m) -> p (h b) two m", two=2, m=m)[:, :, 1, :]
                dve.tensor_tensor(v, v, q, ALU.mult).then_inc(x_second, 1)

            def put(n):
                dve.wait_ge(pairs_full, n + 1)
                kind, i = PAIRS[n]
                o = ps[:, 4 + 2 * (n % 2):6 + 2 * (n % 2), :].rearrange("p b c -> p (b c)")[:, 0:HG_H * P]
                if kind == "diag":
                    dve.tensor_tensor(st[:, 6 * i:6 * i + 6, :], o.rearrange("p (j c) -> p j c", c=P),
                                      ident.unsqueeze(1).to_broadcast([P, 6, P]), ALU.mult).then_inc(pairs_placed, 1)
                else:
                    m = LEVELS[i]
                    dve.wait_ge(pairs_placed, n)
                    if i == 0:
                        dve.wait_ge(cols_in, 64)
                    mask = levels_c[:, i, :].bitcast(U32).rearrange("p (b m) -> p b m", m=m)
                    dve.copy_predicated(
                        out=st[:, :, :].rearrange("p j (b two m) -> p j b two m", two=2, m=m)[:, :, :, 1, :],
                        mask=mask.unsqueeze(1).to_broadcast([P, HG_H * TILES, CHUNK // m, m]),
                        data=o.rearrange("p (j b m) -> p j b m", b=CHUNK // m, m=m)).then_inc(pairs_placed, 1)

            for k in range(MIX2_PIECES):
                kind, i = mixer2_piece(k)
                piece, use = Place(first + k), Place(use0 + k)
                h2 = slice(2 * i, 2 * i + 2)
                if kind == "v":
                    dve.wait_ge(pair_act, use.count(1))
                    dve.tensor_copy(hv[:, 1, 256 * i:256 * (i + 1)],
                                    ps[:, 2 * use.slot(2) + 1, 0:256]).then_inc(pair_free, 1)
                elif kind == "f":
                    add_cross(use, hz[:, h2, :])
                elif kind == "pool":
                    add_cross(use, pads[:, 0, :, PAD:])
                elif kind in ("q", "g"):
                    add_cross(use, (hq if kind == "q" else hg)[:, h2, :])
                n = i + (3 if kind == "g" else 0)
                if kind in ("q", "g"):
                    v = (hq if kind == "q" else hg)[:, h2, :]
                    dve.wait_ge(pair_free, use.count(3))
                    if n:
                        dve.wait_ge(silu_sig, n)
                    if n > 3:
                        dve.wait_ge(g_gated, n - 3)
                    elif n:
                        dve.wait_ge(silu_done, n)
                    dve.tensor_scalar(htmp[:, :, :], v, GATE_FLOOR, None, ALU.max).then_inc(silu_clamped, 1)
                if k + 2 < MIX2_PIECES:
                    convert(piece + 2)
                if kind == "f":
                    z, lg, fl = hz[:, h2, :], hlog[:, h2, :], hfloor[:, h2, :]
                    if i == 0:
                        dve.wait_ge(lb_step, 6)
                        dve.wait_ge(consts2_in, 32)
                    dve.wait_ge(f_ez, i + 1)
                    dve.scalar_tensor_tensor(out=fl, in0=fl, scalar=2.0 ** 63,
                                             in1=hcol[:, LB, h2].unsqueeze(2).to_broadcast([P, 2, T]),
                                             op0=ALU.min, op1=ALU.mult).then_inc(f_floor, 1)
                    dve.wait_ge(f_soft, i + 1)
                    dve.scalar_tensor_tensor(out=lg, in0=z, scalar=0.0, in1=lg, op0=ALU.min,
                                             op1=ALU.subtract).then_inc(f_ls, 1)
                    dve.wait_ge(f_ls, i + 1)
                    dve.tensor_tensor(hk[:, h2, :], lg, z, ALU.subtract).then_inc(f_kexp_in, 1)
                    dve.wait_ge(f_floor_log, i + 1)
                    dve.wait_ge(f_kexp_in, i + 1)
                    dve.tensor_tensor(lg, lg, fl, ALU.add).then_inc(f_log, 1)
                    dve.wait_ge(f_log, i + 1)
                    dve.tensor_tensor_scan(out=hb[:, h2, :].rearrange("p h t -> p (h t)"), data0=restart_c[:, :],
                                           data1=lg.rearrange("p h t -> p (h t)"), initial=0.0, op0=ALU.mult,
                                           op1=ALU.add).then_inc(f_cum, 1)
                if kind in ("q", "g"):
                    dve.wait_ge(silu_soft, n + 1)
                    dve.scalar_tensor_tensor(out=htmp[:, :, :], in0=v, scalar=-1.0, in1=htmp[:, :, :],
                                             op0=ALU.mult, op1=ALU.max).then_inc(silu_max, 1)
                    if kind == "q":
                        dve.wait_ge(silu_sig, n + 1)
                        dve.tensor_tensor(v, v, htmp[:, :, :], ALU.mult).then_inc(silu_done, 1)
                if k == 5:
                    second_gaps(0)
                if k == 7:
                    put(0)
                    put(1)
                if 6 <= k <= 12:
                    second_side(k - 6)
                if 7 <= k <= 12:
                    put(k - 5)
                if 6 <= k <= 11:
                    second_gaps(k - 5)
                if k == 12:
                    second_gaps(7)
                    second_side(7)
                    put(8)
                    dve.wait_ge(pool_hi, 1)
                    split_lo(hT[:, 0:2, T:2 * T], hT[:, 0:2, 0:T], py[:, :, :]).then_inc(y_lo, 1)
                    for r in range(3):
                        dve.wait_ge(o_squared, r + 1)
                        dve.tensor_copy(ho[:, 2 * r:2 * r + 2, :],
                                        ps[:, 4 + r, :].rearrange("p (h t) -> p h t", h=2)).then_inc(o_copied, 1)
                    for r in range(3):
                        v, hs = ho[:, 2 * r:2 * r + 2, :], slice(2 * r, 2 * r + 2)
                        dve.wait_ge(o_rstd, r + 1)
                        dve.wait_ge(o_copied, r + 1)
                        dve.tensor_tensor(v, v, hk[:, hs, :], ALU.mult).then_inc(o_normed, 1)
                        dve.wait_ge(o_normed, r + 1)
                        dve.wait_ge(g_scaled, r + 1)
                        dve.tensor_tensor(v, v, hg[:, hs, :], ALU.mult).then_inc(o_gated, 1)
                        dve.wait_ge(o_hi, r + 1)
                        split_lo(hT[:, 2 + 2 * r:4 + 2 * r, T:2 * T], hT[:, 2 + 2 * r:4 + 2 * r, 0:T], v).then_inc(y_lo, 1)
            dve.wait_ge(x_ready, 4 * 6)
            mlp(Place(6), Place(5), Place(2), Place(first + MIX2_PIECES), Place(use0 + MIX2_USES))
            norm_rows(Place(7), Place(3))


def slab_base(nc, size):
    return nc.sbuf_base - size


_INS = ["x", "w_in", "p_ret", "p_sb", "w_out", "w_up", "w_down", "g_mix", "g_mlp", "g_final", "norm_mix_g_2", "w_in_2",
        "pool_w_2", "pool_scale_2", "hgrn_lb_logits_2", "hgrn_norm_g_2", "w_out_2", "norm_mlp_g_2", "w_up_2",
        "w_down_2", "final_norm_g_2"]


def kernel(**inputs):
    import concourse.bacc as _bacc
    from concourse.bass_utils import run_bass_kernel_spmd as _run

    nc = _bacc.Bacc("TRN2", target_bir_lowering=False, num_devices=1)
    arrays, args = {}, []
    for name, a in [(n, np.ascontiguousarray(inputs[n])) for n in _INS] + list(constants().items()):
        arrays[f"in_{name}_dram"] = a
        args.append(nc.dram_tensor(f"in_{name}_dram", a.shape, mybir.dt.from_np(a.dtype), kind="ExternalInput").ap())
    args.append(nc.dram_tensor("out_0_dram", (1, T, D), F32, kind="ExternalOutput").ap())
    build(nc, *args)
    return _run(nc, [arrays], core_ids=[0]).results[0]["out_0_dram"]
```

```python
import math
from contextlib import ExitStack

import numpy as np

import concourse.bass as bass
from concourse import mybir

F32 = mybir.dt.float32
F32R = mybir.dt.float32r
U32 = mybir.dt.uint32
U8 = mybir.dt.uint8
ALU = mybir.AluOpType
ACT = mybir.ActivationFunctionType

P = 128
D = 1024
T = 256
TILES = T // P
KT = D // P
DEPTH = 2
HALF = 512
RET_H, SB_H, HG_H = 4, 8, 6
CAUSAL = T + P
SB_SCALE = P ** -0.5
CHUNK = 64
LEVELS = (64, 32, 16, 8, 4, 2, 1)
WINDOWS = (2, 4, 8, 16)
PAD = 16
GATE_FLOOR = -40.0
NORM_EPS, RMS_EPS, GN_EPS = 1e-6, 1e-5, 1e-5

RAW_SLOTS, SPLIT_SLOTS = 4, 2
MIX_PIECES, MLP_PIECES, MIX2_PIECES = 44, 32, 17
LAYER_PIECES = MIX_PIECES + MLP_PIECES
FF_PAIRS = MLP_PIECES // 2
MIX_USES, MLP_USES, MIX2_USES = 36, FF_PAIRS, 13
LAYER_USES = MIX_USES + MLP_USES
ALL_PIECES = DEPTH * LAYER_PIECES + MIX2_PIECES + MLP_PIECES


class Place:

    def __init__(self, fixed, *terms):
        self.fixed, self.terms = fixed, terms

    def __add__(self, n):
        return Place(self.fixed + n, *self.terms)

    def slot(self, n):
        assert all(stride % n == 0 for _, stride in self.terms)
        return self.fixed % n

    def count(self, more=0, per=1):
        v = self.fixed // per + more
        for reg, stride in self.terms:
            v = reg * (stride // per) + v
        return v


def constants():
    f = np.float32
    half = P // 2
    inv_freq = (10000.0 ** (-np.arange(half, dtype=f) / f(half))).astype(f)
    ang = np.arange(T, dtype=f)[None, :] * np.concatenate([inv_freq, inv_freq])[:, None]
    rope = np.stack([np.cos(ang), np.sin(ang)], 1).astype(f)
    s, t = np.arange(P)[:, None], np.arange(P)[None, :]
    decay = np.zeros((P, RET_H, CAUSAL), f)
    for h in range(RET_H):
        lg = math.log1p(-(2.0 ** (-5.0 - h)))
        d0 = np.arange(T)[None, :] - s
        decay[:, h, :T] = np.where(d0 >= 0, np.exp(lg * np.maximum(d0, 0)), 0.0) * P ** -0.5
        decay[:, h, T:] = np.where(t >= s, np.exp(lg * np.maximum(t - s, 0)), 0.0) * P ** -0.5
    before = (s < t).astype(f)
    mask = np.concatenate([before, np.ones((P, P), f), before], 1)
    mask = np.stack([mask, mask], 1)
    later = (s > t).astype(f)
    turn = np.zeros((P, P), f)
    turn[np.arange(half) + half, np.arange(half)] = -1.0
    turn[np.arange(half), np.arange(half) + half] = 1.0
    square = np.stack([np.eye(P, dtype=f), np.full((P, P), 1.0 / T, f), later, np.ones((P, P), f), turn], 1)
    levels = np.zeros((P, len(LEVELS), CHUNK), f)
    for n, m in enumerate(LEVELS):
        block = np.arange(CHUNK) // m
        levels[:, n] = (s >= block * 2 * m) & (s < block * 2 * m + m)
    restart = np.ones((P, 2 * T), f)
    restart[:, ::CHUNK] = 0.0
    counts = np.zeros((P, 2, T), f)
    for g, w in enumerate(WINDOWS):
        counts[64 * (g % 2):64 * (g % 2) + 64, g // 2] = 1.0 / np.minimum(np.arange(T) + 1, w)
    return {"rope": rope, "decay": decay, "mask": mask, "square": square,
            "levels": levels, "restart": restart, "counts": counts}


def build(nc, x, w_in, p_ret, p_sb, w_out, w_up, w_down, g_mix, g_mlp, g_final, norm_mix_g_2, w_in_2, pool_w_2,
          pool_scale_2, hgrn_lb_logits_2, hgrn_norm_g_2, w_out_2, norm_mlp_g_2, w_up_2, w_down_2, final_norm_g_2,
          rope, decay, mask, square, levels, restart, counts, out):
    ctx = ExitStack()
    with ctx:
        SLAB = 206 * 1024
        slab = ctx.enter_context(nc.sbuf_tensor("slab", [P, SLAB], U8))
        base = slab_base(nc, SLAB)
        at = [0]

        def place(name, shape, dtype, offset=None):
            size = int(np.prod(shape[1:])) * mybir.dt.size(dtype)
            if offset is None:
                offset = at[0]
                at[0] += -(-size // 32) * 32
            assert offset + size <= SLAB, (name, offset + size - SLAB)
            return nc.alloc_sbuf_tensor_at(name, shape, dtype, offset=base + offset)

        PIECE = 2048

        def parts(piece):
            ahead = DEPTH * LAYER_PIECES
            if not piece.terms and piece.fixed == ahead:
                return slice(0, 512), slice(512, PIECE)
            cut = 1024 if not piece.terms and ahead <= piece.fixed < ahead + MIX2_PIECES else 1216
            return slice(0, cut), slice(cut, PIECE)
        raw = place("raw", [P, RAW_SLOTS, PIECE], F32)
        w_hi = place("w_hi", [P, SPLIT_SLOTS, PIECE], F32R)
        w_lo = place("w_lo", [P, SPLIT_SLOTS, PIECE], F32R)
        xs = place("xs", [P, TILES, D], F32)
        hT = place("hT", [P, KT, 2 * T], F32R)
        gain = place("gain", [P, 2, D], F32)
        htok_at = at[0]
        htok = place("htok", [P, TILES, D], F32)
        carry = place("carry", [P, 2, 2, T], F32)
        sumsq = place("sumsq", [P, 4], F32)
        wide_sums = place("wide_sums", [P, 4], F32)
        wide_scale = place("wide_scale", [P, 2], F32)
        row_sumsq = place("row_sumsq", [P, 2], F32)
        row_scale = place("row_scale", [P, 2], F32)
        meansq = place("meansq", [P, 2], F32)
        rstd = place("rstd", [P, 2], F32)
        powers = place("powers", [P, 2], F32)
        rms_eps = place("rms_eps", [P, 1], F32)
        norm_eps = place("norm_eps", [P, 2], F32)
        gn_eps = place("gn_eps", [P, 1], F32)
        sq_r = place("sq_r", [P, 5, P], F32R, at[0])
        sq_c = place("sq_c", [P, 5, P], F32)
        ident, mean_w, turn = (sq_c[:, i, :] for i in (0, 1, 4))
        later, ones = sq_r[:, 2, :], sq_r[:, 3, :]
        rope_c = place("rope_c", [P, 2, T], F32)
        levels_c = place("levels_c", [P, len(LEVELS), CHUNK], F32)
        hcol = place("hcol", [P, 8, HG_H], F32)
        pool_w = place("pool_w", [P, 2, P], F32)
        mix_c_at = at[0]
        decay_c = place("decay_c", [P, RET_H, CAUSAL], F32)
        mask_c = place("mask_c", [P, 2, CAUSAL], F32)
        mix_at = at[0]
        sb_at = at[0]
        sbqk = place("sbqk", [P, SB_H // 2, 4, T], F32)
        sbT = place("sbT", [P, SB_H, 2 * T], F32R, sb_at)
        sbv = place("sbv", [P, TILES, D], F32)
        ret_at = at[0]
        retqkv = place("retqkv", [P, RET_H, 4, T], F32)
        retT = place("retT", [P, RET_H * 2, 2 * T], F32R, ret_at)
        u_at = at[0]
        gr = place("gr", [P, KT, T], F32)
        squares_at = at[0]
        gates = place("gates", [P, 2, KT, T], F32)
        zs = place("zs", [P, 2, CAUSAL], F32, htok_at)
        soft = place("soft", [P, 2, CAUSAL], F32, htok_at + 2 * CAUSAL * 4)
        logw = place("logw", [P, 2, CAUSAL], F32)
        wts = place("wts", [P, 2, CAUSAL], F32)
        rs = place("rs", [P, CAUSAL], F32)
        y_at = at[0]
        ry = place("ry", [P, 2, 2, T], F32)
        rest_hi = place("rest_hi", [P, 2, CAUSAL], F32R, at[0])
        rest_lo = place("rest_lo", [P, 2, CAUSAL], F32R, htok_at)
        rsq = place("rsq", [P, 2, T], F32)
        rrstd = place("rrstd", [P, T], F32)
        gtmp = place("gtmp", [P, 2, T], F32)
        rsum = place("rsum", [P, T], F32, htok_at)
        squares = place("squares", [P, D], F32, squares_at)
        uT = place("uT", [P, 2, 2, 2 * T], F32R, u_at)
        us = place("us", [P, 2, T], F32, y_at)
        usq = place("usq", [P, 2, T], F32, y_at + 2 * T * 4)
        wide = place("wide", [P, TILES, D], F32, squares_at)
        wide_sq = place("wide_sq", [P, TILES, D], F32, squares_at + TILES * D * 4)
        at[0] = mix_c_at
        restart_c = place("restart_c", [P, 2 * T], F32, htok_at)
        counts_c = place("counts_c", [P, 2, T], F32, htok_at + 2 * T * 4)
        at[0] = mix_at
        yT = place("yT", [P, KT, 2 * T], F32R, at[0])
        hz = place("hz", [P, HG_H, T], F32)
        hlog = place("hlog", [P, HG_H, T], F32)
        hfloor = place("hfloor", [P, HG_H, T], F32)
        hk = place("hk", [P, HG_H, T], F32)
        hq = place("hq", [P, HG_H, T], F32)
        hg = place("hg", [P, HG_H, T], F32)
        hb = place("hb", [P, HG_H, T], F32)
        hv = place("hv", [P, TILES, HG_H * P], F32)
        st = place("st", [P, HG_H * TILES, P], F32)
        cross = place("cross", [P, HG_H, P], F32)
        ho = place("ho", [P, HG_H, T], F32)
        htmp = place("htmp", [P, 2, T], F32)
        pads = place("pads", [P, 5, 2, PAD + T], F32)
        pmix = place("pmix", [P, 2, T], F32)
        btail = place("btail", [P, HG_H, 1], F32)
        LB_LOGIT, LB_EXP, LB, ONE_LESS, HNORM, PSCALE, LB_INV, LB_P = range(8)

        ps = ctx.enter_context(nc.psum_tensor("ps", [P, 8, HALF], F32))

        def sem(name):
            return ctx.enter_context(nc.semaphore(name))

        raw_in = [sem(f"raw_in{i}") for i in range(RAW_SLOTS)]
        hi_ready = sem("hi_ready")
        hi_dve = sem("hi_dve")
        lo_dve = sem("lo_dve")
        lo_pool = sem("lo_pool")
        piece_used = sem("piece_used")
        pair_act = sem("pair_act")
        pair_free = sem("pair_free")
        consts_in = sem("consts_in")
        x_in = [sem("x_in0"), sem("x_in1")]
        ident_in = sem("ident_in")
        gain_in = [sem("gain_in0"), sem("gain_in1")]
        small_set = sem("small_set")
        x_ready = sem("x_ready")
        sq_ready = sem("sq_ready")
        wide_ready, wide_sq_ready, wide_step = (sem(n) for n in ("wide_ready", "wide_sq_ready", "wide_step"))
        mean_ready = sem("mean_ready")
        rstd_ready = sem("rstd_ready")
        h_ready = sem("h_ready")
        h_hi, h_lo, row_sq, row_mean, row_ready = (sem(n) for n in ("h_hi", "h_lo", "row_sq", "row_mean", "row_ready"))
        h_turned = sem("h_turned")
        out_full = sem("out_full")
        down_full = sem("down_full")
        z_full, z_scaled, z_abs, sb_exp, softplus, log_beta, neg_log_rest, masked_rest = (
            sem(n) for n in ("z_full", "z_scaled", "z_abs", "sb_exp", "softplus", "log_beta", "neg_log_rest",
                             "masked_rest"))
        after_full, log_weight, weight_exp, weight_ready, sb_out, sb_hi, sb_lo = (
            sem(n) for n in ("after_full", "log_weight", "weight_exp", "weight_ready", "sb_out", "sb_hi", "sb_lo"))
        ret_summed, square_rounded = sem("ret_summed"), sem("square_rounded")
        rest_rounded, rest_split = sem("rest_rounded"), sem("rest_split")
        turned, rope_cos, rope_sin, rope_done = (sem(n) for n in ("turned", "rope_cos", "rope_sin", "rope_done"))
        ret_scores, ret_decayed, ret_out, ret_copied, ret_mean, ret_centred, ret_squared, ret_var = (
            sem(n) for n in ("ret_scores", "ret_decayed", "ret_out", "ret_copied", "ret_mean", "ret_centred",
                             "ret_squared", "ret_var"))
        ret_log, ret_rstd, ret_normed, ret_gated, ret_hi, ret_lo = (
            sem(n) for n in ("ret_log", "ret_rstd", "ret_normed", "ret_gated", "ret_hi", "ret_lo"))
        gate_clamped, gate_exp, gate_soft, gate_max, gate_sig, gate_done = (
            sem(n) for n in ("gate_clamped", "gate_exp", "gate_soft", "gate_max", "gate_sig", "gate_done"))
        branch_a, branch_b, merged, merged_hi, merged_lo = (
            sem(n) for n in ("branch_a", "branch_b", "merged", "merged_hi", "merged_lo"))
        u_squared, u_hi, u_lo = (sem(n) for n in ("u_squared", "u_hi", "u_lo"))
        consts2_in, cols_in, pads_zero, pool_w_zero, pool_w_in = (
            sem(n) for n in ("consts2_in", "cols_in", "pads_zero", "pool_w_zero", "pool_w_in"))
        lb_step, pool_step, pool_full, pool_hi = (
            sem(n) for n in ("lb_step", "pool_step", "pool_full", "pool_hi"))
        f_clamped, f_soft, f_ls, f_kexp_in, f_kexp, f_k, f_ez, f_floor, f_floor_log, f_log, f_cum = (
            sem(n) for n in ("f_clamped", "f_soft", "f_ls", "f_kexp_in", "f_kexp", "f_k", "f_ez", "f_floor",
                             "f_floor_log", "f_log", "f_cum"))
        silu_clamped, silu_exp, silu_soft, silu_max, silu_sig, silu_done, g_gated, g_scaled = (
            sem(n) for n in ("silu_clamped", "silu_exp", "silu_soft", "silu_max", "silu_sig", "silu_done", "g_gated",
                             "g_scaled"))
        e_first, e_second, e_exp, x_first, x_second, pairs_full, pairs_placed = (
            sem(n) for n in ("e_first", "e_second", "e_exp", "x_first", "x_second", "pairs_full", "pairs_placed"))
        o_full, o_copied, o_squared, o_mean, o_log, o_rstd, o_normed, o_gated, o_hi, y_lo = (
            sem(n) for n in ("o_full", "o_copied", "o_squared", "o_mean", "o_log", "o_rstd", "o_normed", "o_gated",
                             "o_hi", "y_lo"))
        out_sent = sem("out_sent")

        block = ctx.enter_context(nc.Block())

        MIXER = [(name, i) for name, n in (("ga", 4), ("sbq", 4), ("sbk", 4), ("sbv", 4), ("rq", 2), ("rk", 2),
                                           ("rv", 4), ("rg", 4), ("gb", 4), ("psb", 4), ("pret", 4), ("wout", 4))
                 for i in range(n)]
        assert len(MIXER) == MIX_PIECES

        def mixer_piece(k):
            return MIXER[k]

        def mixer_use(k):
            return sum(1 for name, i in MIXER[:k] if name not in ("sbv", "rv") or i % 2)

        def use_of(name, i, L):
            return Place(mixer_use(MIXER.index((name, i))), (L, LAYER_USES))

        BY_TILE = [(0, 0), (0, 1), (1, 0), (1, 1)]
        BY_HALF = [(0, 0), (1, 0), (0, 1), (1, 1)]

        def norm_bank(use, j):
            return 2 * ((j // 2 + use.slot(2)) % 2) + j % 2

        def stages(k):
            todo = []
            for p in range(SB_H // 2):
                if k == 14 + 3 * p:
                    todo.append(("sb_after", p))
                if k == 15 + 3 * p:
                    todo.append(("sb_out", p))
            for p in range(SB_H // 2):
                if k == 12 + 3 * p:
                    todo.append(("sb_scores", p))
            if k in (22, 23):
                todo.append(("rotate", k - 22))
            for lag, name in ((3, "ret_var"), (2, "ret_mean"), (1, "ret_out"), (0, "ret_scores")):
                for h in range(RET_H):
                    if k == 24 + 2 * h + lag:
                        todo.append((name, h))
            return todo

        def mixer2_piece(k):
            for name, n in (("f", 3), ("q", 3), ("pool", 1), ("v", 3), ("g", 3), ("wout", 4)):
                if k < n:
                    return name, k
                k -= n

        PAIRS = [("diag", 0), ("diag", 1)] + [("level", n) for n in range(len(LEVELS))] + [("cross", 0)]

        UNITS = len(LEVELS) + 1
        UNIT_SLOT = 13
        OUT_SLOT = UNIT_SLOT + UNITS
        FIRST_UNITS, LAST_UNITS = UNIT_SLOT // 2, OUT_SLOT // 2 - 1

        def units_beside(k):
            return [s - UNIT_SLOT for s in (2 * k + 1, 2 * k + 2) if 0 <= s - UNIT_SLOT < UNITS]

        def gated_beside(k):
            return {11: (0,), 12: (1, 2)}.get(k, ())

        def firsts(u):
            return u + 1 if u < len(LEVELS) - 1 else u

        @block.sync
        def _(sp):
            def piece_in(piece, source, ahead=0):
                if ahead is not None:
                    sp.wait_ge(lo_dve, (piece + ahead).count(1))
                    sp.wait_ge(lo_pool, (piece + ahead).count(1))
                s = piece.slot(RAW_SLOTS)
                d = raw[:, s, :].rearrange("p (k c) -> p k c", k=source.shape[1])
                sp.dma_start(d, source).then_inc(raw_in[s], 16)

            def gain_load(n, source, read=None):
                sp.wait_ge(*(read or (h_ready, n.count(1) * 4)))
                sp.dma_start(gain[:, n.slot(2), :], source.partition_broadcast(P)).then_inc(gain_in[n.slot(2)], 16)

            def across(w, column):
                return w.rearrange("(k p) c -> p k c", p=P)[:, :, column:column + 256]

            def along(w, row, column):
                return w.rearrange("(k p) c -> p k c", p=P)[:, row:row + 4, column:column + HALF]

            def mlp_loads(piece, up, down):
                ups = up.rearrange("(k p) (i c) -> i p k c", p=P, c=256)
                downs = down.rearrange("(i k p) c -> i p k c", p=P, k=2)
                piece_in(piece, ups[0])
                piece_in(piece + 1, ups[1])
                piece_in(piece + 2, downs[0])
                with sp.Fori(0, (FF_PAIRS - 2) // 2) as i:
                    here = Place(piece.fixed + 3, *piece.terms, (i, 4))
                    for j in range(2):
                        piece_in(here + 2 * j, ups[i * 2 + (2 + j)])
                        piece_in(here + (2 * j + 1), downs[i * 2 + (1 + j)])
                piece_in(piece + 31, downs[FF_PAIRS - 1])

            xt = x.rearrange("b (n p) d -> (b n) p d", p=P)
            for t in range(TILES):
                sp.dma_start(xs[:, t, :], xt[t]).then_inc(x_in[t], 16)
            sp.dma_start(sq_c[:, 0, :], square[:, 0]).then_inc(ident_in, 16)
            COLUMN_0 = MIXER.index(("rq", 0))
            with sp.Fori(0, DEPTH) as L:
                for k in range(MIX_PIECES):
                    kind, i = mixer_piece(k)
                    piece = Place(k, (L, LAYER_PIECES))
                    column = {"rq": 0, "rk": 512, "rv": 1024, "rg": 2048, "sbq": 3072, "sbk": 4096, "sbv": 5120,
                              "ga": 6144, "gb": 7168}.get(kind)
                    if kind in ("sbv", "rv"):
                        source = along(w_in[L], 4 * (i % 2), column + HALF * (i // 2))
                    elif column is not None:
                        source = across(w_in[L], column + 256 * i)
                    elif kind == "wout":
                        source = along(w_out[L], 4 * (i // 2), HALF * (i % 2))
                    else:
                        source = across({"pret": p_ret, "psb": p_sb}[kind][L], 256 * i)
                    piece_in(piece, source, {COLUMN_0 - 1: 1, COLUMN_0: None}.get(k, 0))
                    if k == 0:
                        gain_load(Place(0, (L, 2)), g_mix[L])
                    if k == 1:
                        gain_load(Place(1, (L, 2)), g_mlp[L])
                    if k == 7:
                        sp.dma_start(sq_c[:, 1:5, :], square[:, 1:5]).then_inc(consts_in, 16)
                        sp.dma_start(rope_c[:, :, :], rope).then_inc(consts_in, 16)
                        sp.dma_start(decay_c[:, :, :], decay).then_inc(consts_in, 16)
                        sp.dma_start(mask_c[:, :, :], mask).then_inc(consts_in, 16)
                mlp_loads(Place(MIX_PIECES, (L, LAYER_PIECES)), w_up[L], w_down[L])

            sp.dma_start(levels_c[:, :, :], levels).then_inc(cols_in, 16)
            for row, source, n in ((LB_LOGIT, hgrn_lb_logits_2, HG_H), (HNORM, hgrn_norm_g_2, HG_H),
                                   (PSCALE, pool_scale_2, 2)):
                sp.dma_start(hcol[:, row, 0:n], source[0].rearrange("(h p) -> p h", p=P),
                             allow_slow_non_contiguous=True).then_inc(cols_in, 16)
            sp.wait_ge(pool_w_zero, 1)
            for g in range(len(WINDOWS)):
                lo = 64 * (g % 2)
                sp.dma_start(pool_w[lo:lo + 64, g // 2, lo:lo + 64], pool_w_2[0, g]).then_inc(pool_w_in, 16)
            gain_load(Place(4), g_final)
            gain_load(Place(5), norm_mix_g_2[0])
            first = DEPTH * LAYER_PIECES
            for k in range(MIX2_PIECES):
                kind, i = mixer2_piece(k)
                column = {"pool": 0, "q": 256, "f": 1024, "v": 1792, "g": 2560}.get(kind)
                source = (along(w_out_2[0], 4 * (i // 2), HALF * (i % 2)) if kind == "wout"
                          else across(w_in_2[0], column + 256 * i))
                piece_in(Place(first + k), source)
                if k == 3:
                    gain_load(Place(6), norm_mlp_g_2[0], (x_ready, 4 * 6))
                if k == 3:
                    sp.wait_ge(x_ready, 4 * 6)
                    sp.dma_start(restart_c[:, :], restart).then_inc(consts2_in, 16)
                    sp.dma_start(counts_c[:, :, :], counts).then_inc(consts2_in, 16)
            mlp_loads(Place(first + MIX2_PIECES), w_up_2[0], w_down_2[0])
            gain_load(Place(7), final_norm_g_2, (h_ready, 8 + 4 * 5))
            ot = out.rearrange("b (n p) d -> (b n) p d", p=P)
            for t in range(TILES):
                sp.wait_ge(h_ready, 8 + 4 * 6 + 2 * (t + 1))
                sp.dma_start(ot[t], htok[:, t, :]).then_inc(out_sent, 16)
            sp.wait_ge(out_sent, 16 * TILES)

        @block.tensor
        def _(pe):
            def mm(o, lhsT, rhs, start, stop):
                return pe.matmul(o, lhsT, rhs, start=start, stop=stop)

            def split_ready(piece):
                pe.wait_ge(lo_dve, piece.count(RAW_SLOTS + 1))
                pe.wait_ge(lo_pool, piece.count(RAW_SLOTS + 1))
                s = piece.slot(SPLIT_SLOTS)
                return w_hi[:, s, :], w_lo[:, s, :]

            def across(piece, use, moving, between=None):
                hi, lo = split_ready(piece)
                pe.wait_ge(pair_free, use.count(1))
                for m in range(2):
                    bank = ps[:, 2 * use.slot(2) + m, :]
                    for k in range(KT):
                        c = k * 256 + m * P
                        mm(bank, hi[:, c:c + P], moving[:, k, :], k == 0, False)
                        last = mm(bank[:, T:2 * T], lo[:, c:c + P], moving[:, k, 0:T], False, k == KT - 1)
                    if m == 0 and between:
                        between()
                last.then_inc(piece_used, 1)

            def three(o, stationary, t, hi, lo, start, stop):
                a, b = stationary[:, t * P:(t + 1) * P], stationary[:, T + t * P:T + (t + 1) * P]
                mm(o, a, hi, start, False)
                mm(o, a, lo, False, False)
                return mm(o, b, hi, False, stop)

            def norm(n, piece, use, order):
                by_tile = order is BY_TILE

                def turn_quarter(j):
                    t, c = order[j]
                    pe.wait_ge(h_ready, n.count(0) * 4 + (8 + j + 1))
                    for k in range(4):
                        last = pe.transpose(ps[:, norm_bank(use, j), k * P:(k + 1) * P],
                                            htok[:, t, c * HALF + k * P:c * HALF + (k + 1) * P], ident)
                    last.then_inc(h_turned, 1)

                def products(m, g):
                    bank = ps[:, 2 * use.slot(2) + m, :].rearrange("p (s t) -> p s t", s=2)
                    tokens = slice(g * P, (g + 1) * P) if by_tile else slice(0, T)
                    for k in range(KT) if by_tile else range(4 * g, 4 * g + 4):
                        c = k * 256 + m * P
                        both = hT[:, k, :].rearrange("p (s t) -> p s t", s=2)
                        mm(bank[:, :, tokens], hi[:, c:c + P], both[:, :, tokens], k == 0, False)
                        last = mm(bank[:, 1, tokens], lo[:, c:c + P], both[:, 0, tokens], False, k == KT - 1)
                    return last

                pe.wait_ge(pair_free, use.count(2))
                turn_quarter(0)
                turn_quarter(1)
                hi, lo = split_ready(piece)
                turn_quarter(2)
                pe.wait_ge(h_lo, n.count(0) * 4 + 2)
                products(0, 0)
                turn_quarter(3)
                products(1, 0)
                pe.wait_ge(h_lo, n.count(0) * 4 + 4)
                products(0, 1)
                products(1, 1).then_inc(piece_used, 1)

            def down(piece, i, first, last_one, slot):
                hi, lo = split_ready(piece)
                pe.wait_ge(u_lo, i.count(1))
                for t, c in BY_TILE:
                    for k in range(2):
                        w = slice(k * D + c * HALF, k * D + (c + 1) * HALF)
                        last = three(ps[:, 4 + 2 * t + c, :], uT[:, slot, k, :], t, hi[:, w], lo[:, w],
                                     first and k == 0, last_one and k == 1)
                    if last_one and (t, c) != BY_TILE[-1]:
                        last.then_inc(down_full, 1)
                last.then_inc(piece_used, 1)

            def mlp(n, stage, piece, use):
                norm(n, piece, use, BY_HALF)
                across(piece + 1, use + 1, hT)
                down(piece + 2, Place(0, *stage), True, False, 0)
                with pe.Fori(0, (FF_PAIRS - 2) // 2) as i:
                    here = Place(piece.fixed + 3, *piece.terms, (i, 4))
                    up = Place(use.fixed + 2, *use.terms, (i, 2))
                    for j in range(2):
                        across(here + 2 * j, up + j, hT)
                        down(here + (2 * j + 1), Place(1 + j, *stage, (i, 2)), False, False, (1 + j) % 2)
                down(piece + 31, Place(FF_PAIRS - 1, *stage), False, True, 1)

            def out_piece(piece, i, moving=hT):
                hi, lo = split_ready(piece)
                for t in range(TILES):
                    for k in range(4):
                        w = slice(k * HALF, (k + 1) * HALF)
                        last = three(ps[:, 4 + 2 * t + i % 2, :], moving[:, 4 * (i // 2) + k, :], t, hi[:, w], lo[:, w],
                                     i < 2 and k == 0, i >= 2 and k == 3)
                    if (i, t) in ((2, 0), (3, 0)):
                        last.then_inc(out_full, 1)
                last.then_inc(piece_used, 1)

            def causal(bank, lhs0, lhs1, rhs):
                mm(bank[:, 0:T], lhs0, rhs, True, True)
                return mm(bank[:, T:CAUSAL], lhs1, rhs[:, P:T], True, True)

            pe.wait_ge(ident_in, 16)
            with pe.Fori(0, DEPTH) as L:
                norm(Place(0, (L, 2)), Place(0, (L, LAYER_PIECES)), Place(0, (L, LAYER_USES)), BY_TILE)

                def stage(name, i):
                    pair, head = Place(i, (L, SB_H // 2)), Place(i, (L, RET_H))
                    if name == "sb_scores":
                        pe.wait_ge(pair_free, use_of("sbk", 3, L).count(3))
                        for j in range(2):
                            q, k = sbqk[:, i, j, :], sbqk[:, i, 2 + j, :]
                            last = causal(ps[:, 4 + j, :], k[:, 0:P], k[:, P:T], q)
                        last.then_inc(z_full, 1)
                    elif name == "sb_after":
                        pe.wait_ge(rest_split, pair.count(1))
                        pe.wait_ge(square_rounded, Place(0, (L, 1)).count(1))
                        for j in range(2):
                            bank = ps[:, 6 + j, :]
                            hi, lo = rest_hi[:, j, :], rest_lo[:, j, :]
                            mm(bank[:, 0:T], later, hi[:, 0:T], True, False)
                            mm(bank[:, 0:T], later, lo[:, 0:T], False, False)
                            mm(bank[:, P:T], ones, hi[:, T:CAUSAL], False, False)
                            mm(bank[:, P:T], ones, lo[:, T:CAUSAL], False, True)
                            mm(bank[:, T:CAUSAL], later, hi[:, T:CAUSAL], True, False)
                            last = mm(bank[:, T:CAUSAL], later, lo[:, T:CAUSAL], False, True)
                        last.then_inc(after_full, 1)
                    elif name == "sb_out":
                        pe.wait_ge(weight_ready, pair.count(1))
                        pe.wait_ge(pair_free, use_of("sbv", 2 * (i // 2), L).count(3))
                        for j in range(2):
                            o = ps[:, 6, j * T:(j + 1) * T]
                            c = (2 * i + j) * P
                            mm(o, sbv[:, 0, c:c + P], wts[:, j, 0:T], True, False)
                            last = mm(o[:, P:T], sbv[:, 1, c:c + P], wts[:, j, T:CAUSAL], False, True)
                        last.then_inc(sb_out, 1)
                    elif name == "rotate":
                        pe.wait_ge(pair_free, use_of("rk", 1, L).count(3))
                        pe.wait_ge(z_scaled, Place(3, (L, 4)).count(1))
                        if i:
                            pe.wait_ge(rope_sin, Place(0, (L, 2)).count(1))
                        for j in range(2):
                            last = mm(ps[:, 4 + j, :], turn, retqkv[:, 2 * j:2 * j + 2, i, :], True, True)
                        last.then_inc(turned, 1)
                    elif name == "ret_scores":
                        pe.wait_ge(rope_done, Place(1, (L, 2)).count(1))
                        if i:
                            pe.wait_ge(ret_decayed, head.count(0))
                        k = retqkv[:, i, 1, :]
                        causal(ps[:, 4, :], k[:, 0:P], k[:, P:T], retqkv[:, i, 0, :]).then_inc(ret_scores, 1)
                    elif name == "ret_out":
                        pe.wait_ge(ret_decayed, head.count(1))
                        pe.wait_ge(pair_free, use_of("rv", 2 * (i // 2), L).count(3))
                        for e in range(2):
                            o = ps[:, 5, e * T:(e + 1) * T]
                            mm(o, retqkv[:, i, 2, e * P:(e + 1) * P], rs[:, 0:T], True, False)
                            last = mm(o[:, P:T], retqkv[:, i, 3, e * P:(e + 1) * P], rs[:, T:CAUSAL], False, True)
                        last.then_inc(ret_out, 1)
                    elif name == "ret_mean":
                        if i == 0:
                            pe.wait_ge(sb_lo, Place(3, (L, 4)).count(1))
                        pe.wait_ge(ret_summed, head.count(0) * 2 + 1)
                        mm(ps[:, 6, 0:T], mean_w, rsum[:, :], True, True).then_inc(ret_mean, 1)
                    elif name == "ret_var":
                        pe.wait_ge(ret_summed, head.count(1) * 2)
                        mm(ps[:, 7, 0:T], mean_w, rsq[:, 0, :], True, True).then_inc(ret_var, 1)

                for k in range(MIX_PIECES):
                    kind, i = mixer_piece(k)
                    piece = Place(k, (L, LAYER_PIECES))
                    use = Place(mixer_use(k), (L, LAYER_USES))
                    if kind in ("sbv", "rv"):
                        hi, lo = split_ready(piece)
                        if i % 2 == 0:
                            pe.wait_ge(pair_free, use.count(1))
                        for t in range(TILES):
                            for kk in range(4):
                                w = slice(kk * HALF, (kk + 1) * HALF)
                                last = three(ps[:, 2 * use.slot(2) + t, :], hT[:, 4 * (i % 2) + kk, :], t, hi[:, w],
                                             lo[:, w], i % 2 == 0 and kk == 0, i % 2 == 1 and kk == 3)
                        last.then_inc(piece_used, 1)
                    elif kind == "wout":
                        pe.wait_ge(merged_lo, Place(2 * (i // 2) + 1, (L, 4)).count(1))
                        out_piece(piece, i)
                    else:
                        if kind == "pret":
                            pe.wait_ge(ret_lo, Place(RET_H - 1, (L, RET_H)).count(1))
                        if kind == "psb":
                            pe.wait_ge(sb_lo, Place(3, (L, 4)).count(1))
                        if k:
                            across(piece, use, {"pret": retT, "psb": sbT}.get(kind, hT))
                    if k == 11:
                        pe.wait_ge(consts_in, Place(4, (L, 4)).count(0) * 16)
                    for s in stages(k):
                        stage(*s)
                mlp(Place(1, (L, 2)), ((L, FF_PAIRS),), Place(MIX_PIECES, (L, LAYER_PIECES)),
                    Place(MIX_USES, (L, LAYER_USES)))

            first, use0 = DEPTH * LAYER_PIECES, DEPTH * LAYER_USES
            norm(Place(4), Place(first), Place(use0), BY_TILE)

            def pairs(n):
                kind, i = PAIRS[n]
                if n >= 2:
                    pe.wait_ge(pairs_placed, n - 1)
                o = ps[:, 4 + 2 * (n % 2):6 + 2 * (n % 2), :].rearrange("p b c -> p (b c)")
                if kind == "diag":
                    for j in range(6):
                        h, t = divmod(6 * i + j, 2)
                        c = slice(t * P, (t + 1) * P)
                        last = mm(o[:, j * P:(j + 1) * P], hk[:, h, c], hq[:, h, c], True, True)
                elif kind == "level":
                    m = LEVELS[i]
                    if m > 1:
                        pe.wait_ge(x_first, firsts(i))
                    pe.wait_ge(x_second, i + 1)
                    for j in range(HG_H * TILES):
                        tokens = slice((j % 2) * P, (j % 2 + 1) * P)
                        side = (hz, hlog)[i % 2][:, j // 2, tokens]
                        rhs = side.rearrange("p (b two m) -> p b two m", two=2, m=m)[:, :, 1, :]
                        last = mm(o[:, j * CHUNK:(j + 1) * CHUNK].rearrange("p (b m) -> p b m", m=m),
                                  side if m > 1 else hk[:, j // 2, tokens], rhs, True, True)
                else:
                    pe.wait_ge(x_first, firsts(len(LEVELS)))
                    pe.wait_ge(x_second, len(LEVELS) + 1)
                    side = (hz, hlog)[len(LEVELS) % 2]
                    for h in range(HG_H):
                        last = mm(o[:, h * P:(h + 1) * P], side[:, h, 0:P], side[:, h, P:T], True, True)
                last.then_inc(pairs_full, 1)

            def slot(n):
                if n == UNIT_SLOT:
                    pe.wait_ge(f_k, 3)
                    pe.wait_ge(silu_done, 3)
                    pairs(0)
                    pairs(1)
                if 0 <= n - UNIT_SLOT < UNITS:
                    pairs(2 + n - UNIT_SLOT)
                if n == OUT_SLOT:
                    pe.wait_ge(pairs_placed, len(PAIRS))
                    for r in range(3):
                        for j in range(2):
                            h = 2 * r + j
                            o, c = ps[:, 4 + r, j * T:(j + 1) * T], slice(h * P, (h + 1) * P)
                            mm(o[:, 0:P], hv[:, 0, c], st[:, 2 * h, :], True, True)
                            mm(o[:, P:T], hv[:, 0, c], cross[:, h, :], True, False)
                            last = mm(o[:, P:T], hv[:, 1, c], st[:, 2 * h + 1, :], False, True)
                        last.then_inc(o_full, 1)
                if n == OUT_SLOT + 1:
                    pe.wait_ge(pool_step, 9)
                    pe.wait_ge(pool_w_in, 16 * len(WINDOWS))
                    for b in range(2):
                        last = mm(ps[:, 7, b * T:(b + 1) * T], pool_w[:, b, :], pmix[:, b, :], True, True)
                    last.then_inc(pool_full, 1)
                    for r in range(3):
                        pe.wait_ge(o_copied, r + 1)
                        pe.wait_ge(o_squared, r + 1)
                        mm(ps[:, 4 + r, :], mean_w, hb[:, 2 * r:2 * r + 2, :], True, True).then_inc(o_mean, 1)

            for k in range(MIX2_PIECES):
                kind, i = mixer2_piece(k)
                piece, use = Place(first + k), Place(use0 + k)
                if kind == "v":
                    hi, lo = split_ready(piece)
                    pe.wait_ge(pair_free, use.count(1))
                    for t in range(TILES):
                        if t == 1:
                            slot(2 * k)
                        for kk in range(KT):
                            w = slice(kk * 256, (kk + 1) * 256)
                            last = three(ps[:, 2 * use.slot(2) + t, 0:256], hT[:, kk, :], t, hi[:, w], lo[:, w],
                                         kk == 0, kk == KT - 1)
                    last.then_inc(piece_used, 1)
                elif kind == "wout":
                    pe.wait_ge(y_lo, 3 if i < 2 else 5)
                    out_piece(piece, i, yT)
                elif k:
                    across(piece, use, hT, lambda: slot(2 * k))
                slot(2 * k + 1)
            mlp(Place(5), ((1, DEPTH * FF_PAIRS),), Place(first + MIX2_PIECES), Place(use0 + MIX2_USES))

        @block.scalar
        def _(act):
            def convert(piece):
                act.wait_ge(raw_in[piece.slot(RAW_SLOTS)], piece.count(1, RAW_SLOTS) * 16)
                act.wait_ge(piece_used, piece.count(1))
                part = parts(piece)[0]
                act.activation(w_hi[:, piece.slot(SPLIT_SLOTS), part], raw[:, piece.slot(RAW_SLOTS), part],
                               ACT.Copy).then_inc(hi_ready, 1)

            def carry_cross(piece, use):
                act.wait_ge(piece_used, piece.count(SPLIT_SLOTS + 1))
                b = 2 * use.slot(2)
                act.activation(carry[:, use.slot(2), :, :], ps[:, b:b + 2, T:2 * T], ACT.Copy).then_inc(pair_act, 1)

            def square_sums(n, between=None):
                for j, (t, c) in enumerate(BY_TILE):
                    if j == 2 and between:
                        between()
                    act.wait_ge(x_ready, n.count(0) * 4 + (j + 1))
                    half = slice(c * HALF, (c + 1) * HALF)
                    act.activation(htok[:, t, half], xs[:, t, half], ACT.Square, scale=D ** -0.5,
                                   accum_out=sumsq[:, 2 * t + c:2 * t + c + 1]).then_inc(sq_ready, 1)

            def turned_hi(h, use, order):
                for j, (t, c) in enumerate(order):
                    act.wait_ge(h_turned, h.count(0) * 4 + (j + 1))
                    act.activation(hT[:, 4 * c:4 * c + 4, t * P:(t + 1) * P],
                                   ps[:, norm_bank(use, j), :].rearrange("p (k c) -> p k c", c=P),
                                   ACT.Copy).then_inc(h_hi, 1)

            def norm(n, h, piece, use):
                square_sums(n, lambda: convert(piece))
                turned_hi(h, use, BY_TILE)
                convert(piece + 1)

            def mlp(n, h, stage, piece, use):
                convert(piece)
                turned_hi(h, use, BY_HALF)
                convert(piece + 1)
                for t in range(TILES):
                    act.wait_ge(x_ready, n.count(1) * 4)
                    act.activation(squares[:, :], xs[:, t, :], ACT.Square, scale=D ** -0.5,
                                   accum_out=row_sumsq[:, t:t + 1]).then_inc(row_sq, 1)
                    if t == 0:
                        act.wait_ge(row_sq, stage.count(0) * 2 + 1)

                def up(piece, use):
                    carry_cross(piece, use)
                    convert(piece + 2)

                up(piece, use)
                up(piece + 1, use + 1)
                convert(piece + 4)
                steps = (FF_PAIRS - 2) // 2 - 1
                with act.Fori(0, steps) as i:
                    here, u = Place(piece.fixed + 3, *piece.terms, (i, 4)), Place(use.fixed + 2, *use.terms, (i, 2))
                    for j in range(2):
                        up(here + 2 * j, u + j)
                        convert(here + (2 * j + 3))
                here, u = piece + (3 + 4 * steps), use + (2 + 2 * steps)
                up(here, u)
                convert(here + 3)
                up(here + 2, u + 1)

            act.preload_act_table_set("natural_log_exp_and_others")
            act.wait_ge(small_set, 6)
            with act.Fori(0, DEPTH) as L:
                norm(Place(0, (L, 2)), Place(0, (L, 2)), Place(0, (L, LAYER_PIECES)), Place(0, (L, LAYER_USES)))

                def stage(name, i):
                    pair, head = Place(i, (L, SB_H // 2)), Place(i, (L, RET_H))
                    if name == "sb_scores":
                        act.wait_ge(z_full, pair.count(1))
                        act.activation(zs[:, :, :], ps[:, 4:6, 0:CAUSAL], ACT.Copy, scale=SB_SCALE).then_inc(z_scaled, 1)
                        act.wait_ge(z_abs, pair.count(1))
                        act.activation(soft[:, :, :], soft[:, :, :], ACT.Exp).then_inc(sb_exp, 1)
                        act.wait_ge(sb_exp, pair.count(1))
                        act.activation(soft[:, :, :], soft[:, :, :], ACT.Ln, bias=1.0).then_inc(softplus, 1)
                    elif name == "sb_after":
                        act.wait_ge(log_weight, pair.count(1))
                        act.activation(wts[:, :, :], logw[:, :, :], ACT.Exp).then_inc(weight_exp, 1)
                    elif name == "sb_out":
                        act.wait_ge(sb_out, pair.count(1))
                        act.activation(sbT[:, 2 * i:2 * i + 2, 0:T],
                                       ps[:, 6, :].rearrange("p (j t) -> p j t", j=2), ACT.Copy).then_inc(sb_hi, 1)
                    elif name == "ret_out":
                        act.wait_ge(ret_out, head.count(1))
                        act.activation(ry[:, i % 2, :, :], ps[:, 5, :].rearrange("p (e t) -> p e t", e=2),
                                       ACT.Copy).then_inc(ret_copied, 1)
                    elif name == "ret_mean":
                        act.wait_ge(ret_centred, head.count(1))
                        act.activation(rsq[:, :, :], ry[:, i % 2, :, :], ACT.Square).then_inc(ret_squared, 1)
                    elif name == "ret_var":
                        act.wait_ge(ret_var, head.count(1))
                        act.activation(rrstd[:, :], ps[:, 7, 0:T], ACT.Ln, bias=gn_eps[:, 0:1]).then_inc(ret_log, 1)
                        act.wait_ge(ret_log, head.count(1))
                        act.activation(rrstd[:, :], rrstd[:, :], ACT.Exp, scale=-0.5).then_inc(ret_rstd, 1)

                for k in range(MIX_PIECES):
                    kind, i = mixer_piece(k)
                    piece = Place(k, (L, LAYER_PIECES))
                    use = Place(mixer_use(k), (L, LAYER_USES))
                    if kind in ("sbv", "rv"):
                        if i % 2 == 1:
                            act.wait_ge(piece_used, piece.count(SPLIT_SLOTS + 1))
                            b = ps[:, 2 * use.slot(2), :]
                            if kind == "sbv":
                                act.activation(sbv[:, 0, HALF * (i // 2):HALF * (i // 2 + 1)], b,
                                               ACT.Copy).then_inc(pair_act, 1)
                            else:
                                act.activation(retqkv[:, 2 * (i // 2):2 * (i // 2) + 2, 2, :],
                                               b.rearrange("p (h c) -> p h c", h=2), ACT.Copy).then_inc(pair_act, 1)
                    elif kind != "wout":
                        carry_cross(piece, use)
                    if k + 2 < MIX_PIECES:
                        convert(piece + 2)
                    gate = Place({"ga": 0, "rg": 4, "gb": 8}.get(kind, 0) + i, (L, 12))
                    if kind in ("rg", "ga", "gb"):
                        act.wait_ge(gate_clamped, gate.count(1))
                        act.activation(gtmp[:, :, :], gtmp[:, :, :], ACT.Exp, scale=-1.0).then_inc(gate_exp, 1)
                        act.wait_ge(gate_exp, gate.count(1))
                        act.activation(gtmp[:, :, :], gtmp[:, :, :], ACT.Ln, bias=1.0).then_inc(gate_soft, 1)
                        act.wait_ge(gate_max, gate.count(1))
                        o = gtmp[:, :, :] if kind == "rg" else gates[:, kind == "gb", 2 * i:2 * i + 2, :]
                        act.activation(o, gtmp[:, :, :], ACT.Exp, scale=-1.0).then_inc(gate_sig, 1)
                    for s in stages(k):
                        stage(*s)
                mlp(Place(1, (L, 2)), Place(1, (L, 2)), Place(0, (L, 1)), Place(MIX_PIECES, (L, LAYER_PIECES)),
                    Place(MIX_USES, (L, LAYER_USES)))

            first, use0 = DEPTH * LAYER_PIECES, DEPTH * LAYER_USES
            square_sums(Place(4), lambda: convert(Place(first)))
            for j, (t, c) in enumerate(BY_TILE):
                q = slice(c * HALF, (c + 1) * HALF)
                act.wait_ge(wide_ready, j + 1)
                act.activation(wide_sq[:, t, q], wide[:, t, q], ACT.Square, scale=D ** -0.5,
                               accum_out=wide_sums[:, j:j + 1]).then_inc(wide_sq_ready, 1)
            turned_hi(Place(4), Place(use0), BY_TILE)
            convert(Place(first + 1))
            for t in range(TILES):
                act.wait_ge(rstd_ready, 2 * 2 + (t + 1))
                act.activation(xs[:, t, :], wide[:, t, :], ACT.Copy, scale=rstd[:, t:t + 1]).then_inc(x_ready, 2)
            act.wait_ge(lb_step, 1)
            act.activation(hcol[:, LB_EXP, :], hcol[:, LB_EXP, :], ACT.Exp).then_inc(lb_step, 1)

            def exponents(n):
                side = (hz, hlog)[n % 2]
                if n != len(LEVELS) - 1:
                    act.wait_ge(e_first, firsts(n))
                act.wait_ge(e_second, n + 1)
                if n == 0:
                    v = side[:, :, :].rearrange("p h (b two m) -> p (h b) two m", two=2, m=CHUNK)
                    b = hb[:, :, :].rearrange("p h (b two m) -> p (h b) two m", two=2, m=CHUNK)
                    act.activation(v[:, :, 1, :], b[:, :, 1, :], ACT.Exp)
                    act.activation(v[:, :, 0, :], v[:, :, 0, :], ACT.Exp).then_inc(e_exp, 1)
                elif n == len(LEVELS):
                    act.activation(side[:, :, 0:P], side[:, :, 0:P], ACT.Exp)
                    act.activation(side[:, :, P:P + CHUNK], hb[:, :, P:P + CHUNK], ACT.Exp)
                    act.activation(side[:, :, P + CHUNK:T], side[:, :, P + CHUNK:T], ACT.Exp).then_inc(e_exp, 1)
                elif LEVELS[n] == 1:
                    v = side[:, :, :].rearrange("p h (b two) -> p (h b) two", two=2)[:, :, 1]
                    act.activation(v, v, ACT.Exp).then_inc(e_exp, 1)
                else:
                    act.activation(side[:, :, :], side[:, :, :], ACT.Exp).then_inc(e_exp, 1)

            for k in range(MIX2_PIECES):
                kind, i = mixer2_piece(k)
                piece, use = Place(first + k), Place(use0 + k)
                if kind == "v":
                    act.wait_ge(piece_used, piece.count(SPLIT_SLOTS + 1))
                    act.activation(hv[:, 0, 256 * i:256 * (i + 1)], ps[:, 2 * use.slot(2), 0:256],
                                   ACT.Copy).then_inc(pair_act, 1)
                elif kind != "wout":
                    carry_cross(piece, use)
                n = i + (3 if kind == "g" else 0)
                if k + 2 < MIX2_PIECES:
                    convert(piece + 2)
                beside = units_beside(k)
                if k in (FIRST_UNITS - 2, FIRST_UNITS - 1):
                    exponents(k - (FIRST_UNITS - 2))
                if beside and beside[0] + 2 < UNITS:
                    exponents(beside[0] + 2)
                if kind in ("q", "g"):
                    act.wait_ge(silu_clamped, n + 1)
                    act.activation(htmp[:, :, :], htmp[:, :, :], ACT.Exp, scale=-1.0).then_inc(silu_exp, 1)
                    act.wait_ge(silu_exp, n + 1)
                    act.activation(htmp[:, :, :], htmp[:, :, :], ACT.Ln, bias=1.0).then_inc(silu_soft, 1)
                h2 = slice(2 * i, 2 * i + 2)
                if 1 <= k <= 3:
                    last2 = slice(2 * k - 2, 2 * k)
                    act.wait_ge(f_floor, k)
                    act.activation(hfloor[:, last2, :], hfloor[:, last2, :], ACT.Ln, bias=1.0).then_inc(f_floor_log, 1)
                    act.wait_ge(f_kexp_in, k)
                    act.activation(hk[:, last2, :], hk[:, last2, :], ACT.Exp, scale=-1.0).then_inc(f_kexp, 1)
                if kind == "f":
                    act.wait_ge(f_clamped, i + 1)
                    act.activation(hfloor[:, h2, :], hfloor[:, h2, :], ACT.Exp, scale=-1.0).then_inc(f_ez, 1)
                    act.wait_ge(f_ez, i + 1)
                    act.activation(hlog[:, h2, :], hfloor[:, h2, :], ACT.Ln, bias=1.0).then_inc(f_soft, 1)
                if kind in ("q", "g"):
                    act.wait_ge(silu_max, n + 1)
                    act.activation(htmp[:, :, :], htmp[:, :, :], ACT.Exp, scale=-1.0).then_inc(silu_sig, 1)
                if beside and beside[1] + 2 < UNITS:
                    exponents(beside[1] + 2)
                if k == LAST_UNITS:
                    act.wait_ge(pairs_full, len(PAIRS))
                    b = 4 + 2 * ((len(PAIRS) - 1) % 2)
                    act.activation(cross[:, :, :], ps[:, b:b + 2, :].rearrange("p b (h c) -> p (b h) c", c=P)[:, 0:HG_H, :],
                                   ACT.Copy).then_inc(pairs_placed, 1)
                if k == LAST_UNITS + 1:
                    for r in range(3):
                        act.wait_ge(o_full, r + 1)
                        o = ps[:, 4 + r, :].rearrange("p (h t) -> p h t", h=2)
                        act.activation(hb[:, 2 * r:2 * r + 2, :], o, ACT.Square).then_inc(o_squared, 1)
                    for r in range(3):
                        act.wait_ge(o_mean, r + 1)
                        v = hk[:, 2 * r:2 * r + 2, :]
                        act.activation(v, ps[:, 4 + r, :].rearrange("p (h t) -> p h t", h=2), ACT.Ln, scale=T / P,
                                       bias=rms_eps[:, 0:1]).then_inc(o_log, 1)
                        act.wait_ge(o_log, r + 1)
                        act.activation(v, v, ACT.Exp, scale=-0.5).then_inc(o_rstd, 1)
                    act.wait_ge(pool_full, 1)
                    act.wait_ge(cols_in, 64)
                    for b in range(2):
                        act.activation(yT[:, b, 0:T], ps[:, 7, b * T:(b + 1) * T], ACT.Copy,
                                       scale=hcol[:, PSCALE, b:b + 1]).then_inc(pool_hi, 1)
                for r in gated_beside(k):
                    act.wait_ge(o_gated, r + 1)
                    act.activation(yT[:, 2 + 2 * r:4 + 2 * r, 0:T], ho[:, 2 * r:2 * r + 2, :],
                                   ACT.Copy).then_inc(o_hi, 1)
            mlp(Place(6), Place(5), Place(2), Place(first + MIX2_PIECES), Place(use0 + MIX2_USES))
            square_sums(Place(7))

        @block.gpsimd
        def _(pool):
            def convert(piece):
                pool.wait_ge(hi_ready, piece.count(1))
                s, r, part = piece.slot(SPLIT_SLOTS), piece.slot(RAW_SLOTS), parts(piece)[0]
                pool.tensor_tensor(w_lo[:, s, part], raw[:, r, part], w_hi[:, s, part].bitcast(F32),
                                   ALU.subtract).then_inc(lo_pool, 1)

            def scales(m, eps, between=None):
                for t in range(TILES):
                    if t == 1 and between:
                        between()
                    c = slice(t, t + 1)
                    pool.wait_ge(sq_ready, m.count(0) * 4 + 2 * (t + 1))
                    pool.tensor_tensor(meansq[:, c], sumsq[:, 2 * t:2 * t + 1], sumsq[:, 2 * t + 1:2 * t + 2],
                                       ALU.add).then_inc(mean_ready, 1)
                    pool.wait_ge(mean_ready, m.count(0) * 4 + (2 * t + 1))
                    pool.tensor_tensor(meansq[:, c], meansq[:, c], eps, ALU.add).then_inc(mean_ready, 1)
                    pool.wait_ge(mean_ready, m.count(0) * 4 + (2 * t + 2))
                    pool.tensor_tensor(rstd[:, c], meansq[:, c], powers[:, 0:1], ALU.pow).then_inc(rstd_ready, 1)

            def norm(m, eps, piece):
                scales(m, eps, lambda: convert(piece))
                convert(piece + 1)

            def mlp(stage, eps, piece):
                convert(piece)
                convert(piece + 1)
                for t in range(TILES):
                    c = slice(t, t + 1)
                    pool.wait_ge(row_sq, stage.count(0) * 2 + (t + 1))
                    pool.tensor_tensor(row_sumsq[:, c], row_sumsq[:, c], eps, ALU.add).then_inc(row_mean, 1)
                    pool.wait_ge(row_mean, stage.count(0) * 2 + (t + 1))
                    pool.tensor_tensor(row_scale[:, c], row_sumsq[:, c], powers[:, 1:2], ALU.pow).then_inc(row_ready, 1)
                convert(piece + 2)
                steps = (MLP_PIECES - 4) // 4
                with pool.Fori(0, steps) as i:
                    here = Place(piece.fixed + 3, *piece.terms, (i, 4))
                    for j in range(4):
                        convert(here + j)
                for j in range(3 + 4 * steps, MLP_PIECES):
                    convert(piece + j)

            pool.memset(pool_w[:, :, :], 0.0).then_inc(pool_w_zero, 1)
            pool.memset(powers[:, 0:1], -0.5).then_inc(small_set, 1)
            pool.memset(powers[:, 1:2], -1.0).then_inc(small_set, 1)
            pool.memset(rms_eps[:, :], RMS_EPS).then_inc(small_set, 1)
            pool.memset(gn_eps[:, :], GN_EPS).then_inc(small_set, 1)
            pool.memset(norm_eps[:, 0:1], NORM_EPS).then_inc(small_set, 1)
            pool.memset(norm_eps[:, 1:2], RMS_EPS).then_inc(small_set, 1)
            pool.wait_ge(small_set, 6)
            pool.sem_inc(lo_dve, RAW_SLOTS)
            pool.sem_inc(lo_pool, RAW_SLOTS)
            pool.sem_inc(piece_used, SPLIT_SLOTS)
            pool.sem_inc(pair_free, 2)
            pool.sem_inc(h_ready, 8)
            for t in range(TILES):
                pool.wait_ge(x_in[t], 16)
                pool.sem_inc(x_ready, 2)
            with pool.Fori(0, DEPTH) as L:
                norm(Place(0, (L, 1)), norm_eps[:, 0:1], Place(0, (L, LAYER_PIECES)))
                for k in range(MIX_PIECES):
                    if k + 2 < MIX_PIECES:
                        convert(Place(k + 2, (L, LAYER_PIECES)))
                    kind, i = mixer_piece(k)
                    if kind == "rg":
                        pool.wait_ge(gate_sig, Place(4 + i, (L, 12)).count(1))
                        g = gr[:, 2 * i:2 * i + 2, :]
                        pool.tensor_tensor(g, g, gtmp[:, :, :], ALU.mult).then_inc(gate_done, 1)
                    for name, i in stages(k):
                        pair = Place(i, (L, SB_H // 2))
                        if name == "sb_scores":
                            pool.wait_ge(neg_log_rest, pair.count(1))
                            pool.tensor_tensor(zs[:, :, :], zs[:, :, :], mask_c[:, :, :], ALU.mult).then_inc(masked_rest, 1)
                        elif name == "sb_after":
                            pool.wait_ge(weight_exp, pair.count(1))
                            pool.tensor_tensor(wts[:, :, :], wts[:, :, :], mask_c[:, :, :], ALU.mult).then_inc(weight_ready, 1)
                        elif name == "ret_out":
                            head = Place(i, (L, RET_H))
                            pool.wait_ge(ret_copied, head.count(1))
                            if i:
                                pool.wait_ge(ret_mean, head.count(0))
                            pool.tensor_tensor(rsum[:, :], ry[:, i % 2, 0, :], ry[:, i % 2, 1, :],
                                               ALU.add).then_inc(ret_summed, 1)
                        elif name == "ret_mean":
                            pool.wait_ge(ret_squared, Place(i, (L, RET_H)).count(1))
                            pool.tensor_tensor(rsq[:, 0, :], rsq[:, 0, :], rsq[:, 1, :], ALU.add).then_inc(ret_summed, 1)
                        elif name == "rotate":
                            pool.wait_ge(turned, Place(i, (L, 2)).count(1))
                            v = retqkv[:, :, i, :]
                            pool.tensor_tensor(v, v, rope_c[:, 0:1, :].to_broadcast([P, RET_H, T]),
                                               ALU.mult).then_inc(rope_cos, 1)
                mlp(Place(0, (L, 1)), norm_eps[:, 0:1], Place(MIX_PIECES, (L, LAYER_PIECES)))

            first = DEPTH * LAYER_PIECES
            scales(Place(2), norm_eps[:, 0:1], lambda: convert(Place(first)))
            for t in range(TILES):
                c, r1, both = slice(t, t + 1), rstd[:, t:t + 1], wide_scale[:, t:t + 1]
                pool.wait_ge(wide_sq_ready, 2 * (t + 1))
                steps = ((wide_sums[:, 2 * t:2 * t + 1], wide_sums[:, 2 * t + 1:2 * t + 2], ALU.add), (both, r1, ALU.mult),
                         (both, r1, ALU.mult), (both, norm_eps[:, 1:2], ALU.add), (both, powers[:, 0:1], ALU.pow),
                         (both, r1, ALU.mult))
                for j, (a, b, op) in enumerate(steps):
                    if j == 1:
                        pool.wait_ge(rstd_ready, 2 * 2 + (t + 1))
                    if j:
                        pool.wait_ge(wide_step, len(steps) * t + j)
                    pool.tensor_tensor(both, a, b, op).then_inc(wide_step, 1)
            convert(Place(first + 1))
            pool.memset(pads[:, :, :, 0:PAD], 0.0).then_inc(pads_zero, 1)
            lbs = [hcol[:, r, :] for r in (LB_LOGIT, LB_EXP, LB, ONE_LESS)]
            pool.wait_ge(cols_in, 64)
            pool.tensor_tensor(lbs[1], lbs[0], lbs[0], ALU.subtract).then_inc(lb_step, 1)
            pool.wait_ge(lb_step, 3)
            pool.tensor_tensor(hcol[:, LB_P, :], lbs[1], hcol[:, LB_INV, :], ALU.mult).then_inc(lb_step, 1)
            pool.wait_ge(lb_step, 4)
            pool.tensor_tensor(lbs[2], hcol[:, LB_P, :], hcol[:, LB_P, :], ALU.subtract).then_inc(lb_step, 1)
            pool.wait_ge(lb_step, 5)
            pool.tensor_scalar(lbs[3], lbs[2], -1.0, 1.0, ALU.mult, ALU.add).then_inc(lb_step, 1)
            pool.wait_ge(lb_step, 6)

            def first_gaps(n):
                if n >= 2:
                    pool.wait_ge(pairs_full, n + 1)
                else:
                    pool.wait_ge(f_cum, 3)
                    pool.wait_ge(f_k, 3)
                m = LEVELS[n]
                v = (hz, hlog)[n % 2][:, :, :].rearrange("p h (b two m) -> p (h b) two m", two=2, m=m)
                b = hb[:, :, :].rearrange("p h (b two m) -> p (h b) two m", two=2, m=m)
                end = b[:, :, 0, m - 1:m].to_broadcast([P, HG_H * T // (2 * m), m])
                pool.tensor_tensor(v[:, :, 0, :], end, b[:, :, 0, :], ALU.subtract).then_inc(e_first, 1)

            def sides_beside(u):
                if u + 1 < UNITS and u + 1 != len(LEVELS) - 1:
                    first_side(u + 1)
                if u + 2 < len(LEVELS) - 1:
                    first_gaps(u + 2)
                elif u + 2 == len(LEVELS):
                    pool.wait_ge(pairs_full, u + 3)
                    side = (hz, hlog)[len(LEVELS) % 2]
                    pool.tensor_tensor(side[:, :, CHUNK:P], hb[:, :, P - 1:P].to_broadcast([P, HG_H, CHUNK]),
                                       hb[:, :, CHUNK:P], ALU.subtract).then_inc(e_first, 1)

            def first_side(n):
                m = LEVELS[n] if n < len(LEVELS) else P
                pool.wait_ge(e_exp, n + 1)
                v = (hz, hlog)[n % 2][:, :, :].rearrange("p h (b two m) -> p (h b) two m", two=2, m=m)[:, :, 0, :]
                kk = hk[:, :, :].rearrange("p h (b two m) -> p (h b) two m", two=2, m=m)[:, :, 0, :]
                pool.tensor_tensor(v, v, kk, ALU.mult).then_inc(x_first, 1)

            for k in range(MIX2_PIECES):
                if k + 2 < MIX2_PIECES:
                    convert(Place(first + k + 2))
                kind, i = mixer2_piece(k)
                if 1 <= k <= 3:
                    pool.wait_ge(f_kexp, k)
                    last2 = slice(2 * k - 2, 2 * k)
                    v = hk[:, last2, :]
                    pool.tensor_tensor(v, v, lbs[3][:, last2].unsqueeze(2).to_broadcast([P, 2, T]),
                                       ALU.mult).then_inc(f_k, 1)
                for u in units_beside(k):
                    sides_beside(u)
                if k == LAST_UNITS:
                    use = Place(DEPTH * LAYER_USES + 6)
                    pool.wait_ge(pair_free, use.count(3))
                    pool.wait_ge(pads_zero, 1)
                    pool.wait_ge(consts2_in, 32)
                    for j, w in enumerate((1, 2, 4, 8)):
                        b = slice(0 if j < 2 else 1, 2)
                        pool.tensor_tensor(pads[:, j + 1, b, PAD:], pads[:, j, b, PAD:], pads[:, j, b, PAD - w:PAD + T - w],
                                           ALU.add).then_inc(pool_step, 1)
                        pool.wait_ge(pool_step, j + 1)
                if k in (FIRST_UNITS - 3, FIRST_UNITS - 2):
                    first_gaps(k - (FIRST_UNITS - 3))
                if k == FIRST_UNITS - 1:
                    first_side(0)
                if kind == "g":
                    pool.wait_ge(silu_sig, 4 + i)
                    v = hg[:, 2 * i:2 * i + 2, :]
                    pool.tensor_tensor(v, v, htmp[:, :, :], ALU.mult).then_inc(g_gated, 1)
                    pool.wait_ge(g_gated, i + 1)
                    pool.tensor_tensor(v, v, hcol[:, HNORM, 2 * i:2 * i + 2].unsqueeze(2).to_broadcast([P, 2, T]),
                                       ALU.mult).then_inc(g_scaled, 1)
            mlp(Place(2), norm_eps[:, 1:2], Place(first + MIX2_PIECES))
            scales(Place(3), norm_eps[:, 1:2])

        @block.vector
        def _(dve):
            def convert(piece):
                s, r, part = piece.slot(SPLIT_SLOTS), piece.slot(RAW_SLOTS), parts(piece)[1]
                dve.wait_ge(raw_in[r], piece.count(1, RAW_SLOTS) * 16)
                dve.wait_ge(piece_used, piece.count(1))
                dve.tensor_copy(w_hi[:, s, part], raw[:, r, part]).then_inc(hi_dve, 1)
                dve.wait_ge(hi_dve, piece.count(1))
                dve.tensor_tensor(w_lo[:, s, part], raw[:, r, part], w_hi[:, s, part].bitcast(F32),
                                  ALU.subtract).then_inc(lo_dve, 1)

            def split_lo(o, hi, value):
                return dve.tensor_tensor(o, value, hi.bitcast(F32), ALU.subtract)

            def add_cross(use, o):
                dve.wait_ge(pair_act, use.count(1))
                b = 2 * use.slot(2)
                dve.tensor_tensor(o, ps[:, b:b + 2, 0:T], carry[:, use.slot(2), :, :], ALU.add).then_inc(pair_free, 1)

            def quarter(t, c):
                return slice(c * HALF, (c + 1) * HALF)

            def norm_rows(n, m, t):
                dve.wait_ge(rstd_ready, m.count(0) * 2 + (t + 1))
                dve.wait_ge(gain_in[n.slot(2)], n.count(1, 2) * 16)
                for c in range(2):
                    q = quarter(t, c)
                    dve.scalar_tensor_tensor(out=htok[:, t, q], in0=xs[:, t, q], scalar=rstd[:, t:t + 1],
                                             in1=gain[:, n.slot(2), q], op0=ALU.mult, op1=ALU.mult).then_inc(h_ready, 1)

            def turned_lo(h, use, j, t, c):
                dve.wait_ge(h_hi, h.count(0) * 4 + (j + 1))
                split_lo(hT[:, 4 * c:4 * c + 4, T + t * P:T + (t + 1) * P], hT[:, 4 * c:4 * c + 4, t * P:(t + 1) * P],
                         ps[:, norm_bank(use, j), :].rearrange("p (k c) -> p k c", c=P)).then_inc(h_lo, 1)

            def norm(h, piece, use, rows):
                for t in range(TILES):
                    rows(t)
                    if t == 0 and piece.terms:
                        convert(piece)
                    turned_lo(h, use, 2 * t, t, 0)
                    turned_lo(h, use, 2 * t + 1, t, 1)
                convert(piece + 1)

            def out_sums(h, j, piece):
                if j % 2 == 0:
                    dve.wait_ge(out_full, h.count(0, 2) * 2 + (j // 2 + 1))
                else:
                    dve.wait_ge(piece_used, (piece + (j // 2 - 1)).count(SPLIT_SLOTS + 1))

            def down_sums(h, j, piece):
                if j < 3:
                    dve.wait_ge(down_full, h.count(0, 2) * 3 + (j + 1))
                else:
                    dve.wait_ge(piece_used, piece.count(SPLIT_SLOTS + 1))

            def mlp(n, h, stage, piece, use):
                for j, (t, c) in enumerate(BY_HALF):
                    q = quarter(t, c)
                    out_sums(h, j, piece + -1)
                    dve.tensor_tensor(xs[:, t, q], ps[:, 4 + 2 * t + c, :], xs[:, t, q], ALU.add).then_inc(x_ready, 1)
                    dve.wait_ge(x_ready, n.count(0) * 4 + (j + 1))
                    dve.wait_ge(gain_in[n.slot(2)], n.count(1, 2) * 16)
                    dve.tensor_tensor(htok[:, t, q], xs[:, t, q], gain[:, n.slot(2), q], ALU.mult).then_inc(h_ready, 1)
                    if j == 1:
                        convert(piece)
                    for q in {2: (0, 1), 3: (2, 3)}.get(j, ()):
                        turned_lo(h, use, q, *BY_HALF[q])
                convert(piece + 1)

                def up(piece, use, i, slot, before=True):
                    if before:
                        dve.wait_ge(u_lo, i.count(0))
                    dve.wait_ge(pair_act, use.count(1))
                    b = 2 * use.slot(2)
                    dve.tensor_tensor(us[:, :, :], ps[:, b:b + 2, 0:T], carry[:, use.slot(2), :, :],
                                      ALU.add).then_inc(pair_free, 1)
                    dve.wait_ge(pair_free, use.count(3))
                    dve.scalar_tensor_tensor(out=usq[:, :, :], in0=us[:, :, :], scalar=0.0, in1=us[:, :, :],
                                             op0=ALU.max, op1=ALU.mult).then_inc(u_squared, 1)
                    convert(piece + 2)
                    dve.wait_ge(u_squared, i.count(1))
                    dve.tensor_copy(uT[:, slot, :, 0:T], usq[:, :, :]).then_inc(u_hi, 1)
                    dve.wait_ge(u_hi, i.count(1))
                    split_lo(uT[:, slot, :, T:2 * T], uT[:, slot, :, 0:T], usq[:, :, :]).then_inc(u_lo, 1)

                count = lambda i, *more: Place(i, *((reg, stride * FF_PAIRS) for reg, stride in stage.terms), *more) \
                    + stage.fixed * FF_PAIRS
                up(piece, use, count(0), 0, before=False)
                up(piece + 1, use + 1, count(1), 1)
                convert(piece + 4)
                steps = (FF_PAIRS - 2) // 2 - 1
                with dve.Fori(0, steps) as i:
                    here, u = Place(piece.fixed + 3, *piece.terms, (i, 4)), Place(use.fixed + 2, *use.terms, (i, 2))
                    for j in range(2):
                        up(here + 2 * j, u + j, count(2 + j, (i, 2)), j)
                        convert(here + (2 * j + 3))
                here, u = piece + (3 + 4 * steps), use + (2 + 2 * steps)
                up(here, u, count(2 + 2 * steps), 0)
                convert(here + 3)
                up(here + 2, u + 1, count(3 + 2 * steps), 1)
                dve.wait_ge(row_ready, stage.count(1) * 2)
                for j, (t, c) in enumerate(BY_TILE):
                    q = quarter(t, c)
                    down_sums(h, j, piece + 31)
                    dve.scalar_tensor_tensor(out=xs[:, t, q], in0=ps[:, 4 + 2 * t + c, :], scalar=row_scale[:, t:t + 1],
                                             in1=xs[:, t, q], op0=ALU.mult, op1=ALU.add).then_inc(x_ready, 1)

            with dve.Fori(0, DEPTH) as L:
                norm(Place(0, (L, 2)), Place(0, (L, LAYER_PIECES)), Place(0, (L, LAYER_USES)),
                     lambda t: norm_rows(Place(0, (L, 2)), Place(0, (L, 1)), t))

                def stage(name, i):
                    pair, head = Place(i, (L, SB_H // 2)), Place(i, (L, RET_H))
                    if name == "sb_scores":
                        dve.wait_ge(z_scaled, pair.count(1))
                        dve.scalar_tensor_tensor(out=soft[:, :, :], in0=zs[:, :, :], scalar=-1.0, in1=zs[:, :, :],
                                                 op0=ALU.mult, op1=ALU.min).then_inc(z_abs, 1)
                        dve.wait_ge(softplus, pair.count(1))
                        dve.scalar_tensor_tensor(out=logw[:, :, :], in0=zs[:, :, :], scalar=0.0, in1=soft[:, :, :],
                                                 op0=ALU.min, op1=ALU.subtract).then_inc(log_beta, 1)
                        dve.wait_ge(log_beta, pair.count(1))
                        dve.scalar_tensor_tensor(out=zs[:, :, :], in0=zs[:, :, :], scalar=0.0, in1=soft[:, :, :],
                                                 op0=ALU.max, op1=ALU.add).then_inc(neg_log_rest, 1)
                        dve.wait_ge(masked_rest, pair.count(1))
                        dve.tensor_copy(rest_hi[:, :, :], zs[:, :, :]).then_inc(rest_rounded, 1)
                        dve.wait_ge(rest_rounded, pair.count(1))
                        split_lo(rest_lo[:, :, :], rest_hi[:, :, :], zs[:, :, :]).then_inc(rest_split, 1)
                    elif name == "sb_after":
                        dve.wait_ge(after_full, pair.count(1))
                        dve.tensor_tensor(logw[:, :, :], logw[:, :, :], ps[:, 6:8, 0:CAUSAL],
                                          ALU.subtract).then_inc(log_weight, 1)
                    elif name == "sb_out":
                        dve.wait_ge(sb_hi, pair.count(1))
                        split_lo(sbT[:, 2 * i:2 * i + 2, T:2 * T], sbT[:, 2 * i:2 * i + 2, 0:T],
                                 ps[:, 6, :].rearrange("p (j t) -> p j t", j=2)).then_inc(sb_lo, 1)
                    elif name == "rotate":
                        part = Place(i, (L, 2))
                        dve.wait_ge(turned, part.count(1))
                        if i:
                            dve.wait_ge(rope_done, part.count(0))
                        v, tmp = retqkv[:, :, i, :], ry[:, :, :, :].rearrange("p a e t -> p (a e) t")
                        dve.tensor_tensor(tmp, ps[:, 4:6, :].rearrange("p b (h t) -> p (b h) t", h=2),
                                          rope_c[:, 1:2, :].to_broadcast([P, RET_H, T]), ALU.mult).then_inc(rope_sin, 1)
                        dve.wait_ge(rope_cos, part.count(1))
                        dve.wait_ge(rope_sin, part.count(1))
                        dve.tensor_tensor(v, v, tmp, ALU.add).then_inc(rope_done, 1)
                    elif name == "ret_scores":
                        dve.wait_ge(ret_scores, head.count(1))
                        dve.tensor_tensor(rs[:, :], ps[:, 4, 0:CAUSAL], decay_c[:, i, :], ALU.mult).then_inc(ret_decayed, 1)
                    elif name == "ret_mean":
                        dve.wait_ge(ret_mean, head.count(1))
                        y = ry[:, i % 2, :, :]
                        dve.tensor_tensor(y, y, ps[:, 6:7, 0:T].to_broadcast([P, 2, T]), ALU.subtract).then_inc(ret_centred, 1)
                    elif name == "ret_var":
                        y = ry[:, i % 2, :, :]
                        dve.wait_ge(ret_rstd, head.count(1))
                        dve.tensor_tensor(y, y, rrstd[:, :].unsqueeze(1).to_broadcast([P, 2, T]), ALU.mult).then_inc(ret_normed, 1)
                        dve.wait_ge(ret_normed, head.count(1))
                        dve.wait_ge(gate_done, head.count(1))
                        dve.tensor_tensor(y, y, gr[:, 2 * i:2 * i + 2, :], ALU.mult).then_inc(ret_gated, 1)
                        dve.wait_ge(ret_gated, head.count(1))
                        dve.tensor_copy(retT[:, 2 * i:2 * i + 2, 0:T], y).then_inc(ret_hi, 1)
                        dve.wait_ge(ret_hi, head.count(1))
                        split_lo(retT[:, 2 * i:2 * i + 2, T:2 * T], retT[:, 2 * i:2 * i + 2, 0:T], y).then_inc(ret_lo, 1)

                for k in range(MIX_PIECES):
                    kind, i = mixer_piece(k)
                    piece = Place(k, (L, LAYER_PIECES))
                    use = Place(mixer_use(k), (L, LAYER_USES))
                    if kind in ("sbv", "rv"):
                        if i % 2 == 1:
                            dve.wait_ge(pair_act, use.count(1))
                            b = ps[:, 2 * use.slot(2) + 1, :]
                            if kind == "sbv":
                                dve.tensor_copy(sbv[:, 1, HALF * (i // 2):HALF * (i // 2 + 1)], b).then_inc(pair_free, 1)
                            else:
                                dve.tensor_copy(retqkv[:, 2 * (i // 2):2 * (i // 2) + 2, 3, :],
                                                b.rearrange("p (h c) -> p h c", h=2)).then_inc(pair_free, 1)
                    elif kind == "sbq":
                        add_cross(use, sbqk[:, i, 0:2, :])
                    elif kind == "sbk":
                        add_cross(use, sbqk[:, i, 2:4, :])
                    elif kind in ("rq", "rk"):
                        add_cross(use, retqkv[:, 2 * i:2 * i + 2, kind == "rk", :])
                    elif kind == "rg":
                        add_cross(use, gr[:, 2 * i:2 * i + 2, :])
                    elif kind in ("ga", "gb"):
                        add_cross(use, gates[:, kind == "gb", 2 * i:2 * i + 2, :])
                    elif kind in ("psb", "pret"):
                        if kind == "psb" and i == 0:
                            dve.wait_ge(gate_sig, Place(11, (L, 12)).count(1))
                        elif kind == "psb" or i == 0:
                            dve.wait_ge(branch_b, Place((i - 1) % 4, (L, 4)).count(1))
                        else:
                            dve.wait_ge(merged_lo, Place(i - 1, (L, 4)).count(1))
                        add_cross(use, gtmp[:, :, :])
                        rows = slice(2 * i, 2 * i + 2)
                        part = Place(i, (L, 4))
                        dve.wait_ge(pair_free, use.count(3))
                        if kind == "psb":
                            dve.tensor_tensor(gates[:, 1, rows, :], gates[:, 1, rows, :], gtmp[:, :, :],
                                              ALU.mult).then_inc(branch_b, 1)
                        else:
                            dve.tensor_tensor(gtmp[:, :, :], gates[:, 0, rows, :], gtmp[:, :, :],
                                              ALU.mult).then_inc(branch_a, 1)
                            dve.wait_ge(branch_a, part.count(1))
                            dve.tensor_tensor(gtmp[:, :, :], gates[:, 1, rows, :], gtmp[:, :, :],
                                              ALU.add).then_inc(merged, 1)
                            dve.wait_ge(merged, part.count(1))
                            dve.tensor_copy(hT[:, rows, 0:T], gtmp[:, :, :]).then_inc(merged_hi, 1)
                            dve.wait_ge(merged_hi, part.count(1))
                            split_lo(hT[:, rows, T:2 * T], hT[:, rows, 0:T], gtmp[:, :, :]).then_inc(merged_lo, 1)
                    gate = {"ga": 0, "rg": 4, "gb": 8}.get(kind)
                    if gate is not None:
                        gate = Place(gate + i, (L, 12))
                        g = gr[:, 2 * i:2 * i + 2, :] if kind == "rg" else gates[:, kind == "gb", 2 * i:2 * i + 2, :]
                        dve.wait_ge(pair_free, use.count(3))
                        if gate.fixed:
                            dve.wait_ge(gate_sig, gate.count(0))
                        if kind == "rg" and i or kind == "gb" and i == 0:
                            dve.wait_ge(gate_done, Place(i if kind == "rg" else RET_H, (L, RET_H)).count(0))
                        dve.tensor_scalar(gtmp[:, :, :], g, GATE_FLOOR, None, ALU.max).then_inc(gate_clamped, 1)
                    if k + 2 < MIX_PIECES:
                        convert(piece + 2)
                    if gate is not None:
                        dve.wait_ge(gate_soft, gate.count(1))
                        dve.scalar_tensor_tensor(out=gtmp[:, :, :], in0=g, scalar=-1.0, in1=gtmp[:, :, :],
                                                 op0=ALU.mult, op1=ALU.max).then_inc(gate_max, 1)
                    if k == 11:
                        dve.wait_ge(consts_in, Place(4, (L, 4)).count(0) * 16)
                        dve.tensor_copy(sq_r[:, 2:4, :], sq_c[:, 2:4, :]).then_inc(square_rounded, 1)
                    for s in stages(k):
                        stage(*s)
                mlp(Place(1, (L, 2)), Place(1, (L, 2)), Place(0, (L, 1)), Place(MIX_PIECES, (L, LAYER_PIECES)),
                    Place(MIX_USES, (L, LAYER_USES)))

            first, use0 = DEPTH * LAYER_PIECES, DEPTH * LAYER_USES
            dve.wait_ge(gain_in[0], 3 * 16)
            for j, (t, c) in enumerate(BY_TILE):
                q = quarter(t, c)
                dve.wait_ge(x_ready, 4 * 4 + (j + 1))
                dve.tensor_tensor(wide[:, t, q], xs[:, t, q], gain[:, 0, q], ALU.mult).then_inc(wide_ready, 1)
            convert(Place(first))
            dve.wait_ge(gain_in[1], 3 * 16)

            def wide_rows(t):
                dve.wait_ge(wide_step, 6 * (t + 1))
                for c in range(2):
                    q = quarter(t, c)
                    dve.scalar_tensor_tensor(out=htok[:, t, q], in0=wide[:, t, q], scalar=wide_scale[:, t:t + 1],
                                             in1=gain[:, 1, q], op0=ALU.mult, op1=ALU.mult).then_inc(h_ready, 1)

            norm(Place(4), Place(first), Place(use0), wide_rows)
            dve.wait_ge(lb_step, 2)
            dve.reciprocal(hcol[:, LB_INV, :], hcol[:, LB_EXP, :]).then_inc(lb_step, 1)

            def second_gaps(n):
                if n == 0:
                    dve.wait_ge(f_cum, 3)
                    dve.tensor_tensor(btail[:, :, :], hb[:, :, CHUNK - 1:CHUNK], hb[:, :, P - 1:P],
                                      ALU.add).then_inc(e_second, 1)
                    return
                if n >= 2:
                    dve.wait_ge(pairs_full, n + 1)
                side = (hz, hlog)[n % 2]
                if n == len(LEVELS):
                    dve.tensor_tensor(side[:, :, 0:CHUNK], btail[:, :, :].to_broadcast([P, HG_H, CHUNK]),
                                      hb[:, :, 0:CHUNK], ALU.subtract)
                    dve.tensor_tensor(side[:, :, P + CHUNK:T], hb[:, :, P + CHUNK - 1:P + CHUNK].to_broadcast([P, HG_H, CHUNK]),
                                      hb[:, :, P + CHUNK:T], ALU.add).then_inc(e_second, 1)
                    return
                m = LEVELS[n]
                v = side[:, :, :].rearrange("p h (b two m) -> p (h b) two m", two=2, m=m)
                b = hb[:, :, :].rearrange("p h (b two m) -> p (h b) two m", two=2, m=m)
                end = b[:, :, 0, m - 1:m].to_broadcast([P, HG_H * T // (2 * m), m])
                dve.tensor_tensor(v[:, :, 1, :], b[:, :, 1, :], end, ALU.subtract).then_inc(e_second, 1)

            def second_side(n):
                m = LEVELS[n] if n < len(LEVELS) else P
                dve.wait_ge(e_exp, n + 1)
                if n == 0:
                    dve.wait_ge(silu_done, 3)
                v = (hz, hlog)[n % 2][:, :, :].rearrange("p h (b two m) -> p (h b) two m", two=2, m=m)[:, :, 1, :]
                q = hq[:, :, :].rearrange("p h (b two m) -> p (h b) two m", two=2, m=m)[:, :, 1, :]
                dve.tensor_tensor(v, v, q, ALU.mult).then_inc(x_second, 1)

            def put(n):
                dve.wait_ge(pairs_full, n + 1)
                kind, i = PAIRS[n]
                o = ps[:, 4 + 2 * (n % 2):6 + 2 * (n % 2), :].rearrange("p b c -> p (b c)")[:, 0:HG_H * P]
                if kind == "diag":
                    dve.tensor_tensor(st[:, 6 * i:6 * i + 6, :], o.rearrange("p (j c) -> p j c", c=P),
                                      ident.unsqueeze(1).to_broadcast([P, 6, P]), ALU.mult).then_inc(pairs_placed, 1)
                else:
                    m = LEVELS[i]
                    dve.wait_ge(pairs_placed, n)
                    if i == 0:
                        dve.wait_ge(cols_in, 64)
                    mask = levels_c[:, i, :].bitcast(U32).rearrange("p (b m) -> p b m", m=m)
                    dve.copy_predicated(
                        out=st[:, :, :].rearrange("p j (b two m) -> p j b two m", two=2, m=m)[:, :, :, 1, :],
                        mask=mask.unsqueeze(1).to_broadcast([P, HG_H * TILES, CHUNK // m, m]),
                        data=o.rearrange("p (j b m) -> p j b m", b=CHUNK // m, m=m)).then_inc(pairs_placed, 1)

            def take(u):
                if u + 1 < UNITS:
                    second_side(u + 1)
                if u < len(LEVELS):
                    put(2 + u)

            for k in range(MIX2_PIECES):
                kind, i = mixer2_piece(k)
                piece, use = Place(first + k), Place(use0 + k)
                h2 = slice(2 * i, 2 * i + 2)
                if kind == "v":
                    dve.wait_ge(pair_act, use.count(1))
                    dve.tensor_copy(hv[:, 1, 256 * i:256 * (i + 1)],
                                    ps[:, 2 * use.slot(2) + 1, 0:256]).then_inc(pair_free, 1)
                elif kind == "f":
                    add_cross(use, hz[:, h2, :])
                elif kind == "pool":
                    add_cross(use, pads[:, 0, :, PAD:])
                elif kind in ("q", "g"):
                    add_cross(use, (hq if kind == "q" else hg)[:, h2, :])
                n = i + (3 if kind == "g" else 0)
                beside = units_beside(k)
                if k == FIRST_UNITS:
                    put(0)
                    put(1)
                if kind in ("q", "g"):
                    v = (hq if kind == "q" else hg)[:, h2, :]
                    dve.wait_ge(pair_free, use.count(3))
                    if n:
                        dve.wait_ge(silu_sig, n)
                    if n > 3:
                        dve.wait_ge(g_gated, n - 3)
                    elif n:
                        dve.wait_ge(silu_done, n)
                    dve.tensor_scalar(htmp[:, :, :], v, GATE_FLOOR, None, ALU.max).then_inc(silu_clamped, 1)
                if kind == "f":
                    dve.wait_ge(pair_free, use.count(3))
                    dve.tensor_scalar(hfloor[:, h2, :], hz[:, h2, :], GATE_FLOOR, None, ALU.max).then_inc(f_clamped, 1)
                if beside:
                    take(beside[0])
                if k + 2 < MIX2_PIECES:
                    convert(piece + 2)
                if beside and beside[0] + 2 < UNITS:
                    second_gaps(beside[0] + 2)
                if 1 <= k <= 3:
                    last2 = slice(2 * k - 2, 2 * k)
                    lg, fl = hlog[:, last2, :], hfloor[:, last2, :]
                    dve.wait_ge(f_floor_log, k)
                    dve.wait_ge(f_kexp_in, k)
                    dve.tensor_tensor(lg, fl, lg, ALU.subtract).then_inc(f_log, 1)
                    dve.wait_ge(f_log, k)
                    dve.tensor_tensor_scan(out=hb[:, last2, :].rearrange("p h t -> p (h t)"), data0=restart_c[:, :],
                                           data1=lg.rearrange("p h t -> p (h t)"), initial=0.0, op0=ALU.mult,
                                           op1=ALU.add).then_inc(f_cum, 1)
                if kind == "f":
                    z, lg, fl = hz[:, h2, :], hlog[:, h2, :], hfloor[:, h2, :]
                    if i == 0:
                        dve.wait_ge(lb_step, 6)
                        dve.wait_ge(consts2_in, 32)
                    dve.wait_ge(f_ez, i + 1)
                    dve.wait_ge(f_soft, i + 1)
                    dve.tensor_tensor(fl, fl, hcol[:, LB, h2].unsqueeze(2).to_broadcast([P, 2, T]),
                                      ALU.mult).then_inc(f_floor, 1)
                    dve.scalar_tensor_tensor(out=lg, in0=z, scalar=-1.0, in1=lg, op0=ALU.mult,
                                             op1=ALU.max).then_inc(f_ls, 1)
                    dve.wait_ge(f_ls, i + 1)
                    dve.tensor_tensor(hk[:, h2, :], lg, z, ALU.add).then_inc(f_kexp_in, 1)
                if kind in ("q", "g"):
                    dve.wait_ge(silu_soft, n + 1)
                    dve.scalar_tensor_tensor(out=htmp[:, :, :], in0=v, scalar=-1.0, in1=htmp[:, :, :],
                                             op0=ALU.mult, op1=ALU.max).then_inc(silu_max, 1)
                    if kind == "q":
                        dve.wait_ge(silu_sig, n + 1)
                        dve.tensor_tensor(v, v, htmp[:, :, :], ALU.mult).then_inc(silu_done, 1)
                if k in (FIRST_UNITS - 3, FIRST_UNITS - 2):
                    second_gaps(k - (FIRST_UNITS - 3))
                if k == FIRST_UNITS - 1:
                    second_side(0)
                if beside:
                    take(beside[1])
                    if beside[1] + 2 < UNITS:
                        second_gaps(beside[1] + 2)
                if k == LAST_UNITS:
                    dve.wait_ge(pool_step, 4)
                    for g in range(len(WINDOWS)):
                        rows = slice(64 * (g % 2), 64 * (g % 2) + 64)
                        dve.tensor_tensor(pmix[rows, g // 2, :], pads[rows, g + 1, g // 2, PAD:],
                                          counts_c[rows, g // 2, :], ALU.mult).then_inc(pool_step, 1)
                    dve.wait_ge(pool_step, 8)
                    dve.tensor_tensor(pmix[:, :, :], pmix[:, :, :], pads[:, 0, :, PAD:],
                                      ALU.subtract).then_inc(pool_step, 1)
                if k == LAST_UNITS + 1:
                    for r in range(3):
                        dve.wait_ge(o_squared, r + 1)
                        dve.tensor_copy(ho[:, 2 * r:2 * r + 2, :],
                                        ps[:, 4 + r, :].rearrange("p (h t) -> p h t", h=2)).then_inc(o_copied, 1)
                    for r in range(3):
                        dve.wait_ge(o_rstd, r + 1)
                        dve.wait_ge(o_copied, r + 1)
                        v = ho[:, 2 * r:2 * r + 2, :]
                        dve.tensor_tensor(v, v, hk[:, 2 * r:2 * r + 2, :], ALU.mult).then_inc(o_normed, 1)
                    dve.wait_ge(pool_hi, 2)
                    for b in range(2):
                        dve.scalar_tensor_tensor(out=yT[:, b, T:2 * T], in0=ps[:, 7, b * T:(b + 1) * T],
                                                 scalar=hcol[:, PSCALE, b:b + 1], in1=yT[:, b, 0:T].bitcast(F32),
                                                 op0=ALU.mult, op1=ALU.subtract).then_inc(y_lo, 1)
                for r in gated_beside(k):
                    v, hs = ho[:, 2 * r:2 * r + 2, :], slice(2 * r, 2 * r + 2)
                    dve.wait_ge(o_normed, r + 1)
                    dve.wait_ge(g_scaled, r + 1)
                    dve.tensor_tensor(v, v, hg[:, hs, :], ALU.mult).then_inc(o_gated, 1)
                    dve.wait_ge(o_hi, r + 1)
                    split_lo(yT[:, 2 + 2 * r:4 + 2 * r, T:2 * T], yT[:, 2 + 2 * r:4 + 2 * r, 0:T], v).then_inc(y_lo, 1)
            dve.wait_ge(x_ready, 4 * 6)
            mlp(Place(6), Place(5), Place(2), Place(first + MIX2_PIECES), Place(use0 + MIX2_USES))
            for t in range(TILES):
                norm_rows(Place(7), Place(3), t)


def slab_base(nc, size):
    return nc.sbuf_base - size


_INS = ["x", "w_in", "p_ret", "p_sb", "w_out", "w_up", "w_down", "g_mix", "g_mlp", "g_final", "norm_mix_g_2", "w_in_2",
        "pool_w_2", "pool_scale_2", "hgrn_lb_logits_2", "hgrn_norm_g_2", "w_out_2", "norm_mlp_g_2", "w_up_2",
        "w_down_2", "final_norm_g_2"]


def kernel(**inputs):
    import concourse.bacc as _bacc
    from concourse.bass_utils import run_bass_kernel_spmd as _run

    nc = _bacc.Bacc("TRN2", target_bir_lowering=False, num_devices=1)
    arrays, args = {}, []
    for name, a in [(n, np.ascontiguousarray(inputs[n])) for n in _INS] + list(constants().items()):
        arrays[f"in_{name}_dram"] = a
        args.append(nc.dram_tensor(f"in_{name}_dram", a.shape, mybir.dt.from_np(a.dtype), kind="ExternalInput").ap())
    args.append(nc.dram_tensor("out_0_dram", (1, T, D), F32, kind="ExternalOutput").ap())
    build(nc, *args)
    return _run(nc, [arrays], core_ids=[0]).results[0]["out_0_dram"]
```
